# Optimizing a Trainium2 kernel written in Bass

```python
import numpy as np
import jax
import jax.numpy as jnp
from jax import lax

D_MODEL = 1024
BATCH = 1
SEQ = 256
DEPTH = 2

HEAD_DIM = 64
FOX_HEADS = 4
NSA_HEADS = 6
NSA_KV_HEADS = 2
DSA_HEADS = 6
MIX_WIDTH = (FOX_HEADS + NSA_HEADS + DSA_HEADS) * HEAD_DIM
ROPE_THETA = 10000.0
Q_BLOCK = 128
NSA_Q_BLOCK = 64
CMP_LEN = 32
CMP_STRIDE = 16
CMP_HIDDEN = 2 * HEAD_DIM
SEL_BLOCK = 64
SEL_TOPN = 16
WINDOW = 512
IDX_HEADS = 4
IDX_DIM = 64
DSA_TOPK = 256
N_EXPERTS = 64
N_GROUPS = 8
TOPK_GROUPS = 4
MOE_TOPK = 8
EXPERT_DIM = 256
SHARED_DIM = 256
ROUTED_SCALE = 2.5
MOE_BLOCK = 256
ALPHA = (2 * DEPTH) ** 0.25
BETA = (8 * DEPTH) ** -0.25
LN_EPS = 1e-5
NEG = -1e30
FORCE = 1e6

SEGMENTS = (
    ('fox_q', FOX_HEADS * HEAD_DIM), ('fox_k', FOX_HEADS * HEAD_DIM),
    ('fox_v', FOX_HEADS * HEAD_DIM), ('fox_f', FOX_HEADS),
    ('nsa_q', NSA_HEADS * HEAD_DIM),
    ('nsa_kc', NSA_KV_HEADS * HEAD_DIM), ('nsa_vc', NSA_KV_HEADS * HEAD_DIM),
    ('nsa_ks', NSA_KV_HEADS * HEAD_DIM), ('nsa_vs', NSA_KV_HEADS * HEAD_DIM),
    ('nsa_kw', NSA_KV_HEADS * HEAD_DIM), ('nsa_vw', NSA_KV_HEADS * HEAD_DIM),
    ('nsa_g', 3 * NSA_HEADS),
    ('dsa_q', DSA_HEADS * HEAD_DIM), ('dsa_k', HEAD_DIM), ('dsa_v', HEAD_DIM),
    ('idx_q', IDX_HEADS * IDX_DIM), ('idx_k', IDX_DIM), ('idx_w', IDX_HEADS),
)
N_IN = sum(width for _, width in SEGMENTS)

kernel_name = 'hybrid_fox_nsa_dsa_moe_deepnorm'

def _split_columns(h):
    parts, off = {}, 0
    for name, width in SEGMENTS:
        parts[name] = h[..., off:off + width]
        off += width
    return parts

def _rope(x, pos):
    d = x.shape[-1]
    half = d // 2
    inv_freq = ROPE_THETA ** (-jnp.arange(half, dtype=jnp.float32) * (2.0 / d))
    ang = pos.astype(jnp.float32)[:, None] * inv_freq[None, :]
    cos = jnp.cos(ang)[:, None, :]
    sin = jnp.sin(ang)[:, None, :]
    xf = x.astype(jnp.float32)
    x1, x2 = xf[..., :half], xf[..., half:]
    return jnp.concatenate([x1 * cos - x2 * sin, x2 * cos + x1 * sin], axis=-1).astype(x.dtype)

def _layer_norm(x, g, b):
    xf = x.astype(jnp.float32)
    mu = jnp.mean(xf, -1, keepdims=True)
    var = jnp.mean(jnp.square(xf - mu), -1, keepdims=True)
    return ((xf - mu) * lax.rsqrt(var + LN_EPS) * g + b).astype(x.dtype)

def _block_stack(y, batch, seq):
    y = jnp.moveaxis(y, 0, 1)
    return y.reshape((batch, seq) + y.shape[3:])

def _fox_attention(q, k, v, f_logit, f_bias):
    B, T, H, D = q.shape
    scale = D ** -0.5
    log_f = jax.nn.log_sigmoid((f_logit + f_bias).astype(jnp.float32))
    c = jnp.cumsum(log_f, axis=1).transpose(0, 2, 1)
    pos = jnp.arange(T)

    def sweep(i):
        q0 = i * Q_BLOCK
        tq = q0 + jnp.arange(Q_BLOCK)
        qb = lax.dynamic_slice_in_dim(q, q0, Q_BLOCK, axis=1)
        cb = lax.dynamic_slice_in_dim(c, q0, Q_BLOCK, axis=2)
        s = jnp.einsum('bqhd,bkhd->bhqk', qb, k).astype(jnp.float32) * scale
        s = s + (cb[..., :, None] - c[..., None, :])
        s = jnp.where(pos[None, :] <= tq[:, None], s, NEG)
        p = jax.nn.softmax(s, axis=-1).astype(v.dtype)
        return jnp.einsum('bhqk,bkhd->bqhd', p, v)

    return _block_stack(lax.map(sweep, jnp.arange(T // Q_BLOCK)), B, T)

def _compress(tok, pe, w1, w2):
    B, T, G, D = tok.shape
    n_c = (T - CMP_LEN) // CMP_STRIDE + 1
    idx = np.arange(n_c)[:, None] * CMP_STRIDE + np.arange(CMP_LEN)[None, :]
    blk = tok[:, idx] + pe[:, None, :]
    blk = jnp.swapaxes(blk, 2, 3).reshape(B, n_c, G, CMP_LEN * D)
    return jax.nn.gelu(blk @ w1) @ w2

def _nsa_attention(q, kc, vc, ks, vs, kw, vw, gate_logits, cpk, c1k, c2k, cpv, c1v, c2v):
    B, T, H, D = q.shape
    G = kc.shape[2]
    R = H // G
    scale = D ** -0.5
    pos = jnp.arange(T)
    qg = q.reshape(B, T, G, R, D)

    k_cmp = _compress(kc, cpk, c1k, c2k)
    v_cmp = _compress(vc, cpv, c1v, c2v)
    n_c = k_cmp.shape[1]
    c_start = np.arange(n_c) * CMP_STRIDE
    vis_c = (c_start + CMP_LEN - 1)[None, :] <= pos[:, None]
    s_c = jnp.einsum('btgrd,bcgd->bgrtc', qg, k_cmp).astype(jnp.float32) * scale
    p_c = jax.nn.softmax(jnp.where(vis_c, s_c, NEG), axis=-1) * jnp.any(vis_c, -1)[:, None]
    o_cmp = jnp.einsum('bgrtc,bcgd->btgrd', p_c.astype(v_cmp.dtype), v_cmp)

    n_s = T // SEL_BLOCK
    b_start = np.arange(n_s) * SEL_BLOCK
    overlap = ((c_start[:, None] < b_start[None, :] + SEL_BLOCK)
               & (c_start[:, None] + CMP_LEN > b_start[None, :])).astype(np.float32)
    imp = jnp.einsum('bgrtc,cs->bgts', p_c, jnp.asarray(overlap))
    blk_t = (pos // SEL_BLOCK)[:, None]
    jj = jnp.arange(n_s)[None, :]
    forced = (jj == 0) | (jj == blk_t) | (jj == blk_t - 1)
    imp = jnp.where(jj <= blk_t, jnp.where(forced, FORCE, imp), -1.0)
    n_top = min(SEL_TOPN, n_s)
    _, sel = lax.top_k(imp, n_top)

    ks_blk = ks.reshape(B, n_s, SEL_BLOCK, G, D).transpose(0, 3, 1, 2, 4)
    vs_blk = vs.reshape(B, n_s, SEL_BLOCK, G, D).transpose(0, 3, 1, 2, 4)
    kw_pad = jnp.pad(kw, ((0, 0), (WINDOW, 0), (0, 0), (0, 0)))
    vw_pad = jnp.pad(vw, ((0, 0), (WINDOW, 0), (0, 0), (0, 0)))
    gather = jax.vmap(jax.vmap(lambda blocks, ids: blocks[ids]))
    n_keys = n_top * SEL_BLOCK

    def sweep(i):
        q0 = i * NSA_Q_BLOCK
        tq = q0 + jnp.arange(NSA_Q_BLOCK)
        qb = lax.dynamic_slice_in_dim(qg, q0, NSA_Q_BLOCK, axis=1)
        selb = lax.dynamic_slice_in_dim(sel, q0, NSA_Q_BLOCK, axis=2)
        kg = gather(ks_blk, selb).reshape(B, G, NSA_Q_BLOCK, n_keys, D)
        vg = gather(vs_blk, selb).reshape(B, G, NSA_Q_BLOCK, n_keys, D)
        tk = (selb[..., None] * SEL_BLOCK + jnp.arange(SEL_BLOCK)).reshape(B, G, NSA_Q_BLOCK, n_keys)
        s = jnp.einsum('bqgrd,bgqkd->bgrqk', qb, kg).astype(jnp.float32) * scale
        s = jnp.where((tk <= tq[:, None])[:, :, None], s, NEG)
        o_slc = jnp.einsum('bgrqk,bgqkd->bqgrd', jax.nn.softmax(s, axis=-1).astype(vg.dtype), vg)
        kwb = lax.dynamic_slice_in_dim(kw_pad, q0, WINDOW + NSA_Q_BLOCK, axis=1)
        vwb = lax.dynamic_slice_in_dim(vw_pad, q0, WINDOW + NSA_Q_BLOCK, axis=1)
        tw = q0 - WINDOW + jnp.arange(WINDOW + NSA_Q_BLOCK)
        dist = tq[:, None] - tw[None, :]
        band = (dist >= 0) & (dist < WINDOW) & (tw >= 0)[None, :]
        s_w = jnp.einsum('bqgrd,bkgd->bgrqk', qb, kwb).astype(jnp.float32) * scale
        p_w = jax.nn.softmax(jnp.where(band, s_w, NEG), axis=-1).astype(vwb.dtype)
        o_win = jnp.einsum('bgrqk,bkgd->bqgrd', p_w, vwb)
        return o_slc, o_win

    o_slc, o_win = lax.map(sweep, jnp.arange(T // NSA_Q_BLOCK))
    o_slc = _block_stack(o_slc, B, T)
    o_win = _block_stack(o_win, B, T)
    g = jax.nn.sigmoid(gate_logits).reshape(B, T, 3, G, R, 1)
    return g[:, :, 0] * o_cmp + g[:, :, 1] * o_slc + g[:, :, 2] * o_win

def _dsa_attention(q, k, v, iq, ik, iw):
    B, T, H, D = q.shape
    scale = D ** -0.5
    topk = min(DSA_TOPK, T // 4)
    w_idx = iw.astype(jnp.float32) * (IDX_HEADS ** -0.5) * (IDX_DIM ** -0.5)
    pos = jnp.arange(T)
    gather = jax.vmap(lambda rows, ids: rows[ids])

    def sweep(i):
        q0 = i * Q_BLOCK
        tq = q0 + jnp.arange(Q_BLOCK)
        iqb = lax.dynamic_slice_in_dim(iq, q0, Q_BLOCK, axis=1)
        iwb = lax.dynamic_slice_in_dim(w_idx, q0, Q_BLOCK, axis=1)
        dots = jnp.einsum('bqhe,bke->bqhk', iqb, ik).astype(jnp.float32)
        score = jnp.einsum('bqh,bqhk->bqk', iwb, jax.nn.relu(dots))
        score = jnp.where(pos[None, :] <= tq[:, None], score, NEG)
        _, idx = lax.top_k(score, topk)
        kg = gather(k, idx)
        vg = gather(v, idx)
        qb = lax.dynamic_slice_in_dim(q, q0, Q_BLOCK, axis=1)
        s = jnp.einsum('bqhd,bqkd->bhqk', qb, kg).astype(jnp.float32) * scale
        s = jnp.where((idx <= tq[None, :, None])[:, None], s, NEG)
        p = jax.nn.softmax(s, axis=-1).astype(vg.dtype)
        return jnp.einsum('bhqk,bqkd->bqhd', p, vg)

    return _block_stack(lax.map(sweep, jnp.arange(T // Q_BLOCK)), B, T)

def _heads(a, n_heads):
    return a.reshape(a.shape[0], a.shape[1], n_heads, -1)

def _token_mixer(x, w_in, fox_fb, cpk, c1k, c2k, cpv, c1v, c2v, w_out):
    B, T, _ = x.shape
    pos = jnp.arange(T)
    p = _split_columns(x @ w_in)
    G = NSA_KV_HEADS
    o_fox = _fox_attention(_heads(p['fox_q'], FOX_HEADS), _heads(p['fox_k'], FOX_HEADS),
                           _heads(p['fox_v'], FOX_HEADS), p['fox_f'], fox_fb)
    o_nsa = _nsa_attention(
        _rope(_heads(p['nsa_q'], NSA_HEADS), pos),
        _rope(_heads(p['nsa_kc'], G), pos), _heads(p['nsa_vc'], G),
        _rope(_heads(p['nsa_ks'], G), pos), _heads(p['nsa_vs'], G),
        _rope(_heads(p['nsa_kw'], G), pos), _heads(p['nsa_vw'], G),
        p['nsa_g'], cpk, c1k, c2k, cpv, c1v, c2v)
    o_dsa = _dsa_attention(
        _rope(_heads(p['dsa_q'], DSA_HEADS), pos),
        _rope(_heads(p['dsa_k'], 1), pos)[:, :, 0], p['dsa_v'],
        _rope(_heads(p['idx_q'], IDX_HEADS), pos),
        _rope(_heads(p['idx_k'], 1), pos)[:, :, 0], p['idx_w'])
    o = jnp.concatenate([o_fox.reshape(B, T, -1), o_nsa.reshape(B, T, -1),
                         o_dsa.reshape(B, T, -1)], axis=-1)
    return o @ w_out

def _moe(x, w_router, b_router, w_gate, w_up, w_down, ws_gate, ws_up, ws_down):
    B, T, Dm = x.shape
    N = B * T
    E = N_EXPERTS
    xt = x.reshape(N, Dm)
    s = jax.nn.sigmoid((xt @ w_router).astype(jnp.float32))
    sb = s + b_router.astype(jnp.float32)
    grp_score = lax.top_k(sb.reshape(N, N_GROUPS, E // N_GROUPS), 2)[0].sum(-1)
    _, gi = lax.top_k(grp_score, TOPK_GROUPS)
    gmask = jax.nn.one_hot(gi, N_GROUPS, dtype=jnp.float32).sum(1) > 0
    emask = jnp.repeat(gmask, E // N_GROUPS, axis=1)
    _, ei = lax.top_k(jnp.where(emask, sb, NEG), MOE_TOPK)
    gw = jnp.take_along_axis(s, ei, axis=1)
    gw = gw / jnp.sum(gw, -1, keepdims=True) * ROUTED_SCALE

    A = N * MOE_TOPK
    e_flat = ei.reshape(A)
    tok_flat = jnp.repeat(jnp.arange(N), MOE_TOPK)
    order = jnp.argsort(e_flat)
    e_s, tok_s, w_s = e_flat[order], tok_flat[order], gw.reshape(A)[order]
    counts = jnp.bincount(e_flat, length=E)
    start = jnp.cumsum(counts) - counts
    padded = (counts + MOE_BLOCK - 1) // MOE_BLOCK * MOE_BLOCK
    pstart = jnp.cumsum(padded) - padded
    dest = pstart[e_s] + (jnp.arange(A) - start[e_s])
    rows = A + E * MOE_BLOCK
    n_chunks = rows // MOE_BLOCK
    buf = jnp.zeros((rows, Dm), x.dtype).at[dest].set(xt[tok_s])
    chunk_e = jnp.minimum(jnp.searchsorted(pstart + padded, jnp.arange(n_chunks) * MOE_BLOCK, side='right'), E - 1)

    def expert_rows(args):
        xb, e = args
        h = jax.nn.silu(xb @ w_gate[e]) * (xb @ w_up[e])
        return h @ w_down[e]

    ybuf = lax.map(expert_rows, (buf.reshape(n_chunks, MOE_BLOCK, Dm), chunk_e)).reshape(rows, Dm)
    routed = jnp.zeros((N, Dm), x.dtype).at[tok_s].add(ybuf[dest] * w_s[:, None].astype(x.dtype))
    shared = (jax.nn.silu(xt @ ws_gate) * (xt @ ws_up)) @ ws_down
    return (routed + shared).reshape(B, T, Dm)

def setup_inputs(seed: int = 0) -> dict:
    key = jax.random.key(seed)
    ks = jax.random.split(key, 24)

    def nrm(k, shape, scale):
        return jax.random.normal(k, shape, jnp.float32) * scale

    L = DEPTH
    return {
        'x': nrm(ks[0], (BATCH, SEQ, D_MODEL), 1.0),
        'w_in': nrm(ks[1], (L, D_MODEL, N_IN), D_MODEL ** -0.5),
        'fox_forget_bias': 3.0 + nrm(ks[2], (L, FOX_HEADS), 0.5),
        'cmp_pos_k': nrm(ks[3], (L, CMP_LEN, HEAD_DIM), 0.1),
        'cmp_w1_k': nrm(ks[4], (L, CMP_LEN * HEAD_DIM, CMP_HIDDEN), (CMP_LEN * HEAD_DIM) ** -0.5),
        'cmp_w2_k': nrm(ks[5], (L, CMP_HIDDEN, HEAD_DIM), CMP_HIDDEN ** -0.5),
        'cmp_pos_v': nrm(ks[6], (L, CMP_LEN, HEAD_DIM), 0.1),
        'cmp_w1_v': nrm(ks[7], (L, CMP_LEN * HEAD_DIM, CMP_HIDDEN), (CMP_LEN * HEAD_DIM) ** -0.5),
        'cmp_w2_v': nrm(ks[8], (L, CMP_HIDDEN, HEAD_DIM), CMP_HIDDEN ** -0.5),
        'w_out': nrm(ks[9], (L, MIX_WIDTH, D_MODEL), MIX_WIDTH ** -0.5 * BETA),
        'ln1_g': 1.0 + nrm(ks[10], (L, D_MODEL), 0.01),
        'ln1_b': nrm(ks[11], (L, D_MODEL), 0.01),
        'w_router': nrm(ks[12], (L, D_MODEL, N_EXPERTS), D_MODEL ** -0.5),
        'b_router': nrm(ks[13], (L, N_EXPERTS), 0.01),
        'w_gate': nrm(ks[14], (L, N_EXPERTS, D_MODEL, EXPERT_DIM), D_MODEL ** -0.5),
        'w_up': nrm(ks[15], (L, N_EXPERTS, D_MODEL, EXPERT_DIM), D_MODEL ** -0.5),
        'w_down': nrm(ks[16], (L, N_EXPERTS, EXPERT_DIM, D_MODEL), EXPERT_DIM ** -0.5 * BETA),
        'ws_gate': nrm(ks[17], (L, D_MODEL, SHARED_DIM), D_MODEL ** -0.5),
        'ws_up': nrm(ks[18], (L, D_MODEL, SHARED_DIM), D_MODEL ** -0.5),
        'ws_down': nrm(ks[19], (L, SHARED_DIM, D_MODEL), SHARED_DIM ** -0.5 * BETA),
        'ln2_g': 1.0 + nrm(ks[20], (L, D_MODEL), 0.01),
        'ln2_b': nrm(ks[21], (L, D_MODEL), 0.01),
    }

def reference(x, w_in, fox_forget_bias, cmp_pos_k, cmp_w1_k, cmp_w2_k, cmp_pos_v, cmp_w1_v,
              cmp_w2_v, w_out, ln1_g, ln1_b, w_router, b_router, w_gate, w_up, w_down,
              ws_gate, ws_up, ws_down, ln2_g, ln2_b):
    for l in range(DEPTH):
        mix = _token_mixer(x, w_in[l], fox_forget_bias[l], cmp_pos_k[l], cmp_w1_k[l], cmp_w2_k[l],
                           cmp_pos_v[l], cmp_w1_v[l], cmp_w2_v[l], w_out[l])
        x = _layer_norm(ALPHA * x + mix, ln1_g[l], ln1_b[l])
        ffn = _moe(x, w_router[l], b_router[l], w_gate[l], w_up[l], w_down[l],
                   ws_gate[l], ws_up[l], ws_down[l])
        x = _layer_norm(ALPHA * x + ffn, ln2_g[l], ln2_b[l])
    return x


_drawn_inputs = setup_inputs


def setup_inputs(seed=0):
    import zlib

    import numpy as np

    out = dict(_drawn_inputs(seed))
    spreads = {}
    factors = {'cmp_pos_k': 4.265}
    for name, (base, spread) in spreads.items():
        noise = np.random.default_rng([zlib.crc32(name.encode()), seed]).standard_normal(out[name].shape)
        drawn = base * np.exp(spread * noise) if base else spread * noise
        out[name] = jnp.asarray(drawn.astype(out[name].dtype))
    for name, factor in factors.items():
        out[name] = (out[name] * factor).astype(out[name].dtype)
    return out
```

```python
import numpy as np
import concourse.bass as bass
from concourse import mybir
from contextlib import ExitStack

F32 = mybir.dt.float32
F32R = mybir.dt.float32r
BF16 = mybir.dt.bfloat16
I32 = mybir.dt.int32
ALU = mybir.AluOpType
ACT = mybir.ActivationFunctionType
AX = mybir.AxisListType.X

P = 128
DEPTH, D, T = 2, 1024, 256
TT = T // P
KD = D // P
HD = 64
FOX, NSA, GRP, DSA, IDX = 4, 6, 2, 6, 4
REP = NSA // GRP
SCALE = HD ** -0.5
PIECE = 256
N_IN_PIECES, N_OUT_PIECES = 11, 4
RING = 5
CMP_LEN, CMP_STRIDE = 32, 16
NC = (T - CMP_LEN) // CMP_STRIDE + 1
CPAIRS = CMP_LEN // 2
TOPK = min(256, T // 4)
NE, EF = 64, 256
NGRP = 8
MOE_TOPK = 8
PAIRS = NE // 2
SLOTS = 64
ROUNDS = T // SLOTS
EW = KD * 2 * EF + (EF // P) * D
EGU = KD * 2 * EF
ROUTED_SCALE = 2.5
ALPHA = (2 * DEPTH) ** 0.25
LN_EPS = 1e-5
NEG = -1e30
TAKEN = -3.0e38
BIG = 3.0e38

ROPE_PIECES = (0, 1, 7, 8, 9, 10)
TURNED = (0, 1, 3, 4, 5, 7, 8, 9, 10)
TILE_OF = {0: 0, 4: 4, 5: 6, 7: 8, 8: 10, 9: 12, 10: 14}
T_IQ, T_IK, T_DK, T_FQ, T_FK, T_NQ, T_KS, T_DQ, T_KW = 0, 2, 3, 4, 6, 8, 11, 12, 15
V_W, V_D, V_MISC, V_S, V_F = 0, 128, 192, 218, 346
VCOLS = 602
M_F, M_G, M_W = V_MISC, V_MISC + 4, V_MISC + 22

UNITS = ([("fox", 0, 0), ("fox", 1, 1)]
         + [(k, 2 + r, r) for r in range(REP) for k in ("slc", "win")]
         + [("dsa", 5 + i, i) for i in range(3)])
NU = len(UNITS)
TURNS = []
for _u, (_k, _o, _r) in enumerate(UNITS):
    TURNS.append(("unit", _u))
    if _k == "win":
        TURNS.append(("cmp", _r))
TURN_OF_UNIT = {u: v for v, (k, u) in enumerate(TURNS) if k == "unit"}


class Order:

    def __init__(self, eng, sem):
        self.eng, self.sem, self.n = eng, sem, 0

    def mark(self, ins):
        self.n += 1
        ins.then_inc(self.sem, 1)

    def link(self, ins):
        self.mark(ins)
        self.eng.wait_ge(self.sem, self.n)

    def settle(self):
        if self.n:
            self.eng.wait_ge(self.sem, self.n)

    def restart(self):
        self.settle()
        self.eng.sem_clear(self.sem)
        self.n = 0


def build(nc, x, pieces, rows, small, moe_w, ws, router, lnw, consts, out, dbg=None):
    ctx = ExitStack()
    with ctx:
        at = [(nc.sbuf_base + 63) // 64 * 64]

        def place(name, shape, dt=F32, where=None):
            size = int(np.prod(shape[1:])) * (2 if dt == BF16 else 4)
            size = (size + 31) // 32 * 32
            start = at[0] if where is None else where[0]
            t = nc.alloc_sbuf_tensor_at(name, shape, dt, offset=start)
            if where is None:
                at[0] += size
            else:
                where[0] += size
            return t

        ex = [place(f"expert_weights{s}", [P, 2, EW]) for s in range(2)]
        ring_at = at[0]
        piece = [place(f"piece{s}", [P, KD, PIECE]) for s in range(RING)]
        moe_at, ring_end = [ring_at], at[0]
        x_sb = place("x_sb", [P, TT, D])
        xT = place("xT", [P, KD, T])
        c_rows = place("c_rows", [1, 2, FOX * T], where=[at[0] - 4 * KD * T])
        shared_at = at[0]
        qkT = place("qkT", [P, 16, T])
        cmpT = place("cmpT", [P, 2, GRP, T])
        hq = place("hq", [P, 4, PIECE])
        assert at[0] - shared_at == EW * 4
        ln_at = at[0]
        prob = place("prob", [P, 2, 2, 3 * P])
        probT = place("probT", [P, 2, 3 * P])
        vbuf = place("vbuf", [P, TT, VCOLS])
        score = place("score", [P, 3 * P])
        rtmp = place("rtmp", [P, 2, 3 * P], where=[ln_at])
        dmask = place("dmask", [P, 3 * P], BF16)
        route_at = at[0]
        blkT = place("blkT", [P, 2, CPAIRS, GRP, NC])
        rope_tmp = place("rope_tmp", [P, PIECE])
        gates = place("gates", [P, TT, 18])
        fz = place("fz", [P, 4, TT * 4])
        sm_neg = place("sm_neg", [P, 2, 4])
        sm_max = place("sm_max", [P, 2, 4])
        sm_sum = place("sm_sum", [P, 2, 4])
        sm_r = place("sm_r", [P, 2, 4])
        top8 = place("top8", [P, 8])
        w_idx = place("w_idx", [P, TT, IDX])
        hgelu = place("hgelu", [P, 4, 2 * GRP * NC])
        kcT = place("kcT", [P, 16])
        vc_sb = place("vc_sb", [16, GRP, HD])
        pc = place("pc", [P, TT, REP * GRP, 16])
        pcs = place("pcs", [P, 4, TT * REP * GRP])
        smalls = place("smalls", [P, 2 * HD + 2 * CPAIRS])
        biases = place("biases", [P, FOX + NE])
        ln_s = place("ln_s", [P, TT, 24])
        ident = place("ident", [P, P])
        identb = place("identb", [P, P], BF16)
        cmask = place("cmask", [P, P], BF16)
        upper = place("upper", [P, TT, T])
        rope_cs = place("rope_cs", [P, 2, TT, HD])
        misc_c = place("misc_c", [P, TT * 16 + TT + SLOTS])
        cvis = misc_c[:, 0:TT * 16].rearrange("p (t c) -> p t c", t=TT)
        anyvis = misc_c[:, TT * 16:TT * 16 + TT]
        iota1 = misc_c[:, TT * 16 + TT:]
        ones = place("ones", [P, P])
        assert at[0] <= nc.sbuf_usable_end, (at[0], nc.sbuf_usable_end)

        cmask_f = place("cmask_f", [P, P], where=[ring_at])
        wsh = place("shared_weights", [P, EW], where=[shared_at])
        lnp = place("ln_rows", [P, 2, D], where=[ln_at])
        ra = [route_at]
        wr = place("router_w", [P, KD, NE], where=ra)
        rt = place("route", [P, 5, TT, NE], where=[ln_at + 4 * 2 * D + 0])
        xs = [place(f"x_part{j}", [P, TT, D], BF16, where=moe_at) for j in range(3)]
        xgT = [place(f"gathered{s}", [P, KD, P], F32, where=moe_at) for s in range(2)]
        y_hi = place("y_hi", [P, D], F32R, where=moe_at)
        y_lo = place("y_lo", [P, D], F32R, where=moe_at)
        rest = place("x_rest", [P, TT, D], F32, where=[moe_at[0] - 8 * D])
        hot = [place(f"hot{s}", [P, TT, P], BF16, where=moe_at) for s in range(2)]
        hotT = [place(f"hotT{s}", [P, T], F32R, where=moe_at) for s in range(2)]
        h_sb = place("h_sb", [P, EF], F32, where=moe_at)
        hT = place("hT", [P, EF // P, P], F32, where=moe_at)
        sig = place("sig", [P, EF], F32, where=moe_at)
        assert moe_at[0] <= ring_end
        gw2 = place("gate_weights", [P, TT, NE, 3], BF16, where=ra)
        gwr = place("gate_rest", [P, NE], F32, where=ra)
        gslot = place("gate_slot", [P, 2], F32, where=ra)
        flag = place("overflow", [1, 1], I32, where=ra)
        rsm = place("route_small", [P, 24], F32, where=ra)
        assert ra[0] <= route_at + 4 * 2 * CPAIRS * GRP * NC + 4 * PIECE, ra[0] - route_at
        shT = place("shared_hT", [P, 2, T], F32, where=[ring_at + 6 * TT * D])
        shS = place("shared_sig", [P, 2, T], F32, where=[ring_at + 6 * TT * D + 4 * D])

        bank = [ctx.enter_context(nc.psum_tensor(f"bank{b}", [P, 512], F32)) for b in range(8)]

        names = []

        def sem(name):
            s = ctx.enter_context(nc.semaphore(name))
            names.append(s)
            return s

        once = ctx.enter_context(nc.semaphore("constants_loaded"))
        stored = ctx.enter_context(nc.semaphore("output_stored"))
        piece_ld = [sem(f"piece_loaded{s}") for s in range(RING)]
        gu_ld = [sem(f"gate_up_loaded{s}") for s in range(2)]
        dn_ld = [sem(f"down_loaded{s}") for s in range(2)]
        small_ld, ln_ld, ws_ld, wr_ld = sem("smalls_loaded"), sem("ln_rows_loaded"), sem("shared_loaded"), sem("router_loaded")
        xt_ps, xt_sb = sem("x_transposed"), sem("xT_ready")
        proj = sem("projected")
        out_dve, out_act = sem("projection_rotated"), sem("projection_copied")
        hq_dve, hq_act = sem("rotated_heads"), sem("plain_heads")
        turned, turned_out = sem("heads_transposed"), sem("heads_in_sbuf")
        dots, dots_out = sem("index_dots"), sem("index_relu")
        dots_free = sem("index_relu_used")
        dmask_ready = sem("dsa_mask_ready")
        misc_rd, gate_exp, gates_ready = sem("misc_ready"), sem("gate_exp"), sem("gates_ready")
        fabs, fln, lf_ready, cum, c_ready = sem("fox_abs"), sem("fox_ln"), sem("fox_log_forget"), sem("fox_cumsum"), sem("fox_rows_ready")
        blk_ready, hid, gelu_u, gelu_e, gelu_ready = sem("cmp_blocks"), sem("cmp_hidden"), sem("gelu_arg"), sem("gelu_exp"), sem("gelu_ready")
        kv_ps, kv_sb = sem("cmp_kv"), sem("cmp_kv_sb")
        sc_ps, sc_sub, sc_exp, pc_ready = sem("cmp_scores"), sem("cmp_shifted"), sem("cmp_exp"), sem("cmp_probs")
        s_ready, m_ready, e_ready, p_ready = sem("scores"), sem("row_max"), sem("exps"), sem("probs")
        pt_ps, pt_sb, pv, o_sb = sem("probs_turned"), sem("probsT_ready"), sem("values_added"), sem("heads_out")
        mix = sem("mixed")
        ln_var, ln_rs, ln_done, ln_used = sem("ln_variance"), sem("ln_rstd0"), sem("ln_done"), sem("ln_rows_used")
        split_a, split_rest, split_b, split_c = sem("x_part0_ready"), sem("x_rest_ready"), sem("x_part1_ready"), sem("x_part2_ready")
        logits, lg_exp, sel_ready, ranks, routed_ready = sem("router_logits"), sem("router_exp"), sem("selected"), sem("ranks"), sem("routes_ready")
        sh_ps, sh_exp, sh_h, sh_dn = sem("shared_gate_up"), sem("shared_exp"), sem("shared_h"), sem("shared_down")
        dve_own, act_own, pool_own = sem("vector_order"), sem("scalar_order"), sem("pool_order")

        class Sweep:

            def __init__(self, tag):
                self.hot, self.gat, self.xg, self.hotT = sem(tag + "hot_ready"), sem(tag + "gathered"), sem(tag + "gathered_sb"), sem(tag + "hotT_ready")
                self.gu, self.ex, self.h = sem(tag + "gate_up"), sem(tag + "sigmoid"), sem(tag + "h_ready")
                self.ht_ps, self.ht = sem(tag + "h_transposed"), sem(tag + "hT_ready")
                self.dn, self.yh, self.yl, self.sc = sem(tag + "down"), sem(tag + "y_hi_ready"), sem(tag + "y_lo_ready"), sem(tag + "added_back")

        main, over = Sweep("main_"), Sweep("over_")
        over_ld = sem("over_loaded")

        def ps_proj(c, t):
            return bank[(2 * c + t) % 4][:, 0:PIECE]

        def proj_out(c):
            if c in ROPE_PIECES:
                return out_dve, 2 * ROPE_PIECES.index(c) + 1
            if c in (4, 5):
                return hq_ready(c)
            return out_act, 2 * [2, 3, 6].index(c) + 1

        def hq_ready(c):
            if c in ROPE_PIECES:
                return hq_dve, 2 * ROPE_PIECES.index(c) + 1
            return hq_act, 2 * [3, 4, 5].index(c) + 1

        with nc.Block() as block:
            @block.sync
            def _(sp):
                for dst, src in ((x_sb[:, :, :], x.rearrange("b (t p) d -> p (b t) d", p=P)),
                                 (ident[:, :], consts["ident"]), (cmask_f[:, :], consts["cmask"]),
                                 (upper[:, :, :], consts["upper"]),
                                 (rope_cs[:, :, :, :], consts["rope"]), (misc_c[:, :], consts["misc"]),
                                 (ones[:, :], consts["ones"])):
                    sp.dma_start(dst, src).then_inc(once, 16)
                sp.wait_ge(once, 16 * 7)

            @block.vector
            def _(dve):
                dve.wait_ge(once, 16 * 7)
                nc.vector.tensor_copy(identb[:, :], ident[:, :])
                nc.vector.tensor_copy(cmask[:, :], cmask_f[:, :])

        with nc.Fori(0, DEPTH) as layer:
            def of(t):
                return t[bass.ds(layer, 1)]

            with nc.Block() as block:
                @block.sync
                def _(sp):
                    sp.dma_start(smalls[:, :], of(small).rearrange("l p c -> p (l c)")).then_inc(small_ld, 16)
                    sp.dma_start(biases[:, :], of(rows)[0].partition_broadcast(P)).then_inc(small_ld, 16)

                    def load_piece(n):
                        if n >= RING:
                            m = n - RING
                            if m < N_IN_PIECES:
                                sp.wait_ge(proj, 2 * m + 2)
                            elif m < N_IN_PIECES + 2:
                                sp.wait_ge(hid, m - N_IN_PIECES + 1)
                        sp.dma_start(piece[n % RING][:, :, :],
                                     of(pieces)[0, n].rearrange("p (k c) -> p k c", k=KD)).then_inc(piece_ld[n % RING], 16)

                    def load_pair(s, which, pair):
                        a, b, ld = ((0, EGU, gu_ld), (EGU, EW, dn_ld))[which]
                        sp.dma_start(ex[s][:, :, a:b],
                                     of(moe_w)[0, bass.ds(pair * 2, 2), :, a:b].rearrange("e p c -> p e c")).then_inc(ld[s], 16)

                    for n in range(RING):
                        load_piece(n)
                    load_piece(RING)
                    for q in range(4):
                        load_pair(q // 2, q % 2, q // 2)
                        load_piece(RING + 1 + 2 * q)
                        load_piece(RING + 2 + 2 * q)
                    for n in range(RING + 9, N_IN_PIECES + 2 + N_OUT_PIECES):
                        load_piece(n)
                    sp.wait_ge(o_sb, 8)
                    sp.dma_start(wsh[:, :], of(ws)[0]).then_inc(ws_ld, 16)
                    sp.dma_start(lnp[:, :, :].rearrange("p a d -> p (a d)"),
                                 of(lnw)[0, 0].partition_broadcast(P)).then_inc(ln_ld, 16)
                    sp.dma_start(wr[:, :, :].rearrange("p k e -> p (k e)"), of(router)[0]).then_inc(wr_ld, 16)
                    sp.wait_ge(ln_used, 1)
                    sp.dma_start(lnp[:, :, :].rearrange("p a d -> p (a d)"),
                                 of(lnw)[0, 1].partition_broadcast(P)).then_inc(ln_ld, 16)
                    with sp.Fori(1, PAIRS // 2) as i:
                        for s in range(2):
                            sp.wait_ge(main.gu, 2 * i + (s - 1))
                            load_pair(s, 0, 2 * i + s)
                            sp.wait_ge(main.dn, 2 * i + (s - 1))
                            load_pair(s, 1, 2 * i + s)
                    sp.wait_ge(main.sc, PAIRS)
                    more = sp.value_load(flag[0:1, 0:1], min_val=0, max_val=1)
                    with sp.If(more > 0):
                        with sp.Fori(0, ROUNDS - 1) as r:
                            with sp.Fori(0, PAIRS) as n:
                                sp.wait_ge(over.sc, r * PAIRS + n + 1)
                                sp.dma_start(ex[0][:, :, :], of(moe_w)[0, bass.ds(n * 2, 2)].rearrange("e p c -> p e c")).then_inc(over_ld, 16)
                    with sp.Else():
                        sp.nop()
                    sp.nop()

                @block.tensor
                def _(pe):
                    def turn_x(first):
                        for g in range(4):
                            t, k0 = g // 2, (g % 2) * 4
                            b = bank[4 + g % 2]
                            if g >= 2:
                                pe.wait_ge(xt_sb, first + g - 1)
                            elif first:
                                pe.wait_ge(ln_done, TT)
                            for j in range(4):
                                mm = pe.transpose(b[:, j * P:(j + 1) * P], x_sb[:, t, (k0 + j) * P:(k0 + j + 1) * P], ident[:, :])
                            mm.then_inc(xt_ps, 1)
                        pe.wait_ge(xt_sb, first + 4)

                    def project(c):
                        pe.wait_ge(piece_ld[c % RING], 16 * (c // RING + 1))
                        for t in range(TT):
                            if c >= 2:
                                reader, count = proj_out(c - 2)
                                pe.wait_ge(reader, count + t)
                            for k in range(KD):
                                mm = pe.matmul(ps_proj(c, t), xT[:, k, t * P:(t + 1) * P], piece[c % RING][:, k, :],
                                               start=(k == 0), stop=(k == KD - 1))
                            mm.then_inc(proj, 1)

                    turns = [(c, t) for c in TURNED for t in range(TT)]

                    def turn_heads(c):
                        for t in range(TT):
                            j = turns.index((c, t))
                            writer, count = hq_ready(c)
                            pe.wait_ge(writer, count + t)
                            if j >= 2:
                                pe.wait_ge(turned_out, j - 1)
                            b, src = bank[4 + j % 2], hq[:, (2 * c + t) % 4, :]
                            for q in range(1 if c == 3 else 2):
                                mm = pe.transpose(b[:, q * P:(q + 1) * P], src[:, q * P:(q + 1) * P], ident[:, :])
                            mm.then_inc(turned, 1)

                    def pair_dots(b0, b1, tq, tk, after, cols=None):
                        for q, (a, w) in enumerate(((0, P), (P, 2 * P))):
                            for h, b in ((0, b0), (1, b1)):
                                r = slice(h * HD, (h + 1) * HD)
                                mm = pe.matmul(b[:, a:a + w], qkT[r, tq, q * P:(q + 1) * P], qkT[r, tk, 0:w], start=True, stop=(after is None))
                                if after is not None:
                                    mm = after(h, b, q, a, w)
                        return mm

                    def index_dots(i):
                        if i == 0:
                            pe.wait_ge(turned_out, 4)
                        else:
                            pe.wait_ge(dots_out, 2 * i)
                        pair_dots(bank[6], bank[7], T_IQ + i, T_IK, None).then_inc(dots, 1)

                    def fox_rows():
                        pe.wait_ge(lf_ready, 1)
                        pe.wait_ge(dots_out, 4)
                        for h in range(FOX):
                            o = bank[6 + h // 2][0:1, (h % 2) * T:(h % 2 + 1) * T]
                            for t in range(TT):
                                mm = pe.matmul(o, fz[:, 3, t * 4 + h:t * 4 + h + 1], upper[:, t, :], start=(t == 0), stop=(t == TT - 1))
                        mm.then_inc(cum, 1)

                    turn_x(0)
                    project(0)
                    project(1)
                    turn_heads(0)
                    project(2)
                    turn_heads(1)
                    index_dots(0)
                    project(3)
                    index_dots(1)
                    project(4)
                    turn_heads(3)
                    fox_rows()
                    project(5)
                    turn_heads(4)
                    project(6)
                    turn_heads(5)
                    for c in range(7, 11):
                        project(c)
                        if c > 7:
                            turn_heads(c - 1)

                    hidden = bank[6][:, 0:2 * GRP * NC]
                    for kv in range(2):
                        n = N_IN_PIECES + kv
                        pe.wait_ge(piece_ld[n % RING], 16 * (n // RING + 1))
                        if kv == 0:
                            pe.wait_ge(c_ready, 2)
                        pe.wait_ge(blk_ready, kv + 1)
                        w1 = piece[n % RING][:, :, :].rearrange("p k c -> p (k c)")
                        for i in range(CPAIRS):
                            mm = pe.matmul(hidden[:, kv * GRP * NC:(kv + 1) * GRP * NC], w1[:, i * P:(i + 1) * P],
                                      blkT[:, kv, i, :, :].rearrange("p g c -> p (g c)"), start=(i == 0), stop=(i == CPAIRS - 1))
                        mm.then_inc(hid, 1)
                    turn_heads(10)

                    def cmp_kv():
                        pe.wait_ge(gelu_ready, 1)
                        pe.wait_ge(small_ld, 32)
                        hk = hgelu[:, 3, 0:GRP * NC]
                        hv = hgelu[:, 3, GRP * NC:2 * GRP * NC]
                        for g in range(GRP):
                            pe.matmul(bank[7][g * HD:(g + 1) * HD, 0:NC], smalls[:, 0:HD], hk[:, g * NC:(g + 1) * NC], start=True, stop=True)
                        for g in range(GRP):
                            mm = pe.matmul(bank[7][0:NC, 64 + g * HD:64 + (g + 1) * HD], hv[:, g * NC:(g + 1) * NC], smalls[:, HD:2 * HD], start=True, stop=True)
                        mm.then_inc(kv_ps, 1)

                    def cmp_scores():
                        pe.wait_ge(kv_sb, 2)
                        for t in range(TT):
                            for r in range(REP):
                                for g in range(GRP):
                                    rows_ = slice(g * HD, (g + 1) * HD)
                                    c0 = (t * REP + r) * 16
                                    mm = pe.matmul(bank[6 + g][:, c0:c0 + NC], qkT[rows_, T_NQ + r, t * P:(t + 1) * P], kcT[rows_, 0:NC], start=True, stop=True)
                        mm.then_inc(sc_ps, 1)

                    def scores(u):
                        kind, o, i = UNITS[u]
                        b0, b1 = bank[2 * (u % 2)], bank[2 * (u % 2) + 1]
                        if u >= 2:
                            pe.wait_ge(e_ready, u - 1)
                        if u == 0:
                            pe.wait_ge(out_dve, 2 * len(ROPE_PIECES))
                            pe.wait_ge(c_ready, 4)
                        if kind == "dsa":
                            pe.wait_ge(dmask_ready, 1)

                        def causal(h, b, q, a, w):
                            return pe.matmul(b[:, a + w - P:a + w], identb[:, :], cmask[:, :], start=False, stop=True)

                        def fox(h, b, q, a, w):
                            c0 = (2 * i + h) * T
                            pe.matmul(b[:, a:a + w], c_rows[0:1, 0, c0 + q * P:c0 + (q + 1) * P], ones2[0:1, 0:w], start=False, stop=False)
                            pe.matmul(b[:, a:a + w], ones[0:1, 0:P], c_rows[0:1, 1, c0:c0 + w], start=False, stop=False)
                            return causal(h, b, q, a, w)

                        def chosen(h, b, q, a, w):
                            return pe.matmul(b[:, a:a + w], identb[:, :], dmask[:, a:a + w], start=False, stop=True)

                        ones2 = upper[0:1, 0, :]
                        tq, tk, after = {"fox": (T_FQ + i, T_FK + i, fox), "slc": (T_NQ + i, T_KS, causal),
                                         "win": (T_NQ + i, T_KW, causal), "dsa": (T_DQ + i, T_DK, chosen)}[kind]
                        pair_dots(b0, b1, tq, tk, after).then_inc(s_ready, 1)

                    def values(kind, h, i):
                        c = {"fox": V_F + (2 * i + h) * HD, "slc": V_S + h * HD, "win": V_W + h * HD, "dsa": V_D}[kind]
                        return slice(c, c + HD)

                    def turn_probs(v):
                        what, u = TURNS[v]
                        if v >= 1:
                            pe.wait_ge(pt_sb, v)
                        else:
                            pe.wait_ge(turned_out, 18)
                        if what == "unit":
                            pe.wait_ge(p_ready, u + 1)
                            for h in range(2):
                                for j in range(3):
                                    mm = pe.transpose(bank[4 + h][:, j * P:(j + 1) * P], prob[:, u % 2, h, j * P:(j + 1) * P], ident[:, :])
                        else:
                            pe.wait_ge(pc_ready, 1)
                            for g in range(GRP):
                                for t in range(TT):
                                    mm = pe.transpose(bank[4][0:NC, (g * TT + t) * P:(g * TT + t + 1) * P], pc[:, t, u * GRP + g, 0:NC], ident[:, :])
                        mm.then_inc(pt_ps, 1)

                    def add_values(v):
                        what, u = TURNS[v]
                        pe.wait_ge(pt_sb, v + 1)
                        if what == "unit":
                            kind, o, i = UNITS[u]
                            first, last = kind != "win", kind not in ("slc", "win")
                            if first and o >= 2:
                                pe.wait_ge(o_sb, o - 1)
                            if o == 0:
                                pe.wait_ge(sc_sub, 1)
                            ob = bank[6 + o % 2]
                            for h in range(2):
                                pe.matmul(ob[h * HD:(h + 1) * HD, 0:T], vbuf[:, 0, values(kind, h, i)], probT[:, h, 0:T], start=first, stop=False, skip_group_check=True)
                            for h in range(2):
                                mm = pe.matmul(ob[h * HD:(h + 1) * HD, P:T], vbuf[:, 1, values(kind, h, i)], probT[:, h, T:T + P], start=False, stop=last, skip_group_check=True)
                        else:
                            o = 2 + u
                            for g in range(GRP):
                                mm = pe.matmul(bank[6 + o % 2][g * HD:(g + 1) * HD, 0:T], vc_sb[0:NC, g, :],
                                               probT[0:NC, :, :].rearrange("p h c -> p (h c)")[:, g * T:(g + 1) * T], start=False, stop=True, skip_group_check=True)
                        mm.then_inc(pv, 1)

                    scores(0)
                    cmp_kv()
                    scores(1)
                    cmp_scores()
                    for v, (what, u) in enumerate(TURNS):
                        turn_probs(v)
                        if what == "unit" and u + 2 < NU:
                            scores(u + 2)
                        add_values(v)

                    pe.wait_ge(e_ready, NU)
                    for n in range(N_OUT_PIECES):
                        m = N_IN_PIECES + 2 + n
                        pe.wait_ge(piece_ld[m % RING], 16 * (m // RING + 1))
                        pe.wait_ge(o_sb, 8)
                        for t in range(TT):
                            for k in range(KD):
                                mm = pe.matmul(bank[2 * t + n // 2][:, (n % 2) * PIECE:(n % 2 + 1) * PIECE],
                                               xT[:, k, t * P:(t + 1) * P], piece[m % RING][:, k, :], start=(k == 0), stop=(k == KD - 1))
                        mm.then_inc(mix, 1)

                    turn_x(4)
                    pe.wait_ge(wr_ld, 16)
                    for t in range(TT):
                        for k in range(KD):
                            mm = pe.matmul(bank[6][:, t * NE:(t + 1) * NE], xT[:, k, t * P:(t + 1) * P], wr[:, k, :], start=(k == 0), stop=(k == KD - 1))
                    mm.then_inc(logits, 1)
                    pe.wait_ge(ws_ld, 16)
                    for f in range(4):
                        for k in range(KD):
                            mm = pe.matmul(bank[4 + f // 2][:, (f % 2) * T:(f % 2 + 1) * T], wsh[:, k * 2 * EF + f * P:k * 2 * EF + (f + 1) * P],
                                           xT[:, k, :], start=(k == 0), stop=(k == KD - 1))
                    mm.then_inc(sh_ps, 1)
                    pe.wait_ge(sel_ready, 1)
                    sel0, sel1 = rt[:, 2, 0, :], rt[:, 2, 1, :]
                    pe.matmul(bank[7][:, 0:NE], upper[:, 0, 0:P], sel0, start=True, stop=True)
                    pe.matmul(bank[7][:, NE:2 * NE], upper[:, 0, P:T], sel0, start=True, stop=False)
                    pe.matmul(bank[7][:, NE:2 * NE], upper[:, 1, P:T], sel1, start=False, stop=True)
                    pe.matmul(bank[7][0:1, 2 * NE:3 * NE], ones[:, 0:1], sel0, start=True, stop=False)
                    pe.matmul(bank[7][0:1, 2 * NE:3 * NE], ones[:, 0:1], sel1, start=False, stop=True).then_inc(ranks, 1)
                    pe.wait_ge(sh_h, 1)
                    for t in range(TT):
                        for c in range(2):
                            for f in range(2):
                                mm = pe.matmul(bank[2 * t + c][:, :], shT[:, f, t * P:(t + 1) * P], wsh[:, EGU + f * D + c * 512:EGU + f * D + (c + 1) * 512],
                                               start=(f == 0), stop=False, skip_group_check=True)
                    mm.then_inc(sh_dn, 1)

                    A, B, C, R = bank[4], bank[5], bank[6], bank[7]
                    R_hot = R[:, 0:P].bitcast(BF16)

                    def gather(sw, par, n, k):
                        pe.wait_ge(sw.hot, k)
                        H = hot[par]
                        for t in range(TT):
                            pe.transpose(R_hot[:, t * P:(t + 1) * P], H[:, t, :], identb[:, :])
                        for t in range(TT):
                            pe.matmul(R[:, P:P + 6], H[:, t, :], gw2[:, t, bass.ds(n * 2, 2), :].rearrange("p e h -> p (e h)"), start=(t == 0), stop=(t == TT - 1))
                        for d in range(KD):
                            o = (A, B)[d // 4][:, (d % 4) * P:(d % 4 + 1) * P]
                            for j in range(3 * TT):
                                mm = pe.matmul(o, xs[j // TT][:, j % TT, d * P:(d + 1) * P], H[:, j % TT, :], start=(j == 0), stop=(j == 3 * TT - 1))
                        mm.then_inc(sw.gat, 1)

                    def gate_up(sw, par, W, k):
                        pe.wait_ge(sw.xg, 2 * k)
                        for d in range(KD):
                            for e in range(2):
                                mm = pe.matmul(C[e * SLOTS:(e + 1) * SLOTS, :], xgT[par][:, d, e * SLOTS:(e + 1) * SLOTS],
                                               W[:, e, d * 2 * EF:(d + 1) * 2 * EF], start=(d == 0), stop=(d == KD - 1))
                        mm.then_inc(sw.gu, 1)

                    def turn_h(sw, k):
                        pe.wait_ge(sw.h, k)
                        for f in range(EF // P):
                            mm = pe.transpose(R[:, T + f * P:T + (f + 1) * P], h_sb[:, f * P:(f + 1) * P], ident[:, :])
                        mm.then_inc(sw.ht_ps, 1)

                    def down(sw, W, k):
                        pe.wait_ge(sw.ht, k)
                        for c in range(2):
                            for f in range(2):
                                for e in range(2):
                                    mm = pe.matmul((A, B)[c][e * SLOTS:(e + 1) * SLOTS, :], hT[:, f, e * SLOTS:(e + 1) * SLOTS],
                                                   W[:, e, EGU + f * D + c * 512:EGU + f * D + (c + 1) * 512], start=(f == 0), stop=(f == 1))
                        mm.then_inc(sw.dn, 1)

                    def add_back(sw, par, k):
                        pe.wait_ge(sw.yl, k)
                        pe.wait_ge(sw.hotT, k)
                        for t in range(TT):
                            for c in range(2):
                                for y in (y_hi, y_lo):
                                    mm = pe.matmul(bank[2 * t + c][:, :], hotT[par][:, t * P:(t + 1) * P], y[:, c * 512:(c + 1) * 512],
                                                   start=False, stop=False, skip_group_check=True)
                        mm.then_inc(sw.sc, 1)

                    def step(s, n, i, first=False, last=False):
                        pe.wait_ge(gu_ld[s], 16 * i + 16)
                        gate_up(main, s, ex[s], n + 1)
                        if not last:
                            if not first:
                                pe.wait_ge(main.yl, n)
                            pe.wait_ge(main.hotT, n + 1)
                            gather(main, 1 - s, n + 1, n + 2)
                        turn_h(main, n + 1)
                        if not first:
                            add_back(main, 1 - s, n)
                        pe.wait_ge(dn_ld[s], 16 * i + 16)
                        if not last:
                            pe.wait_ge(main.xg, 2 * (n + 2))
                        down(main, ex[s], n + 1)

                    pe.wait_ge(split_b, TT)
                    pe.wait_ge(split_c, TT)
                    pe.wait_ge(sh_h, 1)
                    pe.wait_ge(routed_ready, 1)
                    gather(main, 0, 0, 1)
                    step(0, 0, 0, first=True)
                    with pe.Fori(0, PAIRS // 2 - 1) as i:
                        step(1, 2 * i + 1, i)
                        step(0, 2 * i + 2, i + 1)
                    step(1, PAIRS - 1, PAIRS // 2 - 1, last=True)
                    add_back(main, 1, PAIRS)

                    more = pe.value_load(flag[0:1, 0:1], min_val=0, max_val=1)
                    with pe.If(more > 0):
                        pe.nop().then_inc(over.sc, 1)
                        with pe.Fori(0, ROUNDS - 1) as r:
                            with pe.Fori(0, PAIRS) as n:
                                k = r * PAIRS + n + 1
                                gather(over, 0, n, k)
                                pe.wait_ge(over_ld, 16 * k)
                                gate_up(over, 0, ex[0], k)
                                turn_h(over, k)
                                down(over, ex[0], k)
                                add_back(over, 0, k)
                    with pe.Else():
                        pe.nop()
                    pe.nop()

                @block.scalar
                def _(act):
                    own = Order(act, act_own)

                    def copy_xT(first):
                        for g in range(4):
                            t, k0 = g // 2, (g % 2) * 4
                            act.wait_ge(xt_ps, first + g + 1)
                            act.copy(xT[:, k0:k0 + 4, t * P:(t + 1) * P], bank[4 + g % 2][:, :].rearrange("p (k c) -> p k c", k=4)).then_inc(xt_sb, 1)

                    def read_plain(c):
                        for t in range(TT):
                            act.wait_ge(proj, 2 * c + t + 1)
                            ps, slot = ps_proj(c, t), (2 * c + t) % 4
                            if c == 2:
                                act.copy(vbuf[:, t, 0:V_S], ps[:, 0:V_S]).then_inc(out_act, 1)
                            elif c == 6:
                                act.copy(vbuf[:, t, V_F:V_F + PIECE], ps).then_inc(out_act, 1)
                            elif c == 3:
                                act.wait_ge(turned, 2 + t + 1)
                                act.copy(hq[:, slot, 0:P], ps[:, 0:P]).then_inc(hq_act, 1)
                                act.copy(vbuf[:, t, V_S:V_S + P], ps[:, P:2 * P]).then_inc(out_act, 1)
                            else:
                                if c == 5:
                                    act.wait_ge(turned, 4 + t + 1)
                                act.copy(hq[:, slot, :], ps).then_inc(hq_act, 1)

                    def read_turned(c):
                        for t in range(TT):
                            j = 2 * TURNED.index(c) + t
                            act.wait_ge(turned, j + 1)
                            b = bank[4 + j % 2]
                            cols = slice(t * P, (t + 1) * P)
                            halves = (slice(0, HD), slice(HD, P))
                            if c == 1:
                                for src, n in ((0, T_IK), (1, T_DK)):
                                    for dst in range(2):
                                        own.mark(act.copy(qkT[halves[dst], n, cols], b[halves[src], 0:P]))
                            elif c in TILE_OF:
                                n = TILE_OF[c]
                                src = b[:, 0:2 * P].rearrange("p (a c) -> p a c", a=2)
                                own.mark(act.copy(qkT[:, n:n + 2, cols], src))
                            if c in (1, 3):
                                kv, o = (0, P) if c == 1 else (1, 0)
                                lo = 1 if t == 0 else 0
                                for g in range(GRP):
                                    own.mark(act.copy(cmpT[0:HD, kv, g, cols], b[halves[g], o:o + P]))
                                    own.mark(act.copy(cmpT[HD:P, kv, g, t * P + lo - 1:(t + 1) * P - 1], b[halves[g], o + lo:o + P]))
                            own.settle()
                            act.nop().then_inc(turned_out, 1)

                    def relu_dots(i):
                        act.wait_ge(dots, i + 1)
                        if i == 1:
                            act.wait_ge(dots_free, 2)
                        for h in range(2):
                            act.activation(rtmp[:, h, :], bank[6 + h][:, 0:3 * P], ACT.Relu).then_inc(dots_out, 1)

                    def misc():
                        own.settle()
                        act.wait_ge(out_act, 2)
                        for t in range(TT):
                            act.activation(gates[:, t, :], vbuf[:, t, M_G:M_G + 18], ACT.Exp, scale=-1.0).then_inc(gate_exp, 1)
                        act.wait_ge(fabs, 1)
                        own.link(act.activation(fz[:, 2, :], fz[:, 1, :], ACT.Exp, scale=-1.0))
                        act.activation(fz[:, 3, :], fz[:, 2, :], ACT.Ln, bias=1.0).then_inc(fln, 1)

                    def fox_rows_out():
                        act.wait_ge(cum, 1)
                        act.wait_ge(proj, 2 * N_IN_PIECES)
                        for b in range(2):
                            o = slice(b * 512, (b + 1) * 512)
                            act.activation(c_rows[0:1, 0, o], bank[6 + b][0:1, :], ACT.Copy, scale=1 / SCALE).then_inc(c_ready, 1)
                            act.activation(c_rows[0:1, 1, o], bank[6 + b][0:1, :], ACT.Copy, scale=-1 / SCALE).then_inc(c_ready, 1)

                    copy_xT(0)
                    read_turned(0)
                    read_plain(2)
                    misc()
                    read_turned(1)
                    relu_dots(0)
                    read_plain(3)
                    relu_dots(1)
                    read_plain(4)
                    read_turned(3)
                    read_plain(5)
                    read_turned(4)
                    read_plain(6)
                    read_turned(5)
                    for c in range(8, 11):
                        read_turned(c - 1)
                    fox_rows_out()
                    read_turned(10)

                    act.wait_ge(gelu_u, 1)
                    act.activation(hgelu[:, 2, :], hgelu[:, 1, :], ACT.Exp, scale=1.0).then_inc(gelu_e, 1)
                    act.wait_ge(kv_ps, 1)
                    act.copy(kcT[:, 0:NC], bank[7][:, 0:NC]).then_inc(kv_sb, 1)
                    act.copy(vc_sb[0:NC, :, :], bank[7][0:NC, 64:64 + P].rearrange("p (g c) -> p g c", g=GRP)).then_inc(kv_sb, 1)
                    act.wait_ge(sc_sub, 1)
                    act.activation(pc[:, :, :, 0:NC], pc[:, :, :, 0:NC], ACT.Exp, scale=SCALE).then_inc(sc_exp, 1)

                    def exps(u):
                        act.wait_ge(m_ready, u + 1)
                        if u >= 2:
                            act.wait_ge(pt_ps, TURN_OF_UNIT[u - 2] + 1)
                        for h in range(2):
                            for q, (a, w) in enumerate(((0, P), (P, 2 * P))):
                                c = 2 * h + q
                                own.mark(act.activation(prob[:, u % 2, h, a:a + w], bank[2 * (u % 2) + h][:, a:a + w], ACT.Exp,
                                                        bias=sm_neg[:, u % 2, c:c + 1], scale=SCALE, accum_out=sm_sum[:, u % 2, c:c + 1]))
                        own.settle()
                        act.nop().then_inc(e_ready, 1)

                    exps(0)
                    for v, (what, u) in enumerate(TURNS):
                        if what == "unit" and u + 1 < NU:
                            exps(u + 1)
                        act.wait_ge(pt_ps, v + 1)
                        if v >= 1:
                            act.wait_ge(pv, v)
                        if what == "unit":
                            for h in range(2):
                                own.mark(act.copy(probT[:, h, :], bank[4 + h][:, 0:3 * P]))
                        else:
                            own.mark(act.copy(probT[0:NC, :, :].rearrange("p h c -> p (h c)")[:, 0:2 * T], bank[4][0:NC, :]))
                        own.settle()
                        act.nop().then_inc(pt_sb, 1)
                        kind, o, _ = UNITS[u] if what == "unit" else ("cmp", 2 + u, 0)
                        if kind in ("fox", "dsa", "cmp"):
                            act.wait_ge(pv, v + 1)
                            act.copy(xT[:, o, :], bank[6 + o % 2][:, 0:T]).then_inc(o_sb, 1)

                    def rstd(first):
                        for t in range(TT):
                            act.wait_ge(ln_var, first + t + 1)
                            own.link(act.activation(ln_s[:, t, 16:17], ln_s[:, t, 15:16], ACT.Ln))
                            act.activation(ln_s[:, t, 17:18], ln_s[:, t, 16:17], ACT.Exp, scale=-0.5).then_inc(ln_rs, 1)

                    rstd(0)
                    copy_xT(4)
                    act.wait_ge(mix, N_OUT_PIECES)
                    for t in range(TT):
                        act.copy(xs[0][:, t, :], x_sb[:, t, :]).then_inc(split_a, 1)
                    for t in range(TT):
                        act.wait_ge(split_rest, t + 1)
                        act.copy(xs[1][:, t, :], rest[:, t, :]).then_inc(split_b, 1)
                    act.wait_ge(logits, 1)
                    act.activation(rt[:, 0, :, :].rearrange("p t e -> p (t e)"), bank[6][:, 0:TT * NE], ACT.Exp, scale=-1.0).then_inc(lg_exp, 1)
                    act.wait_ge(sh_ps, 1)
                    act.activation(shS[:, :, :].rearrange("p f c -> p (f c)"), bank[4][:, :], ACT.Exp, scale=-1.0).then_inc(sh_exp, 1)

                    A, B, C = bank[4], bank[5], bank[6]

                    def sigmoid(sw, k):
                        act.wait_ge(sw.gu, k)
                        act.activation(sig[:, :], C[:, 0:EF], ACT.Sigmoid).then_inc(sw.ex, 1)

                    def read_gathered(sw, par, k):
                        act.wait_ge(sw.gat, k)
                        act.copy(xgT[par][:, 0:4, :], A[:, :].rearrange("p (k c) -> p k c", k=4)).then_inc(sw.xg, 1)

                    def y_high(sw, par, k):
                        act.wait_ge(sw.dn, k)
                        act.wait_ge(sw.hotT, k)
                        for c in range(2):
                            act.activation(y_hi[:, c * 512:(c + 1) * 512], (A, B)[c][:, :], ACT.Copy, scale=gslot[:, par:par + 1]).then_inc(sw.yh, 1)

                    def step(s, n, last=False):
                        sigmoid(main, n + 1)
                        if not last:
                            read_gathered(main, 1 - s, n + 2)
                        y_high(main, s, n + 1)

                    act.wait_ge(sh_h, 1)
                    read_gathered(main, 0, 1)
                    step(0, 0)
                    with act.Fori(0, PAIRS // 2 - 1) as i:
                        step(1, 2 * i + 1)
                        step(0, 2 * i + 2)
                    step(1, PAIRS - 1, last=True)
                    more = act.value_load(flag[0:1, 0:1], min_val=0, max_val=1)
                    with act.If(more > 0):
                        with act.Fori(0, ROUNDS - 1) as r:
                            with act.Fori(0, PAIRS) as n:
                                k = r * PAIRS + n + 1
                                read_gathered(over, 0, k)
                                sigmoid(over, k)
                                y_high(over, 0, k)
                    with act.Else():
                        act.nop()
                    rstd(TT)

                @block.vector
                def _(dve):
                    own = Order(dve, dve_own)
                    V = nc.vector

                    def rotate(c):
                        for t in range(TT):
                            j = 2 * TURNED.index(c) + t
                            slot = (2 * c + t) % 4
                            dve.wait_ge(proj, 2 * c + t + 1)
                            if c >= 7:
                                prev = {7: 5, 8: 4, 9: 7, 10: 8}[c]
                                dve.wait_ge(turned, 2 * TURNED.index(prev) + t + 1)
                            ps = ps_proj(c, t)
                            ph = ps.rearrange("p (h a c) -> p h a c", h=4, a=2)
                            cs = rope_cs[:, 0, t:t + 1, :].broadcast_to([P, 4, HD])
                            tm = rope_tmp[:, :].rearrange("p (h a c) -> p h a c", h=4, a=2)
                            own.mark(V.tensor_tensor(hq[:, slot, :].rearrange("p (h c) -> p h c", h=4), ps.rearrange("p (h c) -> p h c", h=4), cs, ALU.mult))
                            for a in range(2):
                                sn = rope_cs[:, 1, t:t + 1, a * 32:(a + 1) * 32].broadcast_to([P, 4, 32])
                                own.mark(V.tensor_tensor(tm[:, :, a, :], ph[:, :, 1 - a, :], sn, ALU.mult))
                            own.settle()
                            dve.nop().then_inc(out_dve, 1)
                            own.link(V.tensor_tensor(hq[:, slot, :], hq[:, slot, :], rope_tmp[:, :], ALU.add))
                            dve.nop().then_inc(hq_dve, 1)

                    def misc():
                        dve.wait_ge(out_act, 2)
                        dve.wait_ge(small_ld, 32)
                        for t in range(TT):
                            own.mark(V.tensor_tensor(fz[:, 0, t * 4:t * 4 + 4], vbuf[:, t, M_F:M_F + 4], biases[:, 0:FOX], ALU.add))
                            own.mark(V.tensor_scalar(w_idx[:, t, :], vbuf[:, t, M_W:M_W + 4], IDX ** -0.5, HD ** -0.5, ALU.mult, ALU.mult))
                        own.settle()
                        own.link(V.tensor_scalar(fz[:, 1, :], fz[:, 0, :], -1.0, None, ALU.mult))
                        V.tensor_tensor(fz[:, 1, :], fz[:, 1, :], fz[:, 0, :], ALU.max).then_inc(fabs, 1)
                        dve.wait_ge(gate_exp, 2)
                        own.link(V.tensor_scalar(gates[:, :, :], gates[:, :, :], 1.0, None, ALU.add))
                        own.link(V.reciprocal(gates[:, :, :], gates[:, :, :]))
                        own.link(V.tensor_scalar(fz[:, 0, :], fz[:, 0, :], 0.0, None, ALU.min))
                        dve.wait_ge(fln, 1)
                        V.tensor_tensor(fz[:, 3, :], fz[:, 0, :], fz[:, 3, :], ALU.subtract).then_inc(lf_ready, 1)

                    def index_sum(i):
                        for h in range(2):
                            n = 2 * i + h
                            dve.wait_ge(dots_out, n + 1)
                            for t, (a, w) in enumerate(((0, P), (P, 2 * P))):
                                wt = w_idx[:, t, n:n + 1]
                                if n == 0:
                                    own.mark(V.tensor_scalar(score[:, a:a + w], rtmp[:, h, a:a + w], wt, None, ALU.mult))
                                else:
                                    own.mark(V.scalar_tensor_tensor(score[:, a:a + w], rtmp[:, h, a:a + w], wt, score[:, a:a + w], ALU.mult, ALU.add))
                            own.settle()
                            dve.nop().then_inc(dots_free, 1)

                    def index_top():
                        for a in (0, 2 * P):
                            own.mark(V.tensor_tensor(score[:, a:a + P], score[:, a:a + P], cmask[:, :], ALU.add))
                        own.settle()
                        for a, w in ((0, P), (P, 2 * P)):
                            s = score[:, a:a + w]
                            for _ in range(TOPK // 8):
                                own.link(V.max(top8[:, :], s))
                                own.link(V.match_replace(s, top8[:, :], s, TAKEN))
                        own.link(V.tensor_scalar(score[:, :], score[:, :], -2.0e38, NEG, ALU.is_gt, ALU.mult))
                        for a in (0, 2 * P):
                            own.mark(V.tensor_tensor(score[:, a:a + P], score[:, a:a + P], cmask[:, :], ALU.add))
                        own.settle()
                        V.tensor_copy(dmask[:, :], score[:, :]).then_inc(dmask_ready, 1)

                    def blocks(kv):
                        dve.wait_ge(turned_out, 4 if kv == 0 else 6)
                        dve.wait_ge(small_ld, 32)
                        pe_row = smalls[:, 2 * HD + kv * CPAIRS:2 * HD + (kv + 1) * CPAIRS]
                        for i in range(CPAIRS):
                            src = cmpT[:, kv, :, 2 * i:2 * i + CMP_STRIDE * (NC - 1) + 1:CMP_STRIDE]
                            own.mark(V.tensor_scalar(blkT[:, kv, i, :, :], src, pe_row[:, i:i + 1], None, ALU.add))
                        own.settle()
                        dve.nop().then_inc(blk_ready, 1)

                    rotate(0)
                    rotate(1)
                    misc()
                    index_sum(0)
                    index_sum(1)
                    blocks(0)
                    blocks(1)
                    index_top()
                    for c in range(7, 11):
                        rotate(c)

                    def maxima(u):
                        dve.wait_ge(s_ready, u + 1)
                        m = sm_max[:, u % 2, :].rearrange("p (h q) -> p h q", h=2)
                        for h in range(2):
                            for q, (a, w) in enumerate(((0, P), (P, 2 * P))):
                                own.mark(V.tensor_reduce(m[:, h, q:q + 1], bank[2 * (u % 2) + h][:, a:a + w], AX, ALU.max))
                        own.settle()
                        V.tensor_scalar(sm_neg[:, u % 2, :], sm_max[:, u % 2, :], -SCALE, None, ALU.mult).then_inc(m_ready, 1)

                    gv = gates[:, :, :].rearrange("p t (b g r) -> p b r g t", b=3, g=GRP)

                    def normalise(u):
                        kind, o, i = UNITS[u]
                        dve.wait_ge(e_ready, u + 1)
                        r = sm_r[:, u % 2, :]
                        own.link(V.reciprocal(r, sm_sum[:, u % 2, :]))
                        if kind in ("slc", "win"):
                            rv = r.rearrange("p (h q) -> p h q", h=2)
                            own.link(V.tensor_tensor(rv, rv, gv[:, 1 if kind == "slc" else 2, i], ALU.mult))
                        for h in range(2):
                            for q, (a, w) in enumerate(((0, P), (P, 2 * P))):
                                pr = prob[:, u % 2, h, a:a + w]
                                own.mark(V.tensor_scalar(pr, pr, r[:, 2 * h + q:2 * h + q + 1], None, ALU.mult))
                        own.settle()
                        dve.nop().then_inc(p_ready, 1)

                    dve.wait_ge(hid, 2)
                    h_ps = bank[6][:, 0:2 * GRP * NC]
                    hx, hu, he, ho = (hgelu[:, j, :] for j in range(4))
                    own.link(V.tensor_copy(hx, h_ps))
                    own.link(V.tensor_tensor(hu, hx, hx, ALU.mult))
                    c1 = float(np.sqrt(2 / np.pi))
                    own.link(V.tensor_scalar(hu, hu, -2 * c1 * 0.044715, -2 * c1, ALU.mult, ALU.add))
                    own.link(V.tensor_tensor(hu, hu, hx, ALU.mult))
                    V.tensor_scalar(hu, hu, 80.0, None, ALU.min).then_inc(gelu_u, 1)
                    maxima(0)
                    dve.wait_ge(gelu_e, 1)
                    own.link(V.tensor_scalar(he, he, 1.0, None, ALU.add))
                    own.link(V.reciprocal(he, he))
                    V.tensor_tensor(ho, hx, he, ALU.mult).then_inc(gelu_ready, 1)
                    maxima(1)
                    dve.wait_ge(sc_ps, 1)
                    heads = REP * GRP
                    for t in range(TT):
                        for g in range(GRP):
                            ps = bank[6 + g][:, t * REP * 16:(t + 1) * REP * 16].rearrange("p (h c) -> p h c", h=REP)[:, :, 0:NC]
                            own.mark(V.tensor_tensor(pc[:, t, g:heads:GRP, 0:NC], ps, cvis[:, t:t + 1, 0:NC].broadcast_to([P, REP, NC]), ALU.add))
                    own.settle()
                    own.link(V.tensor_reduce(pcs[:, 0, :].rearrange("p (t h) -> p t h", t=TT), pc[:, :, :, 0:NC], AX, ALU.max))
                    for t in range(TT):
                        mx = pcs[:, 0, t * heads:(t + 1) * heads].unsqueeze(2).broadcast_to([P, heads, NC])
                        own.mark(V.tensor_tensor(pc[:, t, :, 0:NC], pc[:, t, :, 0:NC], mx, ALU.subtract))
                    own.settle()
                    dve.nop().then_inc(sc_sub, 1)

                    def cmp_norm():
                        dve.wait_ge(sc_exp, 1)
                        own.link(V.tensor_reduce(pcs[:, 1, :].rearrange("p (t h) -> p t h", t=TT), pc[:, :, :, 0:NC], AX, ALU.add))
                        own.link(V.reciprocal(pcs[:, 2, :], pcs[:, 1, :]))
                        for t in range(TT):
                            w = pcs[:, 2, t * heads:(t + 1) * heads]
                            wv = w.rearrange("p (r g) -> p r g", r=REP)
                            own.link(V.scalar_tensor_tensor(wv, wv, anyvis[:, t:t + 1], gv[:, 0, :, :, t], ALU.mult, ALU.mult))
                            own.mark(V.tensor_tensor(pc[:, t, :, 0:NC], pc[:, t, :, 0:NC], w.unsqueeze(2).broadcast_to([P, heads, NC]), ALU.mult))
                        own.settle()
                        dve.nop().then_inc(pc_ready, 1)

                    normalise(0)
                    cmp_norm()
                    for u in range(1, NU):
                        if u + 1 < NU:
                            maxima(u + 1)
                        normalise(u)

                    def norm(first):
                        for t in range(TT):
                            for c in range(2):
                                xx = x_sb[:, t, c * 512:(c + 1) * 512]
                                own.link(V.scalar_tensor_tensor(xx, xx, ALPHA, bank[2 * t + c][:, :], ALU.mult, ALU.add))
                                own.mark(V.bn_stats(ln_s[:, t, c * 6:c * 6 + 6], xx))
                            own.settle()
                            own.link(V.bn_aggr(ln_s[:, t, 12:14], ln_s[:, t, 0:12]))
                            V.tensor_scalar(ln_s[:, t, 15:16], ln_s[:, t, 13:14], LN_EPS, None, ALU.add).then_inc(ln_var, 1)
                        for t in range(TT):
                            dve.wait_ge(ln_rs, first + t + 1)
                            y0, h, r = ln_s[:, t, 17:18], ln_s[:, t, 18:19], ln_s[:, t, 19:20]
                            own.link(V.tensor_tensor(h, y0, y0, ALU.mult))
                            own.link(V.tensor_tensor(h, h, ln_s[:, t, 15:16], ALU.mult))
                            own.link(V.tensor_scalar(h, h, -0.5, 1.5, ALU.mult, ALU.add))
                            own.link(V.tensor_tensor(r, y0, h, ALU.mult))
                            xx = x_sb[:, t, :]
                            own.link(V.tensor_scalar(xx, xx, ln_s[:, t, 12:13], r, ALU.subtract, ALU.mult))
                            dve.wait_ge(ln_ld, 16 * (2 if first else 1))
                            own.link(V.tensor_tensor(xx, xx, lnp[:, 0, :], ALU.mult))
                            V.tensor_tensor(xx, xx, lnp[:, 1, :], ALU.add).then_inc(ln_done, 1)

                    dve.wait_ge(mix, N_OUT_PIECES)
                    norm(0)
                    dve.wait_ge(ln_done, TT)
                    dve.nop().then_inc(ln_used, 1)
                    for t in range(TT):
                        dve.wait_ge(split_a, t + 1)
                        V.tensor_tensor(rest[:, t, :], x_sb[:, t, :], xs[0][:, t, :], ALU.subtract).then_inc(split_rest, 1)
                    for t in range(TT):
                        dve.wait_ge(split_b, t + 1)
                        V.tensor_tensor(xs[2][:, t, :], rest[:, t, :], xs[1][:, t, :], ALU.subtract).then_inc(split_c, 1)

                    sg, sb, sl, gw, rk = (rt[:, j, :, :] for j in range(5))
                    dve.wait_ge(lg_exp, 1)
                    own.link(V.tensor_scalar(sg, sg, 1.0, None, ALU.add))
                    own.link(V.reciprocal(sg, sg))
                    own.link(V.tensor_tensor(sb, sg, biases[:, FOX:FOX + NE].unsqueeze(1).broadcast_to([P, TT, NE]), ALU.add))
                    for t in range(TT):
                        grp, tk, gm = rsm[:, 0:8], rsm[:, 8:16], rsm[:, 16:24]
                        for g in range(NGRP):
                            own.mark(V.max(gw[:, t, g * 8:(g + 1) * 8], sb[:, t, g * 8:(g + 1) * 8]))
                        own.settle()
                        best = gw[:, t, :].rearrange("p (g c) -> p g c", g=NGRP)
                        own.link(V.tensor_reduce(grp, best[:, :, 0:2], AX, ALU.add))
                        own.link(V.max(tk, grp))
                        own.link(V.tensor_scalar(gm, grp, tk[:, 3:4], None, ALU.is_gt))
                        own.link(V.tensor_scalar(rk[:, t, 0:8], grp, tk[:, 3:4], None, ALU.is_equal))
                        own.link(V.tensor_reduce(rk[:, t, 24:25], gm, AX, ALU.add))
                        own.link(V.tensor_tensor_scan(rk[:, t, 8:16], ones[:, 0:8], rk[:, t, 0:8], rk[:, t, 24:25], ALU.mult, ALU.add))
                        own.link(V.tensor_scalar(rk[:, t, 8:16], rk[:, t, 8:16], 4.0, None, ALU.is_le))
                        own.link(V.tensor_tensor(rk[:, t, 0:8], rk[:, t, 0:8], rk[:, t, 8:16], ALU.mult))
                        own.link(V.tensor_tensor(gm, gm, rk[:, t, 0:8], ALU.max))
                        own.link(V.tensor_scalar(rk[:, t, 16:24], gm, -NEG, NEG, ALU.mult, ALU.add))
                        sbg = sb[:, t, :].rearrange("p (g c) -> p g c", g=NGRP)
                        gmb = gm.unsqueeze(2).broadcast_to([P, NGRP, 8])
                        own.link(V.tensor_tensor(sbg, sbg, gmb, ALU.mult))
                        own.link(V.tensor_tensor(sbg, sbg, rk[:, t, 16:24].unsqueeze(2).broadcast_to([P, NGRP, 8]), ALU.add))
                        own.link(V.max(tk, sb[:, t, :]))
                        own.link(V.match_replace(sb[:, t, :], tk, sb[:, t, :], TAKEN))
                        own.link(V.tensor_scalar(sl[:, t, :], sb[:, t, :], -2.0e38, None, ALU.is_le))
                    own.link(V.tensor_tensor(gw, sg, sl, ALU.mult))
                    dve.nop().then_inc(sel_ready, 1)
                    own.link(V.tensor_reduce(rsm[:, 0:TT], gw, AX, ALU.add))
                    own.link(V.reciprocal(rsm[:, 2:2 + TT], rsm[:, 0:TT]))
                    for t in range(TT):
                        own.link(V.tensor_scalar(gw[:, t, :], gw[:, t, :], rsm[:, 2 + t:3 + t], ROUTED_SCALE, ALU.mult, ALU.mult))
                        own.link(V.tensor_copy(gw2[:, t, :, 0], gw[:, t, :]))
                        own.link(V.tensor_tensor(gwr[:, :], gw[:, t, :], gw2[:, t, :, 0], ALU.subtract))
                        own.link(V.tensor_copy(gw2[:, t, :, 1], gwr[:, :]))
                        own.link(V.tensor_tensor(gw2[:, t, :, 2], gwr[:, :], gw2[:, t, :, 1], ALU.subtract))
                    dve.wait_ge(ranks, 1)
                    own.link(V.tensor_copy(rk, bank[7][:, 0:TT * NE].rearrange("p (t e) -> p t e", t=TT)))
                    own.link(V.tensor_reduce(rsm[0:1, 8:9], bank[7][0:1, 2 * NE:3 * NE], AX, ALU.max))
                    own.link(V.tensor_scalar(flag[0:1, 0:1], rsm[0:1, 8:9], float(SLOTS) + 0.5, None, ALU.is_gt))
                    dve.nop().then_inc(routed_ready, 1)

                    dve.wait_ge(sh_exp, 1)
                    flat = "p f c -> p (f c)"
                    s_all = shS[:, :, :].rearrange(flat)
                    own.link(V.tensor_scalar(s_all, s_all, 1.0, None, ALU.add))
                    own.link(V.reciprocal(s_all, s_all))
                    own.link(V.tensor_tensor(s_all, s_all, bank[4][:, :], ALU.mult))
                    V.tensor_tensor(shT[:, :, :].rearrange(flat), s_all, bank[5][:, :], ALU.mult).then_inc(sh_h, 1)
                    dve.wait_ge(sh_h, 1)

                    A, B, C, R = bank[4], bank[5], bank[6], bank[7]
                    R_hot = R[:, 0:P].bitcast(BF16)

                    def one_hot(sw, par, n):
                        for t in range(TT):
                            for e in range(2):
                                ins = V.tensor_scalar(hot[par][:, t, e * SLOTS:(e + 1) * SLOTS], iota1,
                                                      rk[:, t, bass.ds(n * 2 + e, 1)], sl[:, t, bass.ds(n * 2 + e, 1)], ALU.is_equal, ALU.mult)
                                own.mark(ins)
                        own.settle()
                        dve.nop().then_inc(sw.hot, 1)

                    def read_gathered(sw, par, k):
                        dve.wait_ge(sw.gat, k)
                        V.tensor_copy(xgT[par][:, 4:8, :], B[:, :].rearrange("p (k c) -> p k c", k=4)).then_inc(sw.xg, 1)

                    def read_hotT(sw, par):
                        own.mark(V.tensor_copy(hotT[par][:, :], R_hot))
                        for e in range(2):
                            rows_ = slice(e * SLOTS, (e + 1) * SLOTS)
                            own.mark(V.tensor_reduce(gslot[rows_, par:par + 1], R[rows_, P + 3 * e:P + 3 * e + 3], AX, ALU.add))
                        own.settle()
                        dve.nop().then_inc(sw.hotT, 1)

                    def silu(sw, k):
                        dve.wait_ge(sw.ex, k)
                        own.link(V.tensor_tensor(sig[:, :], sig[:, :], C[:, 0:EF], ALU.mult))
                        V.tensor_tensor(h_sb[:, :], sig[:, :], C[:, EF:2 * EF], ALU.mult).then_inc(sw.h, 1)

                    def read_hT(sw, k):
                        dve.wait_ge(sw.ht_ps, k)
                        V.tensor_copy(hT[:, :, :].rearrange("p f c -> p (f c)"), R[:, T:T + EF]).then_inc(sw.ht, 1)

                    def y_low(sw, par, k):
                        for c in range(2):
                            dve.wait_ge(sw.yh, 2 * k + (c - 1))
                            own.mark(V.scalar_tensor_tensor(y_lo[:, c * 512:(c + 1) * 512], (A, B)[c][:, :], gslot[:, par:par + 1],
                                                            y_hi[:, c * 512:(c + 1) * 512].bitcast(F32), ALU.mult, ALU.subtract))
                        own.settle()
                        dve.nop().then_inc(sw.yl, 1)

                    def step(s, n, first=False, last=False):
                        if not last:
                            one_hot(main, 1 - s, n + 1)
                        silu(main, n + 1)
                        if not last:
                            read_gathered(main, 1 - s, n + 2)
                        read_hT(main, n + 1)
                        if not last:
                            if not first:
                                dve.wait_ge(main.sc, n)
                            read_hotT(main, 1 - s)
                        y_low(main, s, n + 1)
                        own.restart()

                    own.restart()
                    one_hot(main, 0, 0)
                    read_gathered(main, 0, 1)
                    read_hotT(main, 0)
                    step(0, 0, first=True)
                    with dve.Fori(0, PAIRS // 2 - 1) as i:
                        step(1, 2 * i + 1)
                        step(0, 2 * i + 2)
                    step(1, PAIRS - 1, last=True)
                    dve.wait_ge(main.sc, PAIRS)
                    own.restart()
                    more = dve.value_load(flag[0:1, 0:1], min_val=0, max_val=1)
                    with dve.If(more > 0):
                        with dve.Fori(0, ROUNDS - 1) as r:
                            own.link(V.tensor_scalar(rk, rk, float(SLOTS), None, ALU.subtract))
                            own.restart()
                            with dve.Fori(0, PAIRS) as n:
                                k = r * PAIRS + n + 1
                                dve.wait_ge(over.sc, k)
                                one_hot(over, 0, n)
                                read_gathered(over, 0, k)
                                read_hotT(over, 0)
                                silu(over, k)
                                read_hT(over, k)
                                y_low(over, 0, k)
                                own.restart()
                        dve.wait_ge(over.sc, (ROUNDS - 1) * PAIRS + 1)
                    with dve.Else():
                        dve.nop()
                    norm(TT)
                    own.settle()

            for s in names:
                nc.gpsimd.sem_clear(s)
            nc.all_engine_barrier()

        with nc.Block() as block:
            @block.sync
            def _(sp):
                sp.dma_start(out.rearrange("b (t p) d -> p (b t) d", p=P), x_sb[:, :, :]).then_inc(stored, 16)
                sp.wait_ge(stored, 16)


def shape_constants():
    i = np.arange(P)
    tok = np.arange(T)
    half = HD // 2
    inv = np.float32(10000.0) ** (-np.arange(half, dtype=np.float32) * np.float32(2.0 / HD))
    ang = tok.astype(np.float32)[:, None] * inv.astype(np.float32)[None, :]
    cos, sin = np.cos(ang), np.sin(ang)
    rope = np.stack([np.concatenate([cos, cos], 1), np.concatenate([-sin, sin], 1)])
    rope = rope.reshape(2, TT, P, HD).transpose(2, 0, 1, 3)
    last = np.arange(NC) * CMP_STRIDE + CMP_LEN - 1
    vis = last[None, :] <= tok[:, None]
    cvis = np.zeros((T, 16), np.float32)
    cvis[:, :NC] = np.where(vis, 0.0, NEG)
    misc = np.concatenate([cvis.reshape(TT, P, 16).transpose(1, 0, 2).reshape(P, TT * 16),
                           vis.any(1).astype(np.float32).reshape(TT, P).T,
                           np.broadcast_to(np.arange(1, SLOTS + 1, dtype=np.float32), (P, SLOTS))], 1)
    return {
        "ident": np.eye(P, dtype=np.float32), 
        "cmask": np.where(i[None, :] <= i[:, None], 0.0, NEG).astype(np.float32),
        "upper": (tok[:, None] <= tok[None, :]).astype(np.float32).reshape(TT, P, T).transpose(1, 0, 2).copy(),
        "rope": np.ascontiguousarray(rope, np.float32), "misc": np.ascontiguousarray(misc, np.float32),
        "ones": np.ones((P, P), np.float32),
    }


def column_order():
    at, off = {}, 0
    for name, width in (("fox_q", 256), ("fox_k", 256), ("fox_v", 256), ("fox_f", 4), ("nsa_q", 384), ("nsa_kc", 128), ("nsa_vc", 128),
                        ("nsa_ks", 128), ("nsa_vs", 128), ("nsa_kw", 128), ("nsa_vw", 128), ("nsa_g", 18), ("dsa_q", 384),
                        ("dsa_k", 64), ("dsa_v", 64), ("idx_q", 256), ("idx_k", 64), ("idx_w", 4)):
        at[name] = np.arange(off, off + width)
        off += width

    def head(name, h):
        return at[name][h * HD:(h + 1) * HD]

    nq = [head("nsa_q", g * REP + r) for r in range(REP) for g in range(GRP)]
    return [
        at["idx_q"],
        np.concatenate([at["idx_k"], at["dsa_k"], at["nsa_kc"]]),
        np.concatenate([at["nsa_vw"], at["dsa_v"], at["fox_f"], at["nsa_g"], at["idx_w"]]),
        np.concatenate([at["nsa_vc"], at["nsa_vs"]]),
        at["fox_q"], at["fox_k"], at["fox_v"],
        np.concatenate(nq[0:4]),
        np.concatenate(nq[4:6] + [at["nsa_ks"]]),
        at["dsa_q"][0:PIECE],
        np.concatenate([at["dsa_q"][PIECE:], at["nsa_kw"]]),
    ]


def lay_out(inputs):
    g = {k: np.asarray(v) for k, v in inputs.items()}
    L = DEPTH

    def by_partition(w):
        return w.reshape(L, -1, P, w.shape[-1]).transpose(0, 2, 1, 3)

    npieces = N_IN_PIECES + 2 + N_OUT_PIECES
    pieces = np.zeros((L, npieces, P, KD, PIECE), np.float32)
    w_in = by_partition(g["w_in"])
    for n, cols in enumerate(column_order()):
        pieces[:, n, :, :, :len(cols)] = w_in[:, :, :, cols]
    for n, name in enumerate(("cmp_w1_k", "cmp_w1_v")):
        pieces[:, N_IN_PIECES + n] = by_partition(g[name]).reshape(L, P, KD, PIECE)
    heads = ([0, 1, 2, 3] + [FOX + gg * REP + r for r in range(REP) for gg in range(GRP)] + [FOX + NSA + h for h in range(DSA)])
    w_out = g["w_out"].reshape(L, 16, HD, D)[:, heads].reshape(L, D, D)
    w_out = by_partition(w_out)
    for n in range(N_OUT_PIECES):
        pieces[:, N_IN_PIECES + 2 + n] = w_out[:, :, :, n * PIECE:(n + 1) * PIECE]

    def pos(name):
        return g[name].reshape(L, CPAIRS, P).transpose(0, 2, 1)

    small = np.concatenate([g["cmp_w2_k"], g["cmp_w2_v"], pos("cmp_pos_k"), pos("cmp_pos_v")], 2)
    rows = np.concatenate([g["fox_forget_bias"], g["b_router"]], 1)
    lnw = np.stack([np.concatenate([g["ln1_g"], g["ln1_b"]], 1), np.concatenate([g["ln2_g"], g["ln2_b"]], 1)], 1)

    def expert(gate, up, down):
        n = gate.shape[0]
        o = np.empty((n, P, EW), np.float32)
        gu = o[:, :, :EGU].reshape(n, P, KD, 2, EF)
        gu[:, :, :, 0] = gate.reshape(n, KD, P, EF).transpose(0, 2, 1, 3)
        gu[:, :, :, 1] = up.reshape(n, KD, P, EF).transpose(0, 2, 1, 3)
        o[:, :, :EGU] = gu.reshape(n, P, EGU)
        o[:, :, EGU:] = down.reshape(n, EF // P, P, D).transpose(0, 2, 1, 3).reshape(n, P, -1)
        return o

    moe = expert(g["w_gate"].reshape(L * NE, D, EF), g["w_up"].reshape(L * NE, D, EF), g["w_down"].reshape(L * NE, EF, D))
    return {
        "x": g["x"], "pieces": pieces.reshape(L, npieces, P, KD * PIECE), "rows": rows, "small": small,
        "moe_w": moe.reshape(L, NE, P, EW), "ws": expert(g["ws_gate"], g["ws_up"], g["ws_down"]),
        "router": by_partition(g["w_router"]).reshape(L, P, KD * NE), "lnw": lnw,
    }


def kernel(**inputs):
    import concourse.bacc as _bacc
    from concourse.bass_utils import run_bass_kernel_spmd as _run

    nc = _bacc.Bacc("TRN2", target_bir_lowering=False, num_devices=1)
    arrays, args = {}, {}
    for name, a in {**lay_out(inputs), **{"const_" + k: v for k, v in shape_constants().items()}}.items():
        a = np.ascontiguousarray(a)
        arrays[f"in_{name}"] = a
        args[name] = nc.dram_tensor(f"in_{name}", a.shape, mybir.dt.from_np(a.dtype), kind="ExternalInput").ap()
    out = nc.dram_tensor("out_0", (1, T, D), F32, kind="ExternalOutput").ap()
    consts = {k[6:]: args.pop(k) for k in list(args) if k.startswith("const_")}
    build(nc, consts=consts, out=out, **args)
    r = _run(nc, [arrays], core_ids=[0])
    return r.results[0]["out_0"]
```

```python
import numpy as np
import concourse.bass as bass
from concourse import mybir
from contextlib import ExitStack

F32 = mybir.dt.float32
F32R = mybir.dt.float32r
BF16 = mybir.dt.bfloat16
I32 = mybir.dt.int32
ALU = mybir.AluOpType
ACT = mybir.ActivationFunctionType
AX = mybir.AxisListType.X

P = 128
DEPTH, D, T = 2, 1024, 256
TT = T // P
KD = D // P
HD = 64
FOX, NSA, GRP, DSA, IDX = 4, 6, 2, 6, 4
REP = NSA // GRP
SCALE = HD ** -0.5
PIECE = 256
N_IN_PIECES, N_OUT_PIECES = 11, 4
CROWS = 32
RING = 5
STREAM = [("in", c) for c in range(7)] + [("cmp", 0), ("cmp", 1)] + [("in", c) for c in range(7, 11)] + [("out", n) for n in range(4)]
CMP_LEN, CMP_STRIDE = 32, 16
NC = (T - CMP_LEN) // CMP_STRIDE + 1
CPAIRS = CMP_LEN // 2
TOPK = min(256, T // 4)
NE, EF = 64, 256
NGRP = 8
MOE_TOPK = 8
PAIRS = NE // 2
SLOTS = 64
ROUNDS = T // SLOTS
EW = KD * 2 * EF + (EF // P) * D
EGU = KD * 2 * EF
ROUTED_SCALE = 2.5
ALPHA = (2 * DEPTH) ** 0.25
LN_EPS = 1e-5
LN_CUT = (0, 576)
NEG = -1e30
TAKEN = -3.0e38
BIG = 3.0e38

ROPE_PIECES = (0, 1, 7, 8, 9, 10)
TURNED = (0, 1, 3, 4, 5, 7, 8, 9, 10)
TILE_OF = {0: 0, 4: 4, 5: 6, 7: 8, 8: 10, 9: 12, 10: 14}
T_IQ, T_IK, T_DK, T_FQ, T_FK, T_NQ, T_KS, T_DQ, T_KW = 0, 2, 3, 4, 6, 8, 11, 12, 15
V_W, V_D, V_MISC, V_S, V_F = 0, 128, 192, 218, 346
VCOLS = 602
M_F, M_G, M_W = V_MISC, V_MISC + 4, V_MISC + 22

UNITS = ([("fox", 0, 0), ("fox", 1, 1)]
         + [(k, 2 + r, r) for r in range(REP) for k in ("slc", "win")]
         + [("dsa", 5 + i, i) for i in range(3)])
NU = len(UNITS)
TURNS = []
for _u, (_k, _o, _r) in enumerate(UNITS):
    TURNS.append(("unit", _u))
    if _k == "win":
        TURNS.append(("cmp", _r))
TURN_OF_UNIT = {u: v for v, (k, u) in enumerate(TURNS) if k == "unit"}


class Order:

    def __init__(self, eng, sem):
        self.eng, self.sem, self.n = eng, sem, 0

    def mark(self, ins):
        self.n += 1
        ins.then_inc(self.sem, 1)

    def link(self, ins):
        self.mark(ins)
        self.eng.wait_ge(self.sem, self.n)

    def settle(self):
        if self.n:
            self.eng.wait_ge(self.sem, self.n)

    def restart(self):
        self.settle()
        self.eng.sem_clear(self.sem)
        self.n = 0


def build(nc, x, pieces, rows, small, moe_w, ws, router, lnw, consts, out, dbg=None):
    ctx = ExitStack()
    with ctx:
        at = [(nc.sbuf_base + 63) // 64 * 64]

        def place(name, shape, dt=F32, where=None):
            size = int(np.prod(shape[1:])) * (2 if dt == BF16 else 4)
            size = (size + 31) // 32 * 32
            start = at[0] if where is None else where[0]
            t = nc.alloc_sbuf_tensor_at(name, shape, dt, offset=start)
            if where is None:
                at[0] += size
            else:
                where[0] += size
            return t

        ex = [place(f"expert_weights{s}", [P, 2, EW]) for s in range(2)]
        ring_at = at[0]
        piece = [place(f"piece{s}", [P, KD, PIECE]) for s in range(RING)]
        moe_at, ring_end = [ring_at], at[0]
        x_sb = place("x_sb", [P, TT, D])
        xT = place("xT", [P, KD, T])
        shared_at = at[0]
        qkT = place("qkT", [P, 16, T])
        cmpT = place("cmpT", [P, 2, GRP, T])
        hq = place("hq", [P, 4, PIECE])
        assert at[0] - shared_at == EW * 4
        ln_at = at[0]
        prob = place("prob", [P, 2, 2, 3 * P])
        probT = [place("probT0", [P, 2, 3 * P]), place("probT1", [P, 2, 3 * P], where=[shared_at + 4 * 16 * T])]
        c_rows = place("c_rows", [P, 2, T], where=[ln_at + 4 * 2 * 3 * P])
        vbuf = place("vbuf", [P, TT, VCOLS])
        score = place("score", [P, 3 * P])
        rtmp = place("rtmp", [P, 2, 3 * P], where=[ln_at])
        dmask = place("dmask", [P, 3 * P], BF16)
        route_at = at[0]
        blkT = place("blkT", [P, 2, CPAIRS, CROWS])
        rope_tmp = place("rope_tmp", [P, PIECE])
        gates = place("gates", [P, TT, 18])
        fz = place("fz", [P, 4, TT * 4])
        sm_neg = place("sm_neg", [P, 2, 4])
        sm_max = place("sm_max", [P, 2, 4])
        sm_sum = place("sm_sum", [P, 2, 4])
        sm_r = place("sm_r", [P, 2, 4])
        top8 = place("top8", [P, 8])
        w_idx = place("w_idx", [P, TT, IDX])
        hgelu = place("hgelu", [2 * CROWS, 3, P])
        hgT = place("hgT", [P, 2 * CROWS])
        kcT = place("kcT", [P, 16])
        vc_sb = place("vc_sb", [16, GRP, HD])
        pc = place("pc", [P, TT, REP * GRP, 16])
        pcs = place("pcs", [P, 4, TT * REP * GRP])
        smalls = place("smalls", [P, 2 * HD + 2 * CPAIRS])
        biases = place("biases", [P, FOX + NE])
        ln_s = place("ln_s", [P, TT, 24])
        ident = place("ident", [P, P])
        identb = place("identb", [P, P], BF16)
        cmask = place("cmask", [P, 2, P], BF16)
        upper = place("upper", [P, TT, T])
        rope_cs = place("rope_cs", [P, 2, TT, HD])
        misc_c = place("misc_c", [P, TT * 16 + TT + SLOTS + 4])
        cvis = misc_c[:, 0:TT * 16].rearrange("p (t c) -> p t c", t=TT)
        anyvis = misc_c[:, TT * 16:TT * 16 + TT]
        iota1 = misc_c[:, TT * 16 + TT:TT * 16 + TT + SLOTS]
        row_mix = misc_c[:, TT * 16 + TT + SLOTS:]
        ones = place("ones", [P, T])
        assert at[0] <= nc.sbuf_usable_end

        cmask_f = place("cmask_f", [P, P], where=[shared_at])
        wsh = place("shared_weights", [P, EW], where=[shared_at])
        lnp = place("ln_rows", [P, 2, D], where=[ln_at])
        ra = [route_at]
        wr = place("router_w", [P, KD, NE], where=ra)
        rt = place("route", [P, 5, TT, NE], where=[ln_at + 4 * 2 * D + 0])
        xs = [place(f"x_part{j}", [P, TT, D], BF16, where=moe_at) for j in range(3)]
        xgT = [place(f"gathered{s}", [P, KD, P], F32, where=moe_at) for s in range(2)]
        y_hi = place("y_hi", [P, D], F32R, where=moe_at)
        y_lo = place("y_lo", [P, D], F32R, where=moe_at)
        rest = place("x_rest", [P, TT, D], F32, where=[moe_at[0] - 8 * D])
        hot = [place(f"hot{s}", [P, TT, P], BF16, where=moe_at) for s in range(2)]
        hotT = [place(f"hotT{s}", [P, T], F32R, where=moe_at) for s in range(2)]
        h_sb = place("h_sb", [P, EF], F32, where=moe_at)
        hT = place("hT", [P, EF // P, P], F32, where=moe_at)
        sig = place("sig", [P, EF], F32, where=moe_at)
        assert moe_at[0] <= ring_end
        gw2 = place("gate_weights", [P, TT, NE, 3], BF16, where=ra)
        gwr = place("gate_rest", [P, NE], F32, where=ra)
        gslot = place("gate_slot", [P, 2], F32, where=ra)
        flag = place("overflow", [1, 1], I32, where=ra)
        rsm = place("route_small", [P, 24], F32, where=ra)
        assert ra[0] <= route_at + 4 * 2 * CPAIRS * CROWS + 4 * PIECE, ra[0] - route_at
        shT = place("shared_hT", [P, 2, T], F32, where=[ring_at + 6 * TT * D + 4 * D])
        shS = place("shared_sig", [P, 2, T], F32, where=[ring_at + 6 * TT * D + 4 * D + 8 * T])

        psum = ctx.enter_context(nc.psum_tensor("psum", [P, 8, 512], F32))
        bank = [psum[:, b, :] for b in range(8)]

        names = []

        def sem(name):
            s = ctx.enter_context(nc.semaphore(name))
            names.append(s)
            return s

        once = ctx.enter_context(nc.semaphore("constants_loaded"))
        x_ld = ctx.enter_context(nc.semaphore("x_loaded"))
        stored = ctx.enter_context(nc.semaphore("output_stored"))
        piece_ld = [sem(f"piece_loaded{s}") for s in range(RING)]
        gu_ld = [sem(f"gate_up_loaded{s}") for s in range(2)]
        dn_ld = [sem(f"down_loaded{s}") for s in range(2)]
        small_ld, ln_ld, ws_ld, wr_ld = sem("smalls_loaded"), sem("ln_rows_loaded"), sem("shared_loaded"), sem("router_loaded")
        xt_ps, xt_sb = sem("x_transposed"), sem("xT_ready")
        proj = sem("projected")
        out_dve, out_act = sem("projection_rotated"), sem("projection_copied")
        hq_dve, hq_act = sem("rotated_heads"), sem("plain_heads")
        turned, turned_out = sem("heads_transposed"), sem("heads_in_sbuf")
        dots, dots_out = sem("index_dots"), sem("index_relu")
        dots_free = sem("index_relu_used")
        dmask_ready = sem("dsa_mask_ready")
        misc_rd, gate_exp, gates_ready = sem("misc_ready"), sem("gate_exp"), sem("gates_ready")
        fabs, fln, lf_ready, cum, c_ready = sem("fox_abs"), sem("fox_ln"), sem("fox_log_forget"), sem("fox_cumsum"), sem("fox_rows_ready")
        blk_ready, hid, gelu_u, gelu_e, gelu_ready = sem("cmp_blocks"), sem("cmp_hidden"), sem("gelu_arg"), sem("gelu_exp"), sem("gelu_ready")
        kv_ps, kv_sb = sem("cmp_kv"), sem("cmp_kv_sb")
        sc_ps, sc_sub, sc_exp, pc_ready = sem("cmp_scores"), sem("cmp_shifted"), sem("cmp_exp"), sem("cmp_probs")
        s_ready, m_ready, e_ready, p_ready = sem("scores"), sem("row_max"), sem("exps"), sem("probs")
        pt_ps, pt_sb, pv, o_sb = sem("probs_turned"), sem("probsT_ready"), sem("values_added"), sem("heads_out")
        mix = sem("mixed")
        ln_var, ln_rs, ln_half = sem("ln_variance"), sem("ln_rstd0"), sem("ln_half_normalised")
        ln_done, ln_done_pool = sem("ln_done_by_vector"), sem("ln_done_by_gpsimd")
        pad_ready, hg_ps, hg_sb = sem("block_padding_zero"), sem("gelu_turned"), sem("geluT_ready")
        split_a, split_rest, split_b, split_c = sem("x_part0_ready"), sem("x_rest_ready"), sem("x_part1_ready"), sem("x_part2_ready")
        logits, lg_exp, sel_ready, ranks, routed_ready = sem("router_logits"), sem("router_exp"), sem("selected"), sem("ranks"), sem("routes_ready")
        sh_ps, sh_exp, sh_h = sem("shared_gate_up"), sem("shared_exp"), sem("shared_h")
        dve_own, act_own, pool_own = sem("vector_order"), sem("scalar_order"), sem("pool_order")

        class Sweep:

            def __init__(self, tag):
                self.hot, self.gat, self.xg, self.hotT = sem(tag + "hot_ready"), sem(tag + "gathered"), sem(tag + "gathered_sb"), sem(tag + "hotT_ready")
                self.gu, self.ex, self.h = sem(tag + "gate_up"), sem(tag + "sigmoid"), sem(tag + "h_ready")
                self.ht_ps, self.ht = sem(tag + "h_transposed"), sem(tag + "hT_ready")
                self.dn, self.yh, self.yl, self.sc = sem(tag + "down"), sem(tag + "y_hi_ready"), sem(tag + "y_lo_ready"), sem(tag + "added_back")

        main, over = Sweep("main_"), Sweep("over_")
        over_ld = sem("over_loaded")
        combined = sem("experts_combined")
        early_ps, early_sb = ctx.enter_context(nc.semaphore("first_x_transposed")), ctx.enter_context(nc.semaphore("first_xT_ready"))
        early_piece = ctx.enter_context(nc.semaphore("first_piece_loaded"))
        piece_ahead = sem("next_layers_piece_loaded")

        def piece_count(n):
            return 16 * (n // RING + (n % RING > 0))

        def ps_proj(c, t):
            return bank[(2 * c + t) % 4][:, 0:PIECE]

        def proj_out(c):
            if c in ROPE_PIECES:
                return out_dve, 2 * ROPE_PIECES.index(c) + 1
            if c in (4, 5):
                return hq_ready(c)
            return out_act, 2 * [2, 3, 6].index(c) + 1

        def hq_ready(c):
            if c in ROPE_PIECES:
                return hq_dve, 2 * ROPE_PIECES.index(c) + 1
            return hq_act, 2 * [3, 4, 5].index(c) + 1

        def turn_x(pe, done, t, banks):
            for g in range(2):
                for j in range(4):
                    mm = pe.transpose(banks[g][:, j * P:(j + 1) * P], x_sb[:, t, (g * 4 + j) * P:(g * 4 + j + 1) * P], ident[:, :])
                mm.then_inc(done, 1)

        def normalised(eng, second, t):
            eng.wait_ge(ln_done_pool, second * TT + t + 1)
            if LN_CUT[t]:
                eng.wait_ge(ln_done, second + 1)

        def copy_xT(act, turned_, ready, first, t, banks):
            for g in range(2):
                act.wait_ge(turned_, first + 2 * t + g + 1)
                act.copy(xT[:, 4 * g:4 * g + 4, t * P:(t + 1) * P], banks[g].rearrange("p (k c) -> p k c", k=4)).then_inc(ready, 1)

        with nc.Block() as block:
            @block.sync
            def _(sp):
                for dst, src in ((x_sb[:, :, :], x.rearrange("b (t p) d -> p (b t) d", p=P)),
                                 (ident[:, :], consts["ident"])):
                    sp.dma_start(dst, src).then_inc(x_ld, 16)
                sp.dma_start(piece[0][:, :, :], pieces[DEPTH - 1, 0].rearrange("p (k c) -> p k c", k=KD)).then_inc(early_piece, 16)
                for dst, src in ((cmask_f[:, :], consts["cmask"]),
                                 (upper[:, :, :], consts["upper"]),
                                 (rope_cs[:, :, :, :], consts["rope"]), (misc_c[:, :], consts["misc"]),
                                 (ones[:, :], consts["ones"])):
                    sp.dma_start(dst, src).then_inc(once, 16)
                sp.wait_ge(early_piece, 16)
                sp.wait_ge(once, 16 * 5)

            @block.tensor
            def _(pe):
                pe.wait_ge(x_ld, 32)
                for t in range(TT):
                    turn_x(pe, early_ps, t, (bank[4 + 2 * t], bank[5 + 2 * t]))

            @block.scalar
            def _(act):
                for t in range(TT):
                    copy_xT(act, early_ps, early_sb, 0, t, (bank[4 + 2 * t], bank[5 + 2 * t]))

            @block.vector
            def _(dve):
                dve.wait_ge(x_ld, 32)
                dve.wait_ge(once, 16 * 5)
                nc.vector.tensor_copy(identb[:, :], ident[:, :])
                for a in range(2):
                    nc.vector.tensor_copy(cmask[:, a, :], cmask_f[:, :])

        with nc.Fori(0, DEPTH) as layer:
            def of(t):
                return t[bass.ds(layer, 1)]

            with nc.Block() as block:
                @block.sync
                def _(sp):
                    def load_piece(n):
                        if n >= RING:
                            what, m = STREAM[n - RING]
                            if what == "in":
                                sp.wait_ge(proj, 2 * m + 2)
                            else:
                                sp.wait_ge(hid, 1)
                        sp.dma_start(piece[n % RING][:, :, :],
                                     of(pieces)[0, n].rearrange("p (k c) -> p k c", k=KD)).then_inc(piece_ld[n % RING], 16)

                    def load_pair(s, which, pair):
                        a, b, ld = ((0, EGU, gu_ld), (EGU, EW, dn_ld))[which]
                        sp.dma_start(ex[s][:, :, a:b],
                                     of(moe_w)[0, bass.ds(pair * 2, 2), :, a:b].rearrange("e p c -> p e c")).then_inc(ld[s], 16)

                    for n in range(1, RING):
                        load_piece(n)
                    sp.dma_start(smalls[:, :], of(small).rearrange("l p c -> p (l c)")).then_inc(small_ld, 16)
                    sp.dma_start(biases[:, :], of(rows)[0].partition_broadcast(P)).then_inc(small_ld, 16)
                    load_piece(RING)
                    for q in range(4):
                        load_pair(q // 2, q % 2, q // 2)
                        load_piece(RING + 1 + 2 * q)
                        load_piece(RING + 2 + 2 * q)
                    for n in range(RING + 9, N_IN_PIECES + 2 + N_OUT_PIECES):
                        load_piece(n)
                    sp.wait_ge(o_sb, 8)
                    sp.dma_start(wsh[:, :], of(ws)[0]).then_inc(ws_ld, 16)
                    sp.dma_start(lnp[:, :, :].rearrange("p a d -> p (a d)"),
                                 of(lnw)[0, 0].partition_broadcast(P)).then_inc(ln_ld, 16)
                    sp.dma_start(wr[:, :, :].rearrange("p k e -> p (k e)"), of(router)[0]).then_inc(wr_ld, 16)
                    normalised(sp, 0, TT - 1)
                    sp.dma_start(lnp[:, :, :].rearrange("p a d -> p (a d)"),
                                 of(lnw)[0, 1].partition_broadcast(P)).then_inc(ln_ld, 16)
                    with sp.Fori(1, PAIRS // 2) as i:
                        for s in range(2):
                            sp.wait_ge(main.gu, 2 * i + (s - 1))
                            load_pair(s, 0, 2 * i + s)
                            sp.wait_ge(main.dn, 2 * i + (s - 1))
                            load_pair(s, 1, 2 * i + s)
                    sp.wait_ge(combined, TT)
                    more = sp.value_load(flag[0:1, 0:1], min_val=0, max_val=1)
                    with sp.If(more > 0):
                        with sp.Fori(0, ROUNDS - 1) as r:
                            with sp.Fori(0, PAIRS) as n:
                                sp.wait_ge(over.sc, r * PAIRS + n + 1)
                                sp.dma_start(ex[0][:, :, :], of(moe_w)[0, bass.ds(n * 2, 2)].rearrange("e p c -> p e c")).then_inc(over_ld, 16)
                        sp.wait_ge(over.sc, (ROUNDS - 1) * PAIRS + 1)
                    with sp.Else():
                        sp.nop()
                    sp.dma_start(piece[0][:, :, :], of(pieces)[0, 0].rearrange("p (k c) -> p k c", k=KD)).then_inc(piece_ahead, 16)
                    sp.wait_ge(piece_ahead, 16)

                @block.tensor
                def _(pe):
                    def project(c):
                        n = STREAM.index(("in", c))
                        if n > 0:
                            pe.wait_ge(piece_ld[n % RING], piece_count(n))
                        for t in range(TT):
                            if c >= 2:
                                reader, count = proj_out(c - 2)
                                pe.wait_ge(reader, count + t)
                            for k in range(KD):
                                mm = pe.matmul(ps_proj(c, t), xT[:, k, t * P:(t + 1) * P], piece[n % RING][:, k, :],
                                               start=(k == 0), stop=(k == KD - 1))
                            mm.then_inc(proj, 1)

                    turns = [(c, t) for c in TURNED for t in range(TT)]

                    def turn_heads(c):
                        for t in range(TT):
                            j = turns.index((c, t))
                            writer, count = hq_ready(c)
                            pe.wait_ge(writer, count + t)
                            if j >= 2:
                                pe.wait_ge(turned_out, j - 1)
                            b, src = bank[4 + j % 2], hq[:, (2 * c + t) % 4, :]
                            for q in range(1 if c == 3 else 2):
                                mm = pe.transpose(b[:, q * P:(q + 1) * P], src[:, q * P:(q + 1) * P], ident[:, :])
                            mm.then_inc(turned, 1)

                    def pair_dots(b0, b1, tq, tk, more=True):
                        for q, (a, w) in enumerate(((0, P), (P, 2 * P))):
                            for h, b in ((0, b0), (1, b1)):
                                r = slice(h * HD, (h + 1) * HD)
                                mm = pe.matmul(b[:, a:a + w], qkT[r, tq, q * P:(q + 1) * P], qkT[r, tk, 0:w],
                                               start=(q == 0), stop=not more, skip_group_check=True)
                        return mm

                    def index_dots(i):
                        if i == 0:
                            pe.wait_ge(turned_out, 4)
                        else:
                            pe.wait_ge(dots_out, 2 * i)
                        pair_dots(bank[6], bank[7], T_IQ + i, T_IK, more=False).then_inc(dots, 1)

                    def fox_rows():
                        pe.wait_ge(lf_ready, 1)
                        pe.wait_ge(dots_out, 4)
                        for h in range(FOX):
                            for t in range(TT):
                                lf = fz[:, 3, t * 4 + h:t * 4 + h + 1].broadcast_to([P, 32])
                                mm = pe.matmul(bank[6][h * 32:(h + 1) * 32, 0:T], lf, upper[:, t, :], start=(t == 0), stop=(t == TT - 1))
                        mm.then_inc(cum, 1)

                    def cmp_hidden():
                        pe.wait_ge(c_ready, 2)
                        for kv in range(2):
                            n = STREAM.index(("cmp", kv))
                            pe.wait_ge(piece_ld[n % RING], piece_count(n))
                        pe.wait_ge(pad_ready, 1)
                        pe.wait_ge(blk_ready, 2)
                        for i in range(CPAIRS):
                            for kv in range(2):
                                n = STREAM.index(("cmp", kv))
                                w1 = piece[n % RING][:, :, :].rearrange("p k c -> p (k c)")
                                mm = pe.matmul(bank[7][kv * CROWS:(kv + 1) * CROWS, 0:P], blkT[:, kv, i, :], w1[:, i * P:(i + 1) * P],
                                               start=(i == 0), stop=(i == CPAIRS - 1))
                        mm.then_inc(hid, 1)

                    def cmp_turn():
                        pe.wait_ge(gelu_ready, 1)
                        pe.transpose(bank[6][:, 256:256 + 2 * CROWS], hgelu[:, 2, :], ident[0:2 * CROWS, 0:2 * CROWS]).then_inc(hg_ps, 1)

                    def cmp_kv():
                        pe.wait_ge(hg_sb, 1)
                        pe.wait_ge(small_ld, 32)
                        for g in range(GRP):
                            pe.matmul(bank[6][g * HD:(g + 1) * HD, 0:NC], smalls[:, 0:HD], hgT[:, g * NC:(g + 1) * NC], start=True, stop=True)
                        for g in range(GRP):
                            mm = pe.matmul(bank[6][0:NC, 64 + g * HD:64 + (g + 1) * HD], hgT[:, CROWS + g * NC:CROWS + (g + 1) * NC], smalls[:, HD:2 * HD], start=True, stop=True)
                        mm.then_inc(kv_ps, 1)

                    def cmp_scores():
                        pe.wait_ge(kv_sb, 2)
                        pe.wait_ge(turned_out, 2 * TURNED.index(8) + 2)
                        for t in range(TT):
                            for r in range(REP):
                                for g in range(GRP):
                                    rows_ = slice(g * HD, (g + 1) * HD)
                                    c0 = (t * REP + r) * 16
                                    mm = pe.matmul(bank[6 + g][:, c0:c0 + NC], qkT[rows_, T_NQ + r, t * P:(t + 1) * P], kcT[rows_, 0:NC], start=True, stop=True)
                        mm.then_inc(sc_ps, 1)

                    def scores(u):
                        kind, o, i = UNITS[u]
                        b0, b1 = bank[2 * (u % 2)], bank[2 * (u % 2) + 1]
                        if u >= 2:
                            pe.wait_ge(e_ready, u - 1)
                        if u == 0:
                            pe.wait_ge(out_dve, 2 * len(ROPE_PIECES))
                        if u == 2:
                            pe.wait_ge(turned_out, 2 * len(TURNED))
                        if kind == "dsa":
                            pe.wait_ge(dmask_ready, 1)

                        tq, tk = {"fox": (T_FQ + i, T_FK + i), "slc": (T_NQ + i, T_KS), "win": (T_NQ + i, T_KW), "dsa": (T_DQ + i, T_DK)}[kind]
                        pair_dots(b0, b1, tq, tk)
                        if kind == "fox":
                            for q, (a, w) in enumerate(((0, P), (P, 2 * P))):
                                for h, b in ((0, b0), (1, b1)):
                                    rows_ = slice((2 * i + h) * 32, (2 * i + h) * 32 + 2)
                                    pe.matmul(b[:, a:a + w], c_rows[rows_, 0, q * P:(q + 1) * P], c_rows[rows_, 1, 0:w], start=False, stop=False, skip_group_check=True)
                        for h, b in ((0, b0), (1, b1)):
                            if kind == "dsa":
                                mm = pe.matmul(b[:, 0:3 * P], identb[:, :], dmask[:, :], start=False, stop=True, skip_group_check=True)
                            else:
                                diag = b[:, 0:4 * P].rearrange("p (a c) -> p a c", a=2)[:, :, 0:P]
                                mm = pe.matmul(diag, identb[:, :], cmask[:, :, :], start=False, stop=True, skip_group_check=True)
                        mm.then_inc(s_ready, 1)

                    def values(kind, h, i):
                        c = {"fox": V_F + (2 * i + h) * HD, "slc": V_S + h * HD, "win": V_W + h * HD, "dsa": V_D}[kind]
                        return slice(c, c + HD)

                    def turn_probs(v):
                        what, u = TURNS[v]
                        if v >= 1:
                            pe.wait_ge(pt_sb, v)
                        else:
                            pe.wait_ge(turned_out, 2 * len(TURNED))
                        if what == "unit":
                            pe.wait_ge(p_ready, u + 1)
                            for h in range(2):
                                for j in range(3):
                                    mm = pe.transpose(bank[4 + h][:, j * P:(j + 1) * P], prob[:, u % 2, h, j * P:(j + 1) * P], ident[:, :])
                        else:
                            pe.wait_ge(pc_ready, 1)
                            for g in range(GRP):
                                for t in range(TT):
                                    mm = pe.transpose(bank[4][0:NC, (g * TT + t) * P:(g * TT + t + 1) * P], pc[:, t, u * GRP + g, 0:NC], ident[:, :])
                        mm.then_inc(pt_ps, 1)

                    def add_values(v):
                        what, u = TURNS[v]
                        pe.wait_ge(pt_sb, v + 1)
                        if what == "unit":
                            kind, o, i = UNITS[u]
                            first, last = kind != "win", kind not in ("slc", "win")
                            if first and o >= 2:
                                pe.wait_ge(o_sb, o - 1)
                            if o == 0:
                                pe.wait_ge(sc_sub, 1)
                            ob = bank[6 + o % 2]
                            for h in range(2):
                                pe.matmul(ob[h * HD:(h + 1) * HD, 0:T], vbuf[:, 0, values(kind, h, i)], probT[v % 2][:, h, 0:T], start=first, stop=False, skip_group_check=True)
                            for h in range(2):
                                mm = pe.matmul(ob[h * HD:(h + 1) * HD, P:T], vbuf[:, 1, values(kind, h, i)], probT[v % 2][:, h, T:T + P], start=False, stop=last, skip_group_check=True)
                        else:
                            o = 2 + u
                            for g in range(GRP):
                                mm = pe.matmul(bank[6 + o % 2][g * HD:(g + 1) * HD, 0:T], vc_sb[0:NC, g, :],
                                               probT[v % 2][0:NC, :, :].rearrange("p h c -> p (h c)")[:, g * T:(g + 1) * T], start=False, stop=True, skip_group_check=True)
                        mm.then_inc(pv, 1)

                    project(0)
                    project(1)
                    turn_heads(0)
                    project(2)
                    turn_heads(1)
                    project(3)
                    index_dots(0)
                    project(4)
                    index_dots(1)
                    turn_heads(3)
                    project(5)
                    fox_rows()
                    turn_heads(4)
                    project(6)
                    turn_heads(5)
                    cmp_hidden()
                    project(7)
                    cmp_turn()
                    project(8)
                    cmp_kv()
                    turn_heads(7)
                    project(9)
                    turn_heads(8)
                    cmp_scores()
                    project(10)
                    turn_heads(9)
                    scores(0)
                    turn_heads(10)
                    scores(1)
                    for v, (what, u) in enumerate(TURNS):
                        if what == "unit" and u + 2 < NU:
                            scores(u + 2)
                        turn_probs(v)
                        if v >= 1:
                            add_values(v - 1)
                    add_values(len(TURNS) - 1)

                    pe.wait_ge(e_ready, NU)
                    pe.wait_ge(o_sb, 8)
                    for t in range(TT):
                        for n in range(N_OUT_PIECES):
                            m = STREAM.index(("out", n))
                            if t == 0:
                                pe.wait_ge(piece_ld[m % RING], piece_count(m))
                            for k in range(KD):
                                mm = pe.matmul(bank[2 * t + n // 2][:, (n % 2) * PIECE:(n % 2 + 1) * PIECE],
                                               xT[:, k, t * P:(t + 1) * P], piece[m % RING][:, k, :], start=(k == 0), stop=(k == KD - 1))
                        mm.then_inc(mix, 1)

                    def route(t):
                        normalised(pe, 0, t)
                        turn_x(pe, xt_ps, t, (bank[4 - 2 * t], bank[5 - 2 * t]))
                        pe.wait_ge(xt_sb, 2 * t + 2)
                        for k in range(KD):
                            mm = pe.matmul(bank[5][:, t * NE:(t + 1) * NE], xT[:, k, t * P:(t + 1) * P], wr[:, k, :], start=(k == 0), stop=(k == KD - 1))
                        mm.then_inc(logits, 1)

                    def shared_gate_up(f, t):
                        for k in range(KD):
                            mm = pe.matmul(bank[6 + f // 2][:, (f % 2) * T + t * P:(f % 2) * T + (t + 1) * P], wsh[:, k * 2 * EF + f * P:k * 2 * EF + (f + 1) * P],
                                           xT[:, k, t * P:(t + 1) * P], start=(k == 0), stop=(k == KD - 1))
                        return mm

                    pe.wait_ge(wr_ld, 16)
                    pe.wait_ge(ws_ld, 16)
                    route(0)
                    for f in range(2):
                        shared_gate_up(f, 0)
                    route(1)
                    for f in range(2):
                        shared_gate_up(f, 1)
                    shared_gate_up(2, 0)
                    shared_gate_up(3, 0)
                    shared_gate_up(2, 1)
                    pe.wait_ge(sel_ready, 1)
                    sel0, sel1 = rt[:, 2, 0, :], rt[:, 2, 1, :]
                    pe.matmul(bank[4][:, 0:NE], upper[:, 0, 0:P], sel0, start=True, stop=True)
                    pe.matmul(bank[4][:, NE:2 * NE], upper[:, 0, P:T], sel0, start=True, stop=False)
                    pe.matmul(bank[4][:, NE:2 * NE], upper[:, 1, P:T], sel1, start=False, stop=True)
                    pe.matmul(bank[4][0:1, 2 * NE:3 * NE], ones[:, 0:1], sel0, start=True, stop=False)
                    pe.matmul(bank[4][0:1, 2 * NE:3 * NE], ones[:, 0:1], sel1, start=False, stop=True).then_inc(ranks, 1)
                    shared_gate_up(3, 1).then_inc(sh_ps, 1)
                    A, B, C, R = bank[4], bank[5], bank[6], bank[7]
                    R_hot = R[:, 0:P].bitcast(BF16)

                    def shared_down(t, c):
                        for f in range(2):
                            pe.matmul(bank[2 * t + c][:, :], shT[:, f, t * P:(t + 1) * P], wsh[:, EGU + f * D + c * 512:EGU + f * D + (c + 1) * 512],
                                      start=(f == 0), stop=False, skip_group_check=True)

                    def gather(sw, par, n, k):
                        pe.wait_ge(sw.hot, k)
                        H = hot[par]
                        for t in range(TT):
                            pe.transpose(R_hot[:, t * P:(t + 1) * P], H[:, t, :], identb[:, :])
                        for t in range(TT):
                            pe.matmul(R[:, P:P + 6], H[:, t, :], gw2[:, t, bass.ds(n * 2, 2), :].rearrange("p e h -> p (e h)"), start=(t == 0), stop=(t == TT - 1))
                        for d in range(KD):
                            o = (A, B)[d // 4][:, (d % 4) * P:(d % 4 + 1) * P]
                            for j in range(3 * TT):
                                mm = pe.matmul(o, xs[j // TT][:, j % TT, d * P:(d + 1) * P], H[:, j % TT, :], start=(j == 0), stop=(j == 3 * TT - 1))
                        mm.then_inc(sw.gat, 1)

                    def gate_up(sw, par, W, k):
                        pe.wait_ge(sw.xg, 2 * k)
                        for d in range(KD):
                            for e in range(2):
                                mm = pe.matmul(C[e * SLOTS:(e + 1) * SLOTS, :], xgT[par][:, d, e * SLOTS:(e + 1) * SLOTS],
                                               W[:, e, d * 2 * EF:(d + 1) * 2 * EF], start=(d == 0), stop=(d == KD - 1))
                        mm.then_inc(sw.gu, 1)

                    def turn_h(sw, k):
                        pe.wait_ge(sw.h, k)
                        for f in range(EF // P):
                            mm = pe.transpose(R[:, T + f * P:T + (f + 1) * P], h_sb[:, f * P:(f + 1) * P], ident[:, :])
                        mm.then_inc(sw.ht_ps, 1)

                    def down(sw, W, k):
                        pe.wait_ge(sw.ht, k)
                        for c in range(2):
                            for f in range(2):
                                for e in range(2):
                                    mm = pe.matmul((A, B)[c][e * SLOTS:(e + 1) * SLOTS, :], hT[:, f, e * SLOTS:(e + 1) * SLOTS],
                                                   W[:, e, EGU + f * D + c * 512:EGU + f * D + (c + 1) * 512], start=(f == 0), stop=(f == 1))
                        mm.then_inc(sw.dn, 1)

                    def add_back(sw, par, k, last=False):
                        pe.wait_ge(sw.yl, k)
                        pe.wait_ge(sw.hotT, k)
                        for t in range(TT):
                            for c in range(2):
                                for y in (y_hi, y_lo):
                                    mm = pe.matmul(bank[2 * t + c][:, :], hotT[par][:, t * P:(t + 1) * P], y[:, c * 512:(c + 1) * 512],
                                                   start=False, stop=False, skip_group_check=True)
                            if last:
                                mm.then_inc(combined, 1)
                        if not last:
                            mm.then_inc(sw.sc, 1)

                    def step(s, n, i, first=False, last=False):
                        pe.wait_ge(gu_ld[s], 16 * i + 16)
                        if first:
                            shared_down(0, 0)
                        gate_up(main, s, ex[s], n + 1)
                        if first:
                            shared_down(0, 1)
                            shared_down(1, 0)
                            shared_down(1, 1)
                        if not last:
                            if not first:
                                pe.wait_ge(main.yl, n)
                            pe.wait_ge(main.hotT, n + 1)
                            gather(main, 1 - s, n + 1, n + 2)
                        if last:
                            add_back(main, 1 - s, n)
                        turn_h(main, n + 1)
                        if not first and not last:
                            add_back(main, 1 - s, n)
                        pe.wait_ge(dn_ld[s], 16 * i + 16)
                        if not last:
                            pe.wait_ge(main.xg, 2 * (n + 2))
                        down(main, ex[s], n + 1)

                    pe.wait_ge(split_b, TT)
                    pe.wait_ge(split_c, TT)
                    pe.wait_ge(sh_h, 1)
                    pe.wait_ge(routed_ready, 1)
                    gather(main, 0, 0, 1)
                    step(0, 0, 0, first=True)
                    with pe.Fori(0, PAIRS // 2 - 1) as i:
                        step(1, 2 * i + 1, i)
                        step(0, 2 * i + 2, i + 1)
                    step(1, PAIRS - 1, PAIRS // 2 - 1, last=True)
                    add_back(main, 1, PAIRS, last=True)

                    more = pe.value_load(flag[0:1, 0:1], min_val=0, max_val=1)
                    with pe.If(more > 0):
                        pe.nop().then_inc(over.sc, 1)
                        with pe.Fori(0, ROUNDS - 1) as r:
                            with pe.Fori(0, PAIRS) as n:
                                k = r * PAIRS + n + 1
                                gather(over, 0, n, k)
                                pe.wait_ge(over_ld, 16 * k)
                                gate_up(over, 0, ex[0], k)
                                turn_h(over, k)
                                down(over, ex[0], k)
                                add_back(over, 0, k)
                    with pe.Else():
                        pe.nop()
                    for t in range(TT):
                        normalised(pe, 1, t)
                        turn_x(pe, xt_ps, t, (bank[4 + 2 * t], bank[5 + 2 * t]))

                @block.scalar
                def _(act):
                    own = Order(act, act_own)

                    def read_plain(c):
                        for t in range(TT):
                            act.wait_ge(proj, 2 * c + t + 1)
                            ps, slot = ps_proj(c, t), (2 * c + t) % 4
                            if c == 2:
                                act.copy(vbuf[:, t, 0:V_S], ps[:, 0:V_S]).then_inc(out_act, 1)
                            elif c == 6:
                                act.copy(vbuf[:, t, V_F:V_F + PIECE], ps).then_inc(out_act, 1)
                            elif c == 3:
                                act.wait_ge(turned, 2 + t + 1)
                                act.copy(hq[:, slot, 0:P], ps[:, 0:P]).then_inc(hq_act, 1)
                                act.copy(vbuf[:, t, V_S:V_S + P], ps[:, P:2 * P]).then_inc(out_act, 1)
                            else:
                                if c == 5:
                                    act.wait_ge(turned, 4 + t + 1)
                                act.copy(hq[:, slot, :], ps).then_inc(hq_act, 1)

                    def read_turned(c):
                        for t in range(TT):
                            j = 2 * TURNED.index(c) + t
                            act.wait_ge(turned, j + 1)
                            b = bank[4 + j % 2]
                            cols = slice(t * P, (t + 1) * P)
                            halves = (slice(0, HD), slice(HD, P))
                            if c == 1:
                                for src, n in ((0, T_IK), (1, T_DK)):
                                    for dst in range(2):
                                        own.mark(act.copy(qkT[halves[dst], n, cols], b[halves[src], 0:P]))
                            elif c in TILE_OF:
                                n = TILE_OF[c]
                                src = b[:, 0:2 * P].rearrange("p (a c) -> p a c", a=2)
                                own.mark(act.copy(qkT[:, n:n + 2, cols], src))
                            if c in (1, 3):
                                kv, o = (0, P) if c == 1 else (1, 0)
                                lo = 1 if t == 0 else 0
                                for g in range(GRP):
                                    own.mark(act.copy(cmpT[0:HD, kv, g, cols], b[halves[g], o:o + P]))
                                    own.mark(act.copy(cmpT[HD:P, kv, g, t * P + lo - 1:(t + 1) * P - 1], b[halves[g], o + lo:o + P]))
                            own.settle()
                            act.nop().then_inc(turned_out, 1)

                    def relu_dots(i):
                        act.wait_ge(dots, i + 1)
                        if i == 1:
                            act.wait_ge(dots_free, 2)
                        for h in range(2):
                            act.activation(rtmp[:, h, :], bank[6 + h][:, 0:3 * P], ACT.Relu).then_inc(dots_out, 1)

                    def misc():
                        own.settle()
                        act.wait_ge(out_act, 2)
                        for t in range(TT):
                            act.activation(gates[:, t, :], vbuf[:, t, M_G:M_G + 18], ACT.Exp, scale=-1.0).then_inc(gate_exp, 1)
                        act.wait_ge(fabs, 1)
                        own.link(act.activation(fz[:, 2, :], fz[:, 1, :], ACT.Exp, scale=-1.0))
                        act.activation(fz[:, 3, :], fz[:, 2, :], ACT.Ln, bias=1.0).then_inc(fln, 1)

                    def fox_rows_out():
                        act.wait_ge(cum, 1)
                        act.wait_ge(dots_free, 4)
                        for j in range(2):
                            act.activation(c_rows[:, j, :], bank[6][:, 0:T], ACT.Identity, scale=row_mix[:, 2 * j:2 * j + 1],
                                           bias=row_mix[:, 2 * j + 1:2 * j + 2]).then_inc(c_ready, 1)

                    read_turned(0)
                    read_plain(2)
                    read_turned(1)
                    misc()
                    read_plain(3)
                    relu_dots(0)
                    read_plain(4)
                    relu_dots(1)
                    read_turned(3)
                    read_plain(5)
                    fox_rows_out()
                    read_turned(4)
                    read_plain(6)
                    read_turned(5)
                    act.wait_ge(gelu_u, 1)
                    act.activation(hgelu[:, 1, :], hgelu[:, 1, :], ACT.Exp, scale=1.0).then_inc(gelu_e, 1)
                    act.wait_ge(hg_ps, 1)
                    act.copy(hgT[:, :], bank[6][:, 256:256 + 2 * CROWS]).then_inc(hg_sb, 1)
                    act.wait_ge(kv_ps, 1)
                    act.copy(kcT[:, 0:NC], bank[6][:, 0:NC]).then_inc(kv_sb, 1)
                    act.copy(vc_sb[0:NC, :, :], bank[6][0:NC, 64:64 + P].rearrange("p (g c) -> p g c", g=GRP)).then_inc(kv_sb, 1)
                    read_turned(7)
                    read_turned(8)
                    act.wait_ge(sc_sub, 1)
                    act.activation(pc[:, :, :, 0:NC], pc[:, :, :, 0:NC], ACT.Exp, scale=SCALE).then_inc(sc_exp, 1)
                    read_turned(9)

                    def exps(u):
                        act.wait_ge(m_ready, u + 1)
                        if u >= 2:
                            act.wait_ge(pt_ps, TURN_OF_UNIT[u - 2] + 1)
                        for h in range(2):
                            for q, (a, w) in enumerate(((0, P), (P, 2 * P))):
                                c = 2 * h + q
                                own.mark(act.activation(prob[:, u % 2, h, a:a + w], bank[2 * (u % 2) + h][:, a:a + w], ACT.Exp,
                                                        bias=sm_neg[:, u % 2, c:c + 1], scale=SCALE, accum_out=sm_sum[:, u % 2, c:c + 1]))
                        own.settle()
                        act.nop().then_inc(e_ready, 1)

                    def heads_out(v):
                        what, u = TURNS[v]
                        kind, o, _ = UNITS[u] if what == "unit" else ("cmp", 2 + u, 0)
                        if kind in ("fox", "dsa", "cmp"):
                            act.wait_ge(pv, v + 1)
                            act.copy(xT[:, o, :], bank[6 + o % 2][:, 0:T]).then_inc(o_sb, 1)

                    exps(0)
                    read_turned(10)
                    for v, (what, u) in enumerate(TURNS):
                        if what == "unit" and u + 1 < NU:
                            exps(u + 1)
                        act.wait_ge(pt_ps, v + 1)
                        if v >= 2:
                            act.wait_ge(pv, v - 1)
                        if what == "unit":
                            for h in range(2):
                                own.mark(act.copy(probT[v % 2][:, h, :], bank[4 + h][:, 0:3 * P]))
                        else:
                            own.mark(act.copy(probT[v % 2][0:NC, :, :].rearrange("p h c -> p (h c)")[:, 0:2 * T], bank[4][0:NC, :]))
                        own.settle()
                        act.nop().then_inc(pt_sb, 1)
                        if v >= 1:
                            heads_out(v - 1)
                    heads_out(len(TURNS) - 1)

                    def deviation(first, t):
                        act.wait_ge(ln_var, first + t + 1)
                        act.activation(ln_s[:, t, 16:17], ln_s[:, t, 15:16], ACT.Sqrt).then_inc(ln_rs, 1)

                    def split_x(t):
                        act.copy(xs[0][:, t, :], x_sb[:, t, :]).then_inc(split_a, 1)

                    def router_out(t):
                        act.wait_ge(logits, t + 1)
                        act.activation(rt[:, 0, t, :], bank[5][:, t * NE:(t + 1) * NE], ACT.Sigmoid).then_inc(lg_exp, 1)

                    deviation(0, 0)
                    copy_xT(act, xt_ps, xt_sb, 0, 0, (bank[4], bank[5]))
                    deviation(0, 1)
                    act.wait_ge(mix, TT)
                    split_x(0)
                    router_out(0)
                    copy_xT(act, xt_ps, xt_sb, 0, 1, (bank[2], bank[3]))
                    router_out(1)
                    split_x(1)
                    for t in range(TT):
                        act.wait_ge(split_rest, t + 1)
                        act.copy(xs[1][:, t, :], rest[:, t, :]).then_inc(split_b, 1)
                    act.wait_ge(sh_ps, 1)
                    act.activation(shS[:, :, :].rearrange("p f c -> p (f c)"), bank[6], ACT.Sigmoid).then_inc(sh_exp, 1)

                    A, B, C = bank[4], bank[5], bank[6]

                    def sigmoid(sw, k):
                        act.wait_ge(sw.gu, k)
                        act.activation(sig[:, :], C[:, 0:EF], ACT.Sigmoid).then_inc(sw.ex, 1)

                    def read_gathered(sw, par, k):
                        act.wait_ge(sw.gat, k)
                        act.copy(xgT[par][:, 0:4, :], A[:, :].rearrange("p (k c) -> p k c", k=4)).then_inc(sw.xg, 1)

                    def y_high(sw, par, k):
                        act.wait_ge(sw.dn, k)
                        act.wait_ge(sw.hotT, k)
                        for c in range(2):
                            act.activation(y_hi[:, c * 512:(c + 1) * 512], (A, B)[c][:, :], ACT.Copy, scale=gslot[:, par:par + 1]).then_inc(sw.yh, 1)

                    def step(s, n, last=False):
                        sigmoid(main, n + 1)
                        if not last:
                            read_gathered(main, 1 - s, n + 2)
                        y_high(main, s, n + 1)

                    act.wait_ge(sh_h, 1)
                    read_gathered(main, 0, 1)
                    step(0, 0)
                    with act.Fori(0, PAIRS // 2 - 1) as i:
                        step(1, 2 * i + 1)
                        step(0, 2 * i + 2)
                    step(1, PAIRS - 1, last=True)
                    more = act.value_load(flag[0:1, 0:1], min_val=0, max_val=1)
                    with act.If(more > 0):
                        with act.Fori(0, ROUNDS - 1) as r:
                            with act.Fori(0, PAIRS) as n:
                                k = r * PAIRS + n + 1
                                read_gathered(over, 0, k)
                                sigmoid(over, k)
                                y_high(over, 0, k)
                    with act.Else():
                        act.nop()
                    for t in range(TT):
                        deviation(TT, t)
                    for t in range(TT):
                        copy_xT(act, xt_ps, xt_sb, 4, t, (bank[4 + 2 * t], bank[5 + 2 * t]))

                @block.gpsimd
                def _(pool):
                    own = Order(pool, pool_own)
                    G = nc.gpsimd
                    G.memset(blkT[:, :, :, GRP * NC:CROWS].rearrange("p a i c -> p (a i) c"), 0.0).then_inc(pad_ready, 1)

                    def scale_half(first):
                        for t in range(TT):
                            pool.wait_ge(ln_half, first + t + 1)
                            pool.wait_ge(ln_ld, 16 * (2 if first else 1))
                            cols = slice(LN_CUT[t], D)
                            xx = x_sb[:, t, cols]
                            own.link(G.tensor_tensor(xx, xx, lnp[:, 0, cols], ALU.mult))
                            G.tensor_tensor(xx, xx, lnp[:, 1, cols], ALU.add).then_inc(ln_done_pool, 1)

                    scale_half(0)
                    for t in range(TT):
                        pool.wait_ge(split_a, t + 1)
                        G.tensor_tensor(rest[:, t, :], x_sb[:, t, :], xs[0][:, t, :], ALU.subtract).then_inc(split_rest, 1)
                    for t in range(TT):
                        pool.wait_ge(split_b, t + 1)
                        G.tensor_tensor(xs[2][:, t, :], rest[:, t, :], xs[1][:, t, :], ALU.subtract).then_inc(split_c, 1)
                    scale_half(TT)

                @block.vector
                def _(dve):
                    own = Order(dve, dve_own)
                    V = nc.vector

                    def rotate(c):
                        for t in range(TT):
                            j = 2 * TURNED.index(c) + t
                            slot = (2 * c + t) % 4
                            dve.wait_ge(proj, 2 * c + t + 1)
                            if c >= 7:
                                prev = {7: 5, 8: 4, 9: 7, 10: 8}[c]
                                dve.wait_ge(turned, 2 * TURNED.index(prev) + t + 1)
                            ps = ps_proj(c, t)
                            ph = ps.rearrange("p (h a c) -> p h a c", h=4, a=2)
                            cs = rope_cs[:, 0, t:t + 1, :].broadcast_to([P, 4, HD])
                            tm = rope_tmp[:, :].rearrange("p (h a c) -> p h a c", h=4, a=2)
                            own.mark(V.tensor_tensor(hq[:, slot, :].rearrange("p (h c) -> p h c", h=4), ps.rearrange("p (h c) -> p h c", h=4), cs, ALU.mult))
                            for a in range(2):
                                sn = rope_cs[:, 1, t:t + 1, a * 32:(a + 1) * 32].broadcast_to([P, 4, 32])
                                own.mark(V.tensor_tensor(tm[:, :, a, :], ph[:, :, 1 - a, :], sn, ALU.mult))
                            own.settle()
                            dve.nop().then_inc(out_dve, 1)
                            own.link(V.tensor_tensor(hq[:, slot, :], hq[:, slot, :], rope_tmp[:, :], ALU.add))
                            dve.nop().then_inc(hq_dve, 1)

                    def misc():
                        dve.wait_ge(out_act, 2)
                        dve.wait_ge(small_ld, 32)
                        for t in range(TT):
                            own.mark(V.tensor_tensor(fz[:, 0, t * 4:t * 4 + 4], vbuf[:, t, M_F:M_F + 4], biases[:, 0:FOX], ALU.add))
                            own.mark(V.tensor_scalar(w_idx[:, t, :], vbuf[:, t, M_W:M_W + 4], IDX ** -0.5, HD ** -0.5, ALU.mult, ALU.mult))
                        own.settle()
                        own.link(V.tensor_scalar(fz[:, 1, :], fz[:, 0, :], -1.0, None, ALU.mult))
                        V.tensor_tensor(fz[:, 1, :], fz[:, 1, :], fz[:, 0, :], ALU.max).then_inc(fabs, 1)
                        dve.wait_ge(gate_exp, 2)
                        own.link(V.tensor_scalar(gates[:, :, :], gates[:, :, :], 1.0, None, ALU.add))
                        own.link(V.reciprocal(gates[:, :, :], gates[:, :, :]))
                        own.link(V.tensor_scalar(fz[:, 0, :], fz[:, 0, :], 0.0, None, ALU.min))
                        dve.wait_ge(fln, 1)
                        V.tensor_tensor(fz[:, 3, :], fz[:, 0, :], fz[:, 3, :], ALU.subtract).then_inc(lf_ready, 1)

                    def index_sum(i):
                        for h in range(2):
                            n = 2 * i + h
                            dve.wait_ge(dots_out, n + 1)
                            for t, (a, w) in enumerate(((0, P), (P, 2 * P))):
                                wt = w_idx[:, t, n:n + 1]
                                if n == 0:
                                    own.mark(V.tensor_scalar(score[:, a:a + w], rtmp[:, h, a:a + w], wt, None, ALU.mult))
                                else:
                                    own.mark(V.scalar_tensor_tensor(score[:, a:a + w], rtmp[:, h, a:a + w], wt, score[:, a:a + w], ALU.mult, ALU.add))
                            own.settle()
                            dve.nop().then_inc(dots_free, 1)

                    def index_top():
                        for a in (0, 2 * P):
                            own.mark(V.tensor_tensor(score[:, a:a + P], score[:, a:a + P], cmask[:, 0, :], ALU.add))
                        own.settle()
                        for a, w in ((0, P), (P, 2 * P)):
                            s = score[:, a:a + w]
                            for _ in range(TOPK // 8):
                                own.link(V.max(top8[:, :], s))
                                own.link(V.match_replace(s, top8[:, :], s, TAKEN))
                        own.link(V.tensor_scalar(score[:, :], score[:, :], -2.0e38, NEG, ALU.is_gt, ALU.mult))
                        for a in (0, 2 * P):
                            own.mark(V.tensor_tensor(score[:, a:a + P], score[:, a:a + P], cmask[:, 0, :], ALU.add))
                        own.settle()
                        V.tensor_copy(dmask[:, :], score[:, :]).then_inc(dmask_ready, 1)

                    def blocks(kv):
                        dve.wait_ge(turned_out, 4 if kv == 0 else 6)
                        dve.wait_ge(small_ld, 32)
                        pe_row = smalls[:, 2 * HD + kv * CPAIRS:2 * HD + (kv + 1) * CPAIRS]
                        for i in range(CPAIRS):
                            blk = blkT[:, kv, i, 0:GRP * NC].rearrange("p (g c) -> p g c", g=GRP)
                            src = cmpT[:, kv, :, 2 * i:2 * i + CMP_STRIDE * (NC - 1) + 1:CMP_STRIDE]
                            own.mark(V.tensor_scalar(blk, src, pe_row[:, i:i + 1], None, ALU.add))
                        own.settle()
                        dve.nop().then_inc(blk_ready, 1)

                    rotate(0)
                    rotate(1)
                    misc()
                    index_sum(0)
                    index_sum(1)
                    blocks(0)
                    blocks(1)
                    index_top()

                    def maxima(u):
                        dve.wait_ge(s_ready, u + 1)
                        m = sm_max[:, u % 2, :].rearrange("p (h q) -> p q h", h=2)
                        b = psum[:, 2 * (u % 2):2 * (u % 2) + 2, :]
                        for q, (a, w) in enumerate(((0, P), (P, 2 * P))):
                            own.mark(V.tensor_reduce(m[:, q], b[:, :, a:a + w], AX, ALU.max))
                        own.settle()
                        V.tensor_scalar(sm_neg[:, u % 2, :], sm_max[:, u % 2, :], -SCALE, None, ALU.mult).then_inc(m_ready, 1)

                    gv = gates[:, :, :].rearrange("p t (b g r) -> p b r g t", b=3, g=GRP)

                    def normalise(u):
                        kind, o, i = UNITS[u]
                        dve.wait_ge(e_ready, u + 1)
                        r = sm_r[:, u % 2, :]
                        own.link(V.reciprocal(r, sm_sum[:, u % 2, :]))
                        if kind in ("slc", "win"):
                            rv = r.rearrange("p (h q) -> p h q", h=2)
                            own.link(V.tensor_tensor(rv, rv, gv[:, 1 if kind == "slc" else 2, i], ALU.mult))
                        for h in range(2):
                            for q, (a, w) in enumerate(((0, P), (P, 2 * P))):
                                pr = prob[:, u % 2, h, a:a + w]
                                own.mark(V.tensor_scalar(pr, pr, r[:, 2 * h + q:2 * h + q + 1], None, ALU.mult))
                        own.settle()
                        dve.nop().then_inc(p_ready, 1)

                    dve.wait_ge(hid, 1)
                    hx, hu, ho = (hgelu[:, j, :] for j in range(3))
                    own.link(V.tensor_copy(hx, bank[7][0:2 * CROWS, 0:P]))
                    own.link(V.tensor_tensor(hu, hx, hx, ALU.mult))
                    c1 = float(np.sqrt(2 / np.pi))
                    own.link(V.tensor_scalar(hu, hu, -2 * c1 * 0.044715, -2 * c1, ALU.mult, ALU.add))
                    own.link(V.tensor_tensor(hu, hu, hx, ALU.mult))
                    V.tensor_scalar(hu, hu, 80.0, None, ALU.min).then_inc(gelu_u, 1)
                    dve.wait_ge(gelu_e, 1)
                    own.link(V.tensor_scalar(hu, hu, 1.0, None, ALU.add))
                    own.link(V.reciprocal(hu, hu))
                    V.tensor_tensor(ho, hx, hu, ALU.mult).then_inc(gelu_ready, 1)
                    rotate(7)
                    rotate(8)
                    rotate(9)
                    dve.wait_ge(sc_ps, 1)
                    heads = REP * GRP
                    for t in range(TT):
                        for g in range(GRP):
                            ps = bank[6 + g][:, t * REP * 16:(t + 1) * REP * 16].rearrange("p (h c) -> p h c", h=REP)[:, :, 0:NC]
                            own.mark(V.tensor_tensor(pc[:, t, g:heads:GRP, 0:NC], ps, cvis[:, t:t + 1, 0:NC].broadcast_to([P, REP, NC]), ALU.add))
                    own.settle()
                    own.link(V.tensor_reduce(pcs[:, 0, :].rearrange("p (t h) -> p t h", t=TT), pc[:, :, :, 0:NC], AX, ALU.max))
                    for t in range(TT):
                        mx = pcs[:, 0, t * heads:(t + 1) * heads].unsqueeze(2).broadcast_to([P, heads, NC])
                        own.mark(V.tensor_tensor(pc[:, t, :, 0:NC], pc[:, t, :, 0:NC], mx, ALU.subtract))
                    own.settle()
                    dve.nop().then_inc(sc_sub, 1)
                    rotate(10)

                    def cmp_norm():
                        dve.wait_ge(sc_exp, 1)
                        own.link(V.tensor_reduce(pcs[:, 1, :].rearrange("p (t h) -> p t h", t=TT), pc[:, :, :, 0:NC], AX, ALU.add))
                        own.link(V.reciprocal(pcs[:, 2, :], pcs[:, 1, :]))
                        for t in range(TT):
                            w = pcs[:, 2, t * heads:(t + 1) * heads]
                            wv = w.rearrange("p (r g) -> p r g", r=REP)
                            own.link(V.scalar_tensor_tensor(wv, wv, anyvis[:, t:t + 1], gv[:, 0, :, :, t], ALU.mult, ALU.mult))
                            own.mark(V.tensor_tensor(pc[:, t, :, 0:NC], pc[:, t, :, 0:NC], w.unsqueeze(2).broadcast_to([P, heads, NC]), ALU.mult))
                        own.settle()
                        dve.nop().then_inc(pc_ready, 1)

                    cmp_norm()
                    maxima(0)
                    maxima(1)
                    for u in range(NU):
                        normalise(u)
                        if u + 2 < NU:
                            maxima(u + 2)

                    def norm(first, ready, counts):
                        for t in range(TT):
                            if ready is not None:
                                dve.wait_ge(ready, counts[t])
                            for c in range(2):
                                xx = x_sb[:, t, c * 512:(c + 1) * 512]
                                own.link(V.scalar_tensor_tensor(xx, xx, ALPHA, bank[2 * t + c], ALU.mult, ALU.add))
                                own.mark(V.bn_stats(ln_s[:, t, c * 6:c * 6 + 6], xx))
                            own.settle()
                            own.link(V.bn_aggr(ln_s[:, t, 12:14], ln_s[:, t, 0:12]))
                            V.tensor_scalar(ln_s[:, t, 15:16], ln_s[:, t, 13:14], LN_EPS, None, ALU.add).then_inc(ln_var, 1)
                            dve.wait_ge(ln_rs, first + t + 1)
                            own.link(V.reciprocal(ln_s[:, t, 17:18], ln_s[:, t, 16:17]))
                            y0, h, r = ln_s[:, t, 17:18], ln_s[:, t, 18:19], ln_s[:, t, 19:20]
                            own.link(V.tensor_tensor(h, y0, y0, ALU.mult))
                            own.link(V.tensor_tensor(h, h, ln_s[:, t, 15:16], ALU.mult))
                            own.link(V.tensor_scalar(h, h, -0.5, 1.5, ALU.mult, ALU.add))
                            own.link(V.tensor_tensor(r, y0, h, ALU.mult))
                            cut = LN_CUT[t]
                            V.tensor_scalar(x_sb[:, t, cut:D], x_sb[:, t, cut:D], ln_s[:, t, 12:13], r, ALU.subtract, ALU.mult).then_inc(ln_half, 1)
                            if cut:
                                xx = x_sb[:, t, 0:cut]
                                own.link(V.tensor_scalar(xx, xx, ln_s[:, t, 12:13], r, ALU.subtract, ALU.mult))
                                dve.wait_ge(ln_ld, 16 * (2 if first else 1))
                                own.link(V.tensor_tensor(xx, xx, lnp[:, 0, 0:cut], ALU.mult))
                                V.tensor_tensor(xx, xx, lnp[:, 1, 0:cut], ALU.add).then_inc(ln_done, 1)

                    norm(0, mix, (1, 2))

                    sg, sb, sl, gw, rk = (rt[:, j, :, :] for j in range(5))
                    for t in range(TT):
                        dve.wait_ge(lg_exp, t + 1)
                        own.link(V.tensor_tensor(sb[:, t, :], sg[:, t, :], biases[:, FOX:FOX + NE], ALU.add))
                        grp, tk, gm = rsm[:, 0:8], rsm[:, 8:16], rsm[:, 16:24]
                        for g in range(NGRP):
                            own.mark(V.max(gw[:, t, g * 8:(g + 1) * 8], sb[:, t, g * 8:(g + 1) * 8]))
                        own.settle()
                        best = gw[:, t, :].rearrange("p (g c) -> p g c", g=NGRP)
                        own.link(V.tensor_reduce(grp, best[:, :, 0:2], AX, ALU.add))
                        own.link(V.max(tk, grp))
                        own.link(V.tensor_scalar(gm, grp, tk[:, 3:4], None, ALU.is_gt))
                        own.link(V.tensor_scalar(rk[:, t, 0:8], grp, tk[:, 3:4], None, ALU.is_equal))
                        own.link(V.tensor_reduce(rk[:, t, 24:25], gm, AX, ALU.add))
                        own.link(V.tensor_tensor_scan(rk[:, t, 8:16], ones[:, 0:8], rk[:, t, 0:8], rk[:, t, 24:25], ALU.mult, ALU.add))
                        own.link(V.tensor_scalar(rk[:, t, 8:16], rk[:, t, 8:16], 4.0, None, ALU.is_le))
                        own.link(V.tensor_tensor(rk[:, t, 0:8], rk[:, t, 0:8], rk[:, t, 8:16], ALU.mult))
                        own.link(V.tensor_tensor(gm, gm, rk[:, t, 0:8], ALU.max))
                        own.link(V.tensor_scalar(rk[:, t, 16:24], gm, -NEG, NEG, ALU.mult, ALU.add))
                        sbg = sb[:, t, :].rearrange("p (g c) -> p g c", g=NGRP)
                        gmb = gm.unsqueeze(2).broadcast_to([P, NGRP, 8])
                        own.link(V.tensor_tensor(sbg, sbg, gmb, ALU.mult))
                        own.link(V.tensor_tensor(sbg, sbg, rk[:, t, 16:24].unsqueeze(2).broadcast_to([P, NGRP, 8]), ALU.add))
                        own.link(V.max(tk, sb[:, t, :]))
                        own.link(V.match_replace(sb[:, t, :], tk, sb[:, t, :], TAKEN))
                        own.link(V.tensor_scalar(sl[:, t, :], sb[:, t, :], -2.0e38, None, ALU.is_le))
                    own.link(V.tensor_tensor(gw, sg, sl, ALU.mult))
                    dve.nop().then_inc(sel_ready, 1)
                    own.link(V.tensor_reduce(rsm[:, 0:TT], gw, AX, ALU.add))
                    own.link(V.reciprocal(rsm[:, 2:2 + TT], rsm[:, 0:TT]))
                    for t in range(TT):
                        own.link(V.tensor_scalar(gw[:, t, :], gw[:, t, :], rsm[:, 2 + t:3 + t], ROUTED_SCALE, ALU.mult, ALU.mult))
                        own.link(V.tensor_copy(gw2[:, t, :, 0], gw[:, t, :]))
                        own.link(V.tensor_tensor(gwr[:, :], gw[:, t, :], gw2[:, t, :, 0], ALU.subtract))
                        own.link(V.tensor_copy(gw2[:, t, :, 1], gwr[:, :]))
                        own.link(V.tensor_tensor(gw2[:, t, :, 2], gwr[:, :], gw2[:, t, :, 1], ALU.subtract))
                    dve.wait_ge(ranks, 1)
                    own.link(V.tensor_copy(rk, bank[4][:, 0:TT * NE].rearrange("p (t e) -> p t e", t=TT)))
                    own.link(V.tensor_reduce(rsm[0:1, 8:9], bank[4][0:1, 2 * NE:3 * NE], AX, ALU.max))
                    own.link(V.tensor_scalar(flag[0:1, 0:1], rsm[0:1, 8:9], float(SLOTS) + 0.5, None, ALU.is_gt))
                    dve.nop().then_inc(routed_ready, 1)

                    A, B, C, R = bank[4], bank[5], bank[6], bank[7]
                    R_hot = R[:, 0:P].bitcast(BF16)

                    def one_hot(sw, par, n):
                        for t in range(TT):
                            for e in range(2):
                                ins = V.tensor_scalar(hot[par][:, t, e * SLOTS:(e + 1) * SLOTS], iota1,
                                                      rk[:, t, bass.ds(n * 2 + e, 1)], sl[:, t, bass.ds(n * 2 + e, 1)], ALU.is_equal, ALU.mult)
                                own.mark(ins)
                        own.settle()
                        dve.nop().then_inc(sw.hot, 1)

                    def read_gathered(sw, par, k):
                        dve.wait_ge(sw.gat, k)
                        V.tensor_copy(xgT[par][:, 4:8, :], B[:, :].rearrange("p (k c) -> p k c", k=4)).then_inc(sw.xg, 1)

                    def read_hotT(sw, par):
                        own.mark(V.tensor_copy(hotT[par][:, :], R_hot))
                        for e in range(2):
                            rows_ = slice(e * SLOTS, (e + 1) * SLOTS)
                            own.mark(V.tensor_reduce(gslot[rows_, par:par + 1], R[rows_, P + 3 * e:P + 3 * e + 3], AX, ALU.add))
                        own.settle()
                        dve.nop().then_inc(sw.hotT, 1)

                    def silu(sw, k):
                        dve.wait_ge(sw.ex, k)
                        own.link(V.tensor_tensor(sig[:, :], sig[:, :], C[:, 0:EF], ALU.mult))
                        V.tensor_tensor(h_sb[:, :], sig[:, :], C[:, EF:2 * EF], ALU.mult).then_inc(sw.h, 1)

                    def read_hT(sw, k):
                        dve.wait_ge(sw.ht_ps, k)
                        V.tensor_copy(hT[:, :, :].rearrange("p f c -> p (f c)"), R[:, T:T + EF]).then_inc(sw.ht, 1)

                    def y_low(sw, par, k):
                        for c in range(2):
                            dve.wait_ge(sw.yh, 2 * k + (c - 1))
                            own.mark(V.scalar_tensor_tensor(y_lo[:, c * 512:(c + 1) * 512], (A, B)[c][:, :], gslot[:, par:par + 1],
                                                            y_hi[:, c * 512:(c + 1) * 512].bitcast(F32), ALU.mult, ALU.subtract))
                        own.settle()
                        dve.nop().then_inc(sw.yl, 1)

                    def step(s, n, first=False, last=False):
                        if not last:
                            one_hot(main, 1 - s, n + 1)
                        silu(main, n + 1)
                        if not last:
                            read_gathered(main, 1 - s, n + 2)
                        read_hT(main, n + 1)
                        if not last:
                            if not first:
                                dve.wait_ge(main.sc, n)
                            read_hotT(main, 1 - s)
                        y_low(main, s, n + 1)
                        own.restart()

                    own.restart()
                    one_hot(main, 0, 0)
                    dve.wait_ge(sh_exp, 1)
                    flat = "p f c -> p (f c)"
                    s_all = shS[:, :, :].rearrange(flat)
                    own.link(V.tensor_tensor(s_all, s_all, bank[6], ALU.mult))
                    V.tensor_tensor(shT[:, :, :].rearrange(flat), s_all, bank[7], ALU.mult).then_inc(sh_h, 1)
                    read_gathered(main, 0, 1)
                    read_hotT(main, 0)
                    step(0, 0, first=True)
                    with dve.Fori(0, PAIRS // 2 - 1) as i:
                        step(1, 2 * i + 1)
                        step(0, 2 * i + 2)
                    step(1, PAIRS - 1, last=True)
                    dve.wait_ge(main.sc, PAIRS - 1)
                    own.restart()
                    more = dve.value_load(flag[0:1, 0:1], min_val=0, max_val=1)
                    with dve.If(more > 0):
                        with dve.Fori(0, ROUNDS - 1) as r:
                            dve.wait_ge(combined, TT)
                            own.link(V.tensor_scalar(rk, rk, float(SLOTS), None, ALU.subtract))
                            own.restart()
                            with dve.Fori(0, PAIRS) as n:
                                k = r * PAIRS + n + 1
                                dve.wait_ge(over.sc, k)
                                one_hot(over, 0, n)
                                read_gathered(over, 0, k)
                                read_hotT(over, 0)
                                silu(over, k)
                                read_hT(over, k)
                                y_low(over, 0, k)
                                own.restart()
                        dve.wait_ge(over.sc, (ROUNDS - 1) * PAIRS + 1)
                    with dve.Else():
                        dve.nop()
                    norm(TT, combined, (1, 2))
                    own.settle()

            engines = (nc.sync, nc.scalar, nc.vector, nc.tensor, nc.gpsimd)
            for n, s in enumerate(names):
                engines[n % len(engines)].sem_clear(s)
            nc.all_engine_barrier()

        with nc.Block() as block:
            @block.sync
            def _(sp):
                sp.dma_start(out.rearrange("b (t p) d -> p (b t) d", p=P), x_sb[:, :, :]).then_inc(stored, 16)
                sp.wait_ge(stored, 16)


def shape_constants():
    i = np.arange(P)
    tok = np.arange(T)
    half = HD // 2
    inv = np.float32(10000.0) ** (-np.arange(half, dtype=np.float32) * np.float32(2.0 / HD))
    ang = tok.astype(np.float32)[:, None] * inv.astype(np.float32)[None, :]
    cos, sin = np.cos(ang), np.sin(ang)
    rope = np.stack([np.concatenate([cos, cos], 1), np.concatenate([-sin, sin], 1)])
    rope = rope.reshape(2, TT, P, HD).transpose(2, 0, 1, 3)
    last = np.arange(NC) * CMP_STRIDE + CMP_LEN - 1
    vis = last[None, :] <= tok[:, None]
    cvis = np.zeros((T, 16), np.float32)
    cvis[:, :NC] = np.where(vis, 0.0, NEG)
    misc = np.concatenate([cvis.reshape(TT, P, 16).transpose(1, 0, 2).reshape(P, TT * 16),
                           vis.any(1).astype(np.float32).reshape(TT, P).T,
                           np.broadcast_to(np.arange(1, SLOTS + 1, dtype=np.float32), (P, SLOTS)),
                           np.tile(np.array([[1 / SCALE, 0, 0, 1], [0, 1, -1 / SCALE, 0]], np.float32), (P // 2, 1))], 1)
    return {
        "ident": np.eye(P, dtype=np.float32), 
        "cmask": np.where(i[None, :] <= i[:, None], 0.0, NEG).astype(np.float32),
        "upper": (tok[:, None] <= tok[None, :]).astype(np.float32).reshape(TT, P, T).transpose(1, 0, 2).copy(),
        "rope": np.ascontiguousarray(rope, np.float32), "misc": np.ascontiguousarray(misc, np.float32),
        "ones": np.ones((P, T), np.float32),
    }


def column_order():
    at, off = {}, 0
    for name, width in (("fox_q", 256), ("fox_k", 256), ("fox_v", 256), ("fox_f", 4), ("nsa_q", 384), ("nsa_kc", 128), ("nsa_vc", 128),
                        ("nsa_ks", 128), ("nsa_vs", 128), ("nsa_kw", 128), ("nsa_vw", 128), ("nsa_g", 18), ("dsa_q", 384),
                        ("dsa_k", 64), ("dsa_v", 64), ("idx_q", 256), ("idx_k", 64), ("idx_w", 4)):
        at[name] = np.arange(off, off + width)
        off += width

    def head(name, h):
        return at[name][h * HD:(h + 1) * HD]

    nq = [head("nsa_q", g * REP + r) for r in range(REP) for g in range(GRP)]
    return [
        at["idx_q"],
        np.concatenate([at["idx_k"], at["dsa_k"], at["nsa_kc"]]),
        np.concatenate([at["nsa_vw"], at["dsa_v"], at["fox_f"], at["nsa_g"], at["idx_w"]]),
        np.concatenate([at["nsa_vc"], at["nsa_vs"]]),
        at["fox_q"], at["fox_k"], at["fox_v"],
        np.concatenate(nq[0:4]),
        np.concatenate(nq[4:6] + [at["nsa_ks"]]),
        at["dsa_q"][0:PIECE],
        np.concatenate([at["dsa_q"][PIECE:], at["nsa_kw"]]),
    ]


def lay_out(inputs):
    g = {k: np.asarray(v) for k, v in inputs.items()}
    L = DEPTH

    def by_partition(w):
        return w.reshape(L, -1, P, w.shape[-1]).transpose(0, 2, 1, 3)

    npieces = N_IN_PIECES + 2 + N_OUT_PIECES
    pieces = np.zeros((L, npieces, P, KD, PIECE), np.float32)
    w_in = by_partition(g["w_in"])
    for c, cols in enumerate(column_order()):
        n = STREAM.index(("in", c))
        pieces[:, n, :, :, :len(cols)] = w_in[:, :, :, cols]
    for n, name in enumerate(("cmp_w1_k", "cmp_w1_v")):
        pieces[:, STREAM.index(("cmp", n))] = by_partition(g[name]).reshape(L, P, KD, PIECE)
    heads = ([0, 1, 2, 3] + [FOX + gg * REP + r for r in range(REP) for gg in range(GRP)] + [FOX + NSA + h for h in range(DSA)])
    w_out = g["w_out"].reshape(L, 16, HD, D)[:, heads].reshape(L, D, D)
    w_out = by_partition(w_out)
    for n in range(N_OUT_PIECES):
        pieces[:, STREAM.index(("out", n))] = w_out[:, :, :, n * PIECE:(n + 1) * PIECE]

    pieces[:, 0] = np.roll(pieces[:, 0], -1, 0)

    def pos(name):
        return g[name].reshape(L, CPAIRS, P).transpose(0, 2, 1)

    small = np.concatenate([g["cmp_w2_k"], g["cmp_w2_v"], pos("cmp_pos_k"), pos("cmp_pos_v")], 2)
    rows = np.concatenate([g["fox_forget_bias"], g["b_router"]], 1)
    lnw = np.stack([np.concatenate([g["ln1_g"], g["ln1_b"]], 1), np.concatenate([g["ln2_g"], g["ln2_b"]], 1)], 1)

    def expert(gate, up, down):
        n = gate.shape[0]
        o = np.empty((n, P, EW), np.float32)
        gu = o[:, :, :EGU].reshape(n, P, KD, 2, EF)
        gu[:, :, :, 0] = gate.reshape(n, KD, P, EF).transpose(0, 2, 1, 3)
        gu[:, :, :, 1] = up.reshape(n, KD, P, EF).transpose(0, 2, 1, 3)
        o[:, :, :EGU] = gu.reshape(n, P, EGU)
        o[:, :, EGU:] = down.reshape(n, EF // P, P, D).transpose(0, 2, 1, 3).reshape(n, P, -1)
        return o

    moe = expert(g["w_gate"].reshape(L * NE, D, EF), g["w_up"].reshape(L * NE, D, EF), g["w_down"].reshape(L * NE, EF, D))
    return {
        "x": g["x"], "pieces": pieces.reshape(L, npieces, P, KD * PIECE), "rows": rows, "small": small,
        "moe_w": moe.reshape(L, NE, P, EW), "ws": expert(g["ws_gate"], g["ws_up"], g["ws_down"]),
        "router": by_partition(g["w_router"]).reshape(L, P, KD * NE), "lnw": lnw,
    }


def kernel(**inputs):
    import concourse.bacc as _bacc
    from concourse.bass_utils import run_bass_kernel_spmd as _run

    nc = _bacc.Bacc("TRN2", target_bir_lowering=False, num_devices=1)
    arrays, args = {}, {}
    for name, a in {**lay_out(inputs), **{"const_" + k: v for k, v in shape_constants().items()}}.items():
        a = np.ascontiguousarray(a)
        arrays[f"in_{name}"] = a
        args[name] = nc.dram_tensor(f"in_{name}", a.shape, mybir.dt.from_np(a.dtype), kind="ExternalInput").ap()
    out = nc.dram_tensor("out_0", (1, T, D), F32, kind="ExternalOutput").ap()
    consts = {k[6:]: args.pop(k) for k in list(args) if k.startswith("const_")}
    build(nc, consts=consts, out=out, **args)
    r = _run(nc, [arrays], core_ids=[0])
    return r.results[0]["out_0"]
```

```python
import numpy as np
import concourse.bass as bass
from concourse import mybir
from contextlib import ExitStack

F32 = mybir.dt.float32
F32R = mybir.dt.float32r
BF16 = mybir.dt.bfloat16
I32 = mybir.dt.int32
ALU = mybir.AluOpType
ACT = mybir.ActivationFunctionType
AX = mybir.AxisListType.X

P = 128
DEPTH, D, T = 2, 1024, 256
TT = T // P
KD = D // P
HD = 64
FOX, NSA, GRP, DSA, IDX = 4, 6, 2, 6, 4
REP = NSA // GRP
SCALE = HD ** -0.5
PIECE = 256
N_IN_PIECES, N_OUT_PIECES = 11, 4
CROWS = 32
FROWS = 32
RING = 5
STREAM = [("in", c) for c in range(7)] + [("cmp", 0), ("cmp", 1)] + [("in", c) for c in range(7, 11)] + [("out", n) for n in range(4)]
SPLIT_IN = [n for n, (what, c) in enumerate(STREAM) if what == "in" and c >= 2]
SPLIT_OUT = [n for n, (what, c) in enumerate(STREAM) if what == "out"]
SPLIT = SPLIT_IN + SPLIT_OUT
HI_RING = 4
LO_VECTOR = (2, 3, 6, 12)
LO_POOL = [n for n in SPLIT if n not in LO_VECTOR]
CMP_LEN, CMP_STRIDE = 32, 16
NC = (T - CMP_LEN) // CMP_STRIDE + 1
CPAIRS = CMP_LEN // 2
TOPK = min(256, T // 4)
NE, EF = 64, 256
NGRP = 8
MOE_TOPK = 8
PAIRS = NE // 2
SLOTS = 64
ROUNDS = T // SLOTS
EW = KD * 2 * EF + (EF // P) * D
EGU = KD * 2 * EF
ROUTED_SCALE = 2.5
ALPHA = (2 * DEPTH) ** 0.25
LN_EPS = 1e-5
LN_CUT = (0, 640)
NEG = -1e30
TAKEN = -3.0e38
BIG = 3.0e38

ROPE_PIECES = (0, 1, 7, 8, 9, 10)
TURNED = (0, 1, 3, 4, 5, 7, 8, 9, 10)
TILE_OF = {0: 0, 4: 4, 5: 6, 7: 8, 8: 10, 9: 12, 10: 14}
T_IQ, T_IK, T_DK, T_FQ, T_FK, T_NQ, T_KS, T_DQ, T_KW = 0, 2, 3, 4, 6, 8, 11, 12, 15
V_W, V_D, V_MISC, V_S, V_F = 0, 128, 192, 218, 346
VCOLS = 602
M_F, M_G, M_W = V_MISC, V_MISC + 4, V_MISC + 22

UNITS = ([("fox", 0, 0), ("fox", 1, 1)]
         + [(k, 2 + r, r) for r in range(REP) for k in ("slc", "win")]
         + [("dsa", 5 + i, i) for i in range(3)])
NU = len(UNITS)
TURNS = []
for _u, (_k, _o, _r) in enumerate(UNITS):
    TURNS.append(("unit", _u))
    if _k == "win":
        TURNS.append(("cmp", _r))
TURN_OF_UNIT = {u: v for v, (k, u) in enumerate(TURNS) if k == "unit"}


class Order:

    def __init__(self, eng, sem):
        self.eng, self.sem, self.n = eng, sem, 0

    def mark(self, ins):
        self.n += 1
        ins.then_inc(self.sem, 1)

    def link(self, ins):
        self.mark(ins)
        self.eng.wait_ge(self.sem, self.n)

    def settle(self):
        if self.n:
            self.eng.wait_ge(self.sem, self.n)

    def restart(self):
        self.settle()
        self.eng.sem_clear(self.sem)
        self.n = 0


def build(nc, x, pieces, rows, small, moe_w, ws, router, lnw, consts, out):
    ctx = ExitStack()
    with ctx:
        at = [(nc.sbuf_base + 63) // 64 * 64]

        def place(name, shape, dt=F32, where=None):
            size = int(np.prod(shape[1:])) * (2 if dt == BF16 else 4)
            size = (size + 31) // 32 * 32
            start = at[0] if where is None else where[0]
            t = nc.alloc_sbuf_tensor_at(name, shape, dt, offset=start)
            if where is None:
                at[0] += size
            else:
                where[0] += size
            return t

        ex = [place(f"expert_weights{s}", [P, 2, EW]) for s in range(2)]
        sp_at = [at[0] - 8 * EW]
        piece_hi = [place(f"piece_hi{j}", [P, KD, PIECE], F32R, where=sp_at) for j in range(HI_RING)]
        x_hi = place("x_hi", [P, KD, T], F32R, where=sp_at)
        x_lo = place("x_lo", [P, KD, T], F32R, where=sp_at)
        assert sp_at[0] <= at[0]
        ring_at = at[0]
        piece = [place(f"piece{s}", [P, KD, PIECE]) for s in range(RING)]
        piece_lo = [place(f"piece_lo{s}", [P, KD, PIECE], F32R, where=[ring_at + 4 * s * KD * PIECE]) for s in range(RING)]
        moe_at, ring_end = [ring_at], at[0]
        x_sb = place("x_sb", [P, TT, D])
        xT = place("xT", [P, KD, T])
        shared_at = at[0]
        qkT = place("qkT", [P, 16, T])
        cmpT = place("cmpT", [P, 2, GRP, T])
        hq = place("hq", [P, 4, PIECE])
        assert at[0] - shared_at == EW * 4
        ln_at = at[0]
        prob = place("prob", [P, 2, 2, 3 * P])
        probT = [place("probT0", [P, 2, 3 * P]), place("probT1", [P, 2, 3 * P], where=[shared_at + 4 * 16 * T])]
        c_rows = place("c_rows", [P, 2, T], where=[ln_at + 4 * 2 * 3 * P])
        vbuf = place("vbuf", [P, TT, VCOLS])
        score = place("score", [P, 3 * P])
        rtmp = place("rtmp", [P, 2, 3 * P], where=[ln_at])
        dmask = place("dmask", [P, 3 * P], BF16)
        route_at = at[0]
        blkT = place("blkT", [P, 2, CPAIRS, CROWS])
        rope_tmp = place("rope_tmp", [P, PIECE])
        gates = place("gates", [P, TT, 18])
        fz = place("fz", [P, 4, TT * 4])
        sm_neg = place("sm_neg", [P, 2, 4])
        sm_max = place("sm_max", [P, 2, 4])
        sm_sum = place("sm_sum", [P, 2, 4])
        sm_r = place("sm_r", [P, 2, 4])
        top8 = place("top8", [P, 8])
        w_idx = place("w_idx", [P, TT, IDX])
        hgelu = place("hgelu", [2 * CROWS, 3, P])
        hgT = place("hgT", [P, 2 * CROWS])
        kcT = place("kcT", [P, 16])
        vc_sb = place("vc_sb", [16, GRP, HD])
        pc = place("pc", [P, TT, REP * GRP, 16])
        pcs = place("pcs", [P, 4, TT * REP * GRP])
        smalls = place("smalls", [P, 2 * HD + 2 * CPAIRS])
        biases = place("biases", [P, FOX + NE])
        ln_s = place("ln_s", [P, TT, 24])
        ident = place("ident", [P, P])
        identb = place("identb", [P, P], BF16)
        cmask = place("cmask", [P, 2, P], BF16)
        upper = place("upper", [P, TT, T])
        rope_cs = place("rope_cs", [P, 2, TT, HD])
        misc_c = place("misc_c", [P, TT * 16 + TT + SLOTS + 4])
        cvis = misc_c[:, 0:TT * 16].rearrange("p (t c) -> p t c", t=TT)
        anyvis = misc_c[:, TT * 16:TT * 16 + TT]
        iota1 = misc_c[:, TT * 16 + TT:TT * 16 + TT + SLOTS]
        row_mix = misc_c[:, TT * 16 + TT + SLOTS:]
        ones = place("ones", [P, T])
        assert at[0] <= nc.sbuf_usable_end

        cmask_f = place("cmask_f", [P, P], where=[shared_at])
        wsh = place("shared_weights", [P, EW], where=[shared_at])
        lnp = place("ln_rows", [P, 2, D], where=[ln_at])
        ra = [route_at]
        wr = place("router_w", [P, KD, NE], where=ra)
        rt = place("route", [P, 5, TT, NE], where=[ln_at + 4 * 2 * D + 0])
        xs = [place(f"x_part{j}", [P, TT, D], BF16, where=moe_at) for j in range(3)]
        xgT = [place(f"gathered{s}", [P, KD, P], F32, where=moe_at) for s in range(2)]
        y_hi = place("y_hi", [P, D], F32R, where=moe_at)
        y_lo = place("y_lo", [P, D], F32R, where=moe_at)
        rest = place("x_rest", [P, TT, D], F32, where=[moe_at[0] - 8 * D])
        hot = [place(f"hot{s}", [P, TT, P], BF16, where=moe_at) for s in range(2)]
        hotT = [place(f"hotT{s}", [P, T], F32R, where=moe_at) for s in range(2)]
        h_sb = place("h_sb", [P, EF], F32, where=moe_at)
        hT = place("hT", [P, EF // P, P], F32, where=moe_at)
        sig = place("sig", [P, EF], F32, where=moe_at)
        assert moe_at[0] <= ring_end
        gw2 = place("gate_weights", [P, TT, NE, 3], BF16, where=ra)
        gwr = place("gate_rest", [P, NE], F32, where=ra)
        gslot = place("gate_slot", [P, 2], F32, where=ra)
        flag = place("overflow", [1, 1], I32, where=ra)
        rsm = place("route_small", [P, 24], F32, where=ra)
        assert ra[0] <= route_at + 4 * 2 * CPAIRS * CROWS + 4 * PIECE, ra[0] - route_at
        sh_at = [ln_at + 4 * (2 * D + 5 * TT * NE)]
        shT = place("shared_hT", [P, 2, T], F32, where=sh_at)
        shS = place("shared_sig", [P, 2, T], F32, where=sh_at)
        assert sh_at[0] <= route_at

        bank = [ctx.enter_context(nc.psum_tensor(f"bank{b}", [P, 512], F32))[:, :] for b in range(8)]

        names = []

        def sem(name):
            s = ctx.enter_context(nc.semaphore(name))
            names.append(s)
            return s

        once = ctx.enter_context(nc.semaphore("constants_loaded"))
        x_ld = ctx.enter_context(nc.semaphore("x_loaded"))
        stored = ctx.enter_context(nc.semaphore("output_stored"))
        piece_ld = [sem(f"piece_loaded{s}") for s in range(RING)]
        gu_ld = [[sem(f"gate_up_half{h}_loaded{s}") for s in range(2)] for h in range(2)]
        dn_ld = [sem(f"down_loaded{s}") for s in range(2)]
        small_ld, ln_ld, ws_ld, wr_ld = sem("smalls_loaded"), sem("ln_rows_loaded"), sem("shared_loaded"), sem("router_loaded")
        xt_ps, xt_sb = sem("x_transposed"), sem("xT_ready")
        proj = sem("projected")
        out_dve, out_act = sem("projection_rotated"), sem("projection_copied")
        hq_dve, hq_act = sem("rotated_heads"), sem("plain_heads")
        turned, turned_out = sem("heads_transposed"), sem("heads_in_sbuf")
        dots, dots_out = sem("index_dots"), sem("index_relu")
        dots_free = sem("index_relu_used")
        dmask_ready = sem("dsa_mask_ready")
        misc_rd, gate_exp, gates_ready = sem("misc_ready"), sem("gate_exp"), sem("gates_ready")
        fabs, fln, lf_ready, cum, c_ready = sem("fox_abs"), sem("fox_ln"), sem("fox_log_forget"), sem("fox_cumsum"), sem("fox_rows_ready")
        blk_ready, hid, gelu_u, gelu_e, gelu_ready = sem("cmp_blocks"), sem("cmp_hidden"), sem("gelu_arg"), sem("gelu_exp"), sem("gelu_ready")
        kv_ps, kv_sb = sem("cmp_kv"), sem("cmp_kv_sb")
        sc_ps, sc_sub, sc_exp, pc_ready = sem("cmp_scores"), sem("cmp_shifted"), sem("cmp_exp"), sem("cmp_probs")
        s_ready, m_ready, e_ready, p_ready = sem("scores"), sem("row_max"), sem("exps"), sem("probs")
        pt_ps, pt_sb, pv, o_sb = sem("probs_turned"), sem("probsT_ready"), sem("values_added"), sem("heads_out")
        mix = sem("mixed")
        ln_var, ln_rs, ln_half = sem("ln_variance"), sem("ln_rstd0"), sem("ln_half_normalised")
        ln_done, ln_done_pool = sem("ln_done_by_vector"), sem("ln_done_by_gpsimd")
        pad_ready, hg_ps, hg_sb = sem("block_padding_zero"), sem("gelu_turned"), sem("geluT_ready")
        split_a, split_rest, split_b, split_c = sem("x_part0_ready"), sem("x_rest_ready"), sem("x_part1_ready"), sem("x_part2_ready")
        logits, lg_exp, sel_ready, ranks, routed_ready = sem("router_logits"), sem("router_exp"), sem("selected"), sem("ranks"), sem("routes_ready")
        sh_ps, sh_exp, sh_gate = sem("shared_gate_up"), sem("shared_sigmoid"), sem("shared_silu")
        sh_up, sh_h = sem("shared_up_sb"), sem("shared_h")
        dve_own, act_own, pool_own = sem("vector_order"), sem("scalar_order"), sem("pool_order")

        class Sweep:

            def __init__(self, tag):
                self.hot, self.gat, self.xg, self.hotT = sem(tag + "hot_ready"), sem(tag + "gathered"), sem(tag + "gathered_sb"), sem(tag + "hotT_ready")
                self.gu, self.ex, self.h = sem(tag + "gate_up"), sem(tag + "sigmoid"), sem(tag + "h_ready")
                self.ht_ps, self.ht = sem(tag + "h_transposed"), sem(tag + "hT_ready")
                self.dn, self.yh, self.yl, self.sc = sem(tag + "down"), sem(tag + "y_hi_ready"), sem(tag + "y_lo_ready"), sem(tag + "added_back")

        main, over = Sweep("main_"), Sweep("over_")
        over_ld = sem("over_loaded")
        combined = sem("experts_combined")
        xhi_ready, xlo_ready = sem("x_hi_ready"), sem("x_lo_ready")
        hi_ready, lo_dve, lo_pool = sem("piece_hi_ready"), sem("piece_lo_by_vector"), sem("piece_lo_by_gpsimd")
        heads_split = sem("heads_split")
        early_ps, early_sb = ctx.enter_context(nc.semaphore("first_x_transposed")), ctx.enter_context(nc.semaphore("first_xT_ready"))
        early_piece = ctx.enter_context(nc.semaphore("first_piece_loaded"))
        piece_ahead = sem("next_layers_piece_loaded")

        def piece_count(n):
            return 16 * (n // RING + (n % RING > 0))

        def parts_ready(eng, n):
            if n in LO_VECTOR:
                eng.wait_ge(lo_dve, LO_VECTOR.index(n) + 1)
            else:
                eng.wait_ge(lo_pool, LO_POOL.index(n) + 1)

        def hi_free(eng, n):
            q = SPLIT.index(n)
            if q >= HI_RING:
                what, c = STREAM[SPLIT[q - HI_RING]]
                assert what == "in"
                eng.wait_ge(proj, 2 * c + 2)

        def flat_piece(t):
            return t[:, :, :].rearrange("p k c -> p (k c)")

        def hi_of(n):
            return piece_hi[SPLIT.index(n) % HI_RING]

        def score_bank(u):
            return 2 * ((u + 1) % 2)

        def ps_proj(c, t):
            return bank[(2 * c + t) % 4][:, 0:PIECE]

        def proj_out(c):
            if c in ROPE_PIECES:
                return out_dve, 2 * ROPE_PIECES.index(c) + 1
            if c in (4, 5):
                return hq_ready(c)
            return out_act, 2 * [2, 3, 6].index(c) + 1

        def hq_ready(c):
            if c in ROPE_PIECES:
                return hq_dve, 2 * ROPE_PIECES.index(c) + 1
            return hq_act, 2 * [3, 4, 5].index(c) + 1

        def turn_x(pe, done, t, banks):
            for g in range(2):
                for j in range(4):
                    mm = pe.transpose(banks[g][:, j * P:(j + 1) * P], x_sb[:, t, (g * 4 + j) * P:(g * 4 + j + 1) * P], ident[:, :])
                mm.then_inc(done, 1)

        def normalised(eng, second, t):
            eng.wait_ge(ln_done_pool, second * TT + t + 1)
            if LN_CUT[t]:
                eng.wait_ge(ln_done, second + 1)

        def copy_xT(act, turned_, ready, first, t, banks):
            for g in range(2):
                act.wait_ge(turned_, first + 2 * t + g + 1)
                act.copy(xT[:, 4 * g:4 * g + 4, t * P:(t + 1) * P], banks[g].rearrange("p (k c) -> p k c", k=4)).then_inc(ready, 1)

        with nc.Block() as block:
            @block.sync
            def _(sp):
                for dst, src in ((x_sb[:, :, :], x.rearrange("b (t p) d -> p (b t) d", p=P)),
                                 (ident[:, :], consts["ident"])):
                    sp.dma_start(dst, src).then_inc(x_ld, 16)
                sp.dma_start(piece[0][:, :, :], pieces[DEPTH - 1, 0].rearrange("p (k c) -> p k c", k=KD)).then_inc(early_piece, 16)
                for dst, src in ((cmask_f[:, :], consts["cmask"]),
                                 (upper[:, :, :], consts["upper"]),
                                 (rope_cs[:, :, :, :], consts["rope"]), (misc_c[:, :], consts["misc"]),
                                 (ones[:, :], consts["ones"])):
                    sp.dma_start(dst, src).then_inc(once, 16)
                sp.wait_ge(early_piece, 16)
                sp.wait_ge(once, 16 * 5)

            @block.tensor
            def _(pe):
                pe.wait_ge(x_ld, 32)
                for t in range(TT):
                    turn_x(pe, early_ps, t, (bank[4 + 2 * t], bank[5 + 2 * t]))

            @block.scalar
            def _(act):
                for t in range(TT):
                    copy_xT(act, early_ps, early_sb, 0, t, (bank[4 + 2 * t], bank[5 + 2 * t]))

            @block.vector
            def _(dve):
                dve.wait_ge(x_ld, 32)
                dve.wait_ge(once, 16 * 5)
                nc.vector.tensor_copy(identb[:, :], ident[:, :])
                for a in range(2):
                    nc.vector.tensor_copy(cmask[:, a, :], cmask_f[:, :])

        with nc.Fori(0, DEPTH) as layer:
            def of(t):
                return t[bass.ds(layer, 1)]

            with nc.Block() as block:
                @block.sync
                def _(sp):
                    def load_piece(n):
                        if n >= RING:
                            what, m = STREAM[n - RING]
                            if what == "in":
                                sp.wait_ge(proj, 2 * m + 2)
                            else:
                                sp.wait_ge(hid, 1)
                        sp.dma_start(piece[n % RING][:, :, :],
                                     of(pieces)[0, n].rearrange("p (k c) -> p k c", k=KD)).then_inc(piece_ld[n % RING], 16)

                    def load_pair(s, which, pair):
                        a, b, ld = ((0, EGU // 2, gu_ld[0]), (EGU // 2, EGU, gu_ld[1]), (EGU, EW, dn_ld))[which]
                        sp.dma_start(ex[s][:, :, a:b],
                                     of(moe_w)[0, bass.ds(pair * 2, 2), :, a:b].rearrange("e p c -> p e c")).then_inc(ld[s], 16)

                    for n in range(1, RING):
                        load_piece(n)
                    sp.dma_start(smalls[:, :], of(small).rearrange("l p c -> p (l c)")).then_inc(small_ld, 16)
                    sp.dma_start(biases[:, :], of(rows)[0].partition_broadcast(P)).then_inc(small_ld, 16)
                    for n in range(RING, N_IN_PIECES + 2 + N_OUT_PIECES):
                        load_piece(n)
                        if n in SPLIT_OUT[:3]:
                            load_pair(0, SPLIT_OUT.index(n), 0)
                    sp.wait_ge(o_sb, 8)
                    sp.dma_start(wsh[:, :], of(ws)[0]).then_inc(ws_ld, 16)
                    sp.dma_start(lnp[:, :, :].rearrange("p a d -> p (a d)"),
                                 of(lnw)[0, 0].partition_broadcast(P)).then_inc(ln_ld, 16)
                    sp.dma_start(wr[:, :, :].rearrange("p k e -> p (k e)"), of(router)[0]).then_inc(wr_ld, 16)
                    sp.wait_ge(mix, TT)
                    for which in range(3):
                        load_pair(1, which, 1)
                    normalised(sp, 0, TT - 1)
                    sp.dma_start(lnp[:, :, :].rearrange("p a d -> p (a d)"),
                                 of(lnw)[0, 1].partition_broadcast(P)).then_inc(ln_ld, 16)
                    with sp.Fori(1, PAIRS // 2) as i:
                        for s in range(2):
                            for half in range(2):
                                sp.wait_ge(main.gu, 4 * i + (2 * s - 3 + half))
                                load_pair(s, half, 2 * i + s)
                            sp.wait_ge(main.dn, 2 * i + (s - 1))
                            load_pair(s, 2, 2 * i + s)
                    sp.wait_ge(combined, TT)
                    more = sp.value_load(flag[0:1, 0:1], min_val=0, max_val=1)
                    with sp.If(more > 0):
                        with sp.Fori(0, ROUNDS - 1) as r:
                            with sp.Fori(0, PAIRS) as n:
                                sp.wait_ge(over.sc, r * PAIRS + n + 1)
                                sp.dma_start(ex[0][:, :, :], of(moe_w)[0, bass.ds(n * 2, 2)].rearrange("e p c -> p e c")).then_inc(over_ld, 16)
                        sp.wait_ge(over.sc, (ROUNDS - 1) * PAIRS + 1)
                    with sp.Else():
                        sp.nop()
                    sp.dma_start(piece[0][:, :, :], of(pieces)[0, 0].rearrange("p (k c) -> p k c", k=KD)).then_inc(piece_ahead, 16)
                    sp.wait_ge(piece_ahead, 16)

                @block.tensor
                def _(pe):
                    def three_products(out_, n, t, ks, opens=True):
                        cols = slice(t * P, (t + 1) * P)
                        hi, lo = hi_of(n), piece_lo[n % RING]
                        for k in ks:
                            pe.matmul(out_, x_hi[:, k, cols], hi[:, k, :], start=(k == 0 and opens), stop=False, skip_group_check=True)
                            pe.matmul(out_, x_hi[:, k, cols], lo[:, k, :], start=False, stop=False, skip_group_check=True)
                            mm = pe.matmul(out_, x_lo[:, k, cols], hi[:, k, :], start=False, stop=(k == KD - 1), skip_group_check=True)
                        return mm

                    def project(c, between=None):
                        n = STREAM.index(("in", c))
                        if n in SPLIT:
                            parts_ready(pe, n)
                            pe.wait_ge(xlo_ready, 2)
                        elif n > 0:
                            pe.wait_ge(piece_ld[n % RING], piece_count(n))
                        for t in range(TT):
                            if c >= 2:
                                reader, count = proj_out(c - 2)
                                pe.wait_ge(reader, count + t)
                            if n in SPLIT:
                                for k in range(KD):
                                    if between is not None:
                                        between(t, k)
                                    mm = three_products(ps_proj(c, t), n, t, (k,))
                            else:
                                for k in range(KD):
                                    mm = pe.matmul(ps_proj(c, t), xT[:, k, t * P:(t + 1) * P], piece[n % RING][:, k, :],
                                                   start=(k == 0), stop=(k == KD - 1))
                            mm.then_inc(proj, 1)

                    turns = [(c, t) for c in TURNED for t in range(TT)]

                    def turn_heads(c):
                        for t in range(TT):
                            j = turns.index((c, t))
                            writer, count = hq_ready(c)
                            pe.wait_ge(writer, count + t)
                            if j >= 2:
                                pe.wait_ge(turned_out, j - 1)
                            b, src = bank[4 + j % 2], hq[:, (2 * c + t) % 4, :]
                            for q in range(1 if c == 3 else 2):
                                mm = pe.transpose(b[:, q * P:(q + 1) * P], src[:, q * P:(q + 1) * P], ident[:, :])
                            mm.then_inc(turned, 1)

                    def pair_dots(b0, b1, tq, tk, more=True):
                        for q, (a, w) in enumerate(((0, P), (P, 2 * P))):
                            for h, b in ((0, b0), (1, b1)):
                                r = slice(h * HD, (h + 1) * HD)
                                mm = pe.matmul(b[:, a:a + w], qkT[r, tq, q * P:(q + 1) * P], qkT[r, tk, 0:w],
                                               start=(q == 0), stop=not more, skip_group_check=True)
                        return mm

                    def index_dots(i):
                        if i == 0:
                            pe.wait_ge(turned_out, 4)
                        else:
                            pe.wait_ge(dots_out, 2 * i)
                        pair_dots(bank[6], bank[7], T_IQ + i, T_IK, more=False).then_inc(dots, 1)

                    def fox_rows():
                        pe.wait_ge(lf_ready, 1)
                        pe.wait_ge(dots_out, 4)
                        for h in range(FOX):
                            for t in range(TT):
                                lf = fz[:, 3, t * 4 + h:t * 4 + h + 1].broadcast_to([P, FROWS])
                                mm = pe.matmul(bank[6][h * FROWS:(h + 1) * FROWS, 0:T], lf, upper[:, t, :], start=(t == 0), stop=(t == TT - 1))
                        mm.then_inc(cum, 1)

                    def cmp_hidden():
                        pe.wait_ge(c_ready, 2)
                        for kv in range(2):
                            n = STREAM.index(("cmp", kv))
                            pe.wait_ge(piece_ld[n % RING], piece_count(n))
                        pe.wait_ge(pad_ready, 1)
                        pe.wait_ge(blk_ready, 2)
                        for i in range(CPAIRS):
                            for kv in range(2):
                                n = STREAM.index(("cmp", kv))
                                w1 = piece[n % RING][:, :, :].rearrange("p k c -> p (k c)")
                                mm = pe.matmul(bank[7][kv * CROWS:(kv + 1) * CROWS, 0:P], blkT[:, kv, i, :], w1[:, i * P:(i + 1) * P],
                                               start=(i == 0), stop=(i == CPAIRS - 1))
                        mm.then_inc(hid, 1)

                    def cmp_turn():
                        pe.wait_ge(gelu_ready, 1)
                        pe.transpose(bank[6][:, 256:256 + 2 * CROWS], hgelu[:, 2, :], ident[0:2 * CROWS, 0:2 * CROWS]).then_inc(hg_ps, 1)

                    def cmp_kv():
                        pe.wait_ge(hg_sb, 1)
                        pe.wait_ge(small_ld, 32)
                        for g in range(GRP):
                            pe.matmul(bank[6][g * HD:(g + 1) * HD, 0:NC], smalls[:, 0:HD], hgT[:, g * NC:(g + 1) * NC], start=True, stop=True)
                        for g in range(GRP):
                            mm = pe.matmul(bank[6][0:NC, 64 + g * HD:64 + (g + 1) * HD], hgT[:, CROWS + g * NC:CROWS + (g + 1) * NC], smalls[:, HD:2 * HD], start=True, stop=True)
                        mm.then_inc(kv_ps, 1)

                    def cmp_scores(j):
                        if j == 0:
                            pe.wait_ge(kv_sb, 2)
                            pe.wait_ge(turned_out, 2 * TURNED.index(8) + 2)
                        if j < TT * REP:
                            for g in range(GRP):
                                t, rows_ = j // REP, slice(g * HD, (g + 1) * HD)
                                mm = pe.matmul(bank[6 + g][:, j * 16:j * 16 + NC], qkT[rows_, T_NQ + j % REP, t * P:(t + 1) * P], kcT[rows_, 0:NC], start=True, stop=True)
                            if j == TT * REP - 1:
                                mm.then_inc(sc_ps, 1)

                    def scores(u):
                        kind, o, i = UNITS[u]
                        b0, b1 = bank[score_bank(u)], bank[score_bank(u) + 1]
                        if u >= 2:
                            pe.wait_ge(e_ready, u - 1)
                        if u < 2:
                            pe.wait_ge(out_dve, 2 * ROPE_PIECES.index(9 + u) + 2)
                            pe.wait_ge(turned_out, 2 * TURNED.index(5) + 2)
                        if u == 2:
                            pe.wait_ge(turned_out, 2 * len(TURNED))
                        if kind == "dsa":
                            pe.wait_ge(dmask_ready, 1)

                        tq, tk = {"fox": (T_FQ + i, T_FK + i), "slc": (T_NQ + i, T_KS), "win": (T_NQ + i, T_KW), "dsa": (T_DQ + i, T_DK)}[kind]
                        pair_dots(b0, b1, tq, tk)
                        if kind == "fox":
                            for q, (a, w) in enumerate(((0, P), (P, 2 * P))):
                                for h, b in ((0, b0), (1, b1)):
                                    rows_ = slice((2 * i + h) * FROWS, (2 * i + h + 1) * FROWS)
                                    pe.matmul(b[:, a:a + w], c_rows[rows_, 0, q * P:(q + 1) * P], c_rows[rows_, 1, 0:w], start=False, stop=False, skip_group_check=True)
                        for h, b in ((0, b0), (1, b1)):
                            if kind == "dsa":
                                mm = pe.matmul(b[:, 0:3 * P], identb[:, :], dmask[:, :], start=False, stop=True, skip_group_check=True)
                            else:
                                diag = b[:, 0:4 * P].rearrange("p (a c) -> p a c", a=2)[:, :, 0:P]
                                mm = pe.matmul(diag, identb[:, :], cmask[:, :, :], start=False, stop=True, skip_group_check=True)
                        mm.then_inc(s_ready, 1)

                    def values(kind, h, i):
                        c = {"fox": V_F + (2 * i + h) * HD, "slc": V_S + h * HD, "win": V_W + h * HD, "dsa": V_D}[kind]
                        return slice(c, c + HD)

                    def turn_probs(v):
                        what, u = TURNS[v]
                        if v >= 1:
                            pe.wait_ge(pt_sb, v)
                        else:
                            pe.wait_ge(turned_out, 2 * len(TURNED))
                        if what == "unit":
                            pe.wait_ge(p_ready, u + 1)
                            for h in range(2):
                                for j in range(3):
                                    mm = pe.transpose(bank[4 + h][:, j * P:(j + 1) * P], prob[:, u % 2, h, j * P:(j + 1) * P], ident[:, :])
                        else:
                            pe.wait_ge(pc_ready, 1)
                            for g in range(GRP):
                                for t in range(TT):
                                    mm = pe.transpose(bank[4][0:NC, (g * TT + t) * P:(g * TT + t + 1) * P], pc[:, t, u * GRP + g, 0:NC], ident[:, :])
                        mm.then_inc(pt_ps, 1)

                    def add_values(v):
                        what, u = TURNS[v]
                        pe.wait_ge(pt_sb, v + 1)
                        if what == "unit":
                            kind, o, i = UNITS[u]
                            first, last = kind != "win", kind not in ("slc", "win")
                            if first and o >= 2:
                                pe.wait_ge(o_sb, o - 1)
                            if o == 0:
                                pe.wait_ge(sc_sub, 1)
                            ob = bank[6 + o % 2]
                            for h in range(2):
                                pe.matmul(ob[h * HD:(h + 1) * HD, 0:T], vbuf[:, 0, values(kind, h, i)], probT[v % 2][:, h, 0:T], start=first, stop=False, skip_group_check=True)
                            for h in range(2):
                                mm = pe.matmul(ob[h * HD:(h + 1) * HD, P:T], vbuf[:, 1, values(kind, h, i)], probT[v % 2][:, h, T:T + P], start=False, stop=last, skip_group_check=True)
                        else:
                            o = 2 + u
                            for g in range(GRP):
                                mm = pe.matmul(bank[6 + o % 2][g * HD:(g + 1) * HD, 0:T], vc_sb[0:NC, g, :],
                                               probT[v % 2][0:NC, :, :].rearrange("p h c -> p (h c)")[:, g * T:(g + 1) * T], start=False, stop=True, skip_group_check=True)
                        mm.then_inc(pv, 1)

                    project(0)
                    project(1)
                    turn_heads(0)
                    project(2)
                    turn_heads(1)
                    project(3)
                    index_dots(0)
                    project(4)
                    index_dots(1)
                    turn_heads(3)
                    project(5)
                    fox_rows()
                    turn_heads(4)
                    project(6)
                    turn_heads(5)
                    cmp_hidden()
                    project(7)
                    project(8)
                    cmp_turn()
                    turn_heads(7)
                    cmp_kv()
                    project(9)
                    turn_heads(8)

                    def between(t, k):
                        if t == 0:
                            cmp_scores(k)
                        elif k == 0:
                            scores(0)

                    project(10, between=between)
                    turn_heads(9)
                    scores(1)
                    turn_heads(10)
                    def out_product(t, n, ks):
                        return three_products(bank[2 * t + n // 2][:, (n % 2) * PIECE:(n % 2 + 1) * PIECE], SPLIT_OUT[n], t, ks, opens=(n % 2 == 0))

                    early_k = 4
                    early_parts = [(n, k) for n in range(N_OUT_PIECES) for k in range(early_k)]

                    def out_early(count):
                        for _ in range(count):
                            n, k = early_parts.pop(0)
                            if k == 0:
                                parts_ready(pe, SPLIT_OUT[n])
                            out_product(0, n, (k,))

                    for v, (what, u) in enumerate(TURNS):
                        if what == "unit" and u + 2 < NU:
                            scores(u + 2)
                        if v == len(TURNS) - 2:
                            pe.wait_ge(e_ready, NU - 1)
                            pe.wait_ge(heads_split, early_k)
                            out_early(5)
                        if v == len(TURNS) - 1:
                            out_early(3)
                        turn_probs(v)
                        if v >= 1:
                            add_values(v - 1)
                    out_early(2)
                    add_values(len(TURNS) - 1)
                    out_early(len(early_parts))

                    pe.wait_ge(e_ready, NU)
                    for k in range(early_k, KD):
                        pe.wait_ge(heads_split, k + 1)
                        for n in range(N_OUT_PIECES):
                            mm = out_product(0, n, (k,))
                    mm.then_inc(mix, 1)
                    for n in range(N_OUT_PIECES):
                        mm = out_product(1, n, range(KD))
                    mm.then_inc(mix, 1)

                    def route(t):
                        normalised(pe, 0, t)
                        turn_x(pe, xt_ps, t, (bank[4 - 2 * t], bank[5 - 2 * t]))
                        pe.wait_ge(xt_sb, 2 * t + 2)
                        for k in range(KD):
                            mm = pe.matmul(bank[5][:, t * NE:(t + 1) * NE], xT[:, k, t * P:(t + 1) * P], wr[:, k, :], start=(k == 0), stop=(k == KD - 1))
                        mm.then_inc(logits, 1)

                    def shared_gate_up(f, t, to):
                        for k in range(KD):
                            mm = pe.matmul(to, wsh[:, k * 2 * EF + f * P:k * 2 * EF + (f + 1) * P],
                                           xT[:, k, t * P:(t + 1) * P], start=(k == 0), stop=(k == KD - 1))
                        return mm

                    pe.wait_ge(wr_ld, 16)
                    pe.wait_ge(ws_ld, 16)
                    for t in range(TT):
                        route(t)
                        for f in range(2):
                            mm = shared_gate_up(f, t, bank[6][:, (f * TT + t) * P:(f * TT + t + 1) * P])
                    mm.then_inc(sh_ps, 1)
                    shared_gate_up(2, 0, bank[0][:, 0:P])
                    pe.wait_ge(sel_ready, 1)
                    sel0, sel1 = rt[:, 2, 0, :], rt[:, 2, 1, :]
                    pe.matmul(bank[4][:, 0:NE], upper[:, 0, 0:P], sel0, start=True, stop=True)
                    pe.matmul(bank[4][:, NE:2 * NE], upper[:, 0, P:T], sel0, start=True, stop=False)
                    pe.matmul(bank[4][:, NE:2 * NE], upper[:, 1, P:T], sel1, start=False, stop=True)
                    pe.matmul(bank[4][0:1, 2 * NE:3 * NE], ones[:, 0:1], sel0, start=True, stop=False)
                    pe.matmul(bank[4][0:1, 2 * NE:3 * NE], ones[:, 0:1], sel1, start=False, stop=True).then_inc(ranks, 1)
                    shared_gate_up(2, 1, bank[0][:, P:T]).then_inc(sh_ps, 1)
                    A, B, C, R = bank[4], bank[5], bank[6], bank[7]
                    R_hot = R[:, 0:P].bitcast(BF16)

                    def shared_down(t, c):
                        pe.wait_ge(sh_h, 1)
                        for f in range(2):
                            pe.matmul(bank[2 * t + c][:, :], shT[:, f, t * P:(t + 1) * P], wsh[:, EGU + f * D + c * 512:EGU + f * D + (c + 1) * 512],
                                      start=False, stop=False, skip_group_check=True)

                    def shared_part(n):
                        if n < TT:
                            shared_gate_up(3, n, C[:, 0:P]).then_inc(sh_ps, 1)
                        elif n > TT:
                            shared_down((n - 3) // 2, (n - 3) % 2)

                    def gather(sw, par, n, k, first=False):
                        pe.wait_ge(sw.hot, k)
                        H = hot[par]
                        for t in range(TT):
                            pe.transpose(R_hot[:, t * P:(t + 1) * P], H[:, t, :], identb[:, :])
                        for d in range(KD):
                            o = (A, B)[d // 4][:, (d % 4) * P:(d % 4 + 1) * P]
                            for j in range(3 * TT):
                                pe.matmul(o, xs[j // TT][:, j % TT, d * P:(d + 1) * P], H[:, j % TT, :], start=(j == 0), stop=(j == 3 * TT - 1))
                        if first:
                            pe.wait_ge(routed_ready, 1)
                        for t in range(TT):
                            mm = pe.matmul(R[:, P:P + 6], H[:, t, :], gw2[:, t, bass.ds(n * 2, 2), :].rearrange("p e h -> p (e h)"), start=(t == 0), stop=(t == TT - 1))
                        mm.then_inc(sw.gat, 1)

                    def gate_up(sw, par, W, k, loaded=None):
                        pe.wait_ge(sw.xg, 2 * k)
                        for d in range(KD):
                            if loaded is not None and d == KD // 2:
                                pe.wait_ge(*loaded)
                            for e in range(2):
                                mm = pe.matmul(C[e * SLOTS:(e + 1) * SLOTS, :], xgT[par][:, d, e * SLOTS:(e + 1) * SLOTS],
                                               W[:, e, d * 2 * EF:(d + 1) * 2 * EF], start=(d == 0), stop=(d == KD - 1))
                            if d % (KD // 2) == KD // 2 - 1:
                                mm.then_inc(sw.gu, 1)

                    def turn_h(sw, k):
                        pe.wait_ge(sw.h, k)
                        for f in range(EF // P):
                            mm = pe.transpose(R[:, T + f * P:T + (f + 1) * P], h_sb[:, f * P:(f + 1) * P], ident[:, :])
                        mm.then_inc(sw.ht_ps, 1)

                    def down(sw, W, k):
                        pe.wait_ge(sw.ht, k)
                        for c in range(2):
                            for f in range(2):
                                for e in range(2):
                                    mm = pe.matmul((A, B)[c][e * SLOTS:(e + 1) * SLOTS, :], hT[:, f, e * SLOTS:(e + 1) * SLOTS],
                                                   W[:, e, EGU + f * D + c * 512:EGU + f * D + (c + 1) * 512], start=(f == 0), stop=(f == 1))
                        mm.then_inc(sw.dn, 1)

                    def add_back(sw, par, k, last=False, opens=False):
                        pe.wait_ge(sw.yl, k)
                        pe.wait_ge(sw.hotT, k)
                        for t in range(TT):
                            for c in range(2):
                                for y in (y_hi, y_lo):
                                    mm = pe.matmul(bank[2 * t + c][:, :], hotT[par][:, t * P:(t + 1) * P], y[:, c * 512:(c + 1) * 512],
                                                   start=(opens and y is y_hi), stop=False, skip_group_check=True)
                            if last:
                                mm.then_inc(combined, 1)
                        if not last:
                            mm.then_inc(sw.sc, 1)

                    def step(s, n, i, first=False, last=False, early=False):
                        pe.wait_ge(gu_ld[0][s], 16 * i + 16)
                        if early and 0 < n <= TT:
                            pe.wait_ge(sh_up, n + 1)
                        gate_up(main, s, ex[s], n + 1, loaded=(gu_ld[1][s], 16 * i + 16))
                        if not last:
                            if not first:
                                pe.wait_ge(main.yl, n)
                            pe.wait_ge(main.hotT, n + 1)
                            gather(main, 1 - s, n + 1, n + 2)
                        if last:
                            add_back(main, 1 - s, n)
                        turn_h(main, n + 1)
                        if early:
                            shared_part(n)
                        if not first and not last:
                            add_back(main, 1 - s, n, opens=early and n == 1)
                        pe.wait_ge(dn_ld[s], 16 * i + 16)
                        if not last:
                            pe.wait_ge(main.xg, 2 * (n + 2))
                        down(main, ex[s], n + 1)

                    pe.wait_ge(split_b, TT)
                    pe.wait_ge(split_c, TT)
                    gather(main, 0, 0, 1, first=True)
                    early_pairs = 1 + TT + 4
                    for n in range(early_pairs):
                        step(n % 2, n, n // 2, first=(n == 0), early=True)
                    with pe.Fori(early_pairs // 2, PAIRS // 2 - 1) as i:
                        step(1, 2 * i + 1, i)
                        step(0, 2 * i + 2, i + 1)
                    step(1, PAIRS - 1, PAIRS // 2 - 1, last=True)
                    add_back(main, 1, PAIRS, last=True)

                    more = pe.value_load(flag[0:1, 0:1], min_val=0, max_val=1)
                    with pe.If(more > 0):
                        pe.nop().then_inc(over.sc, 1)
                        with pe.Fori(0, ROUNDS - 1) as r:
                            with pe.Fori(0, PAIRS) as n:
                                k = r * PAIRS + n + 1
                                gather(over, 0, n, k)
                                pe.wait_ge(over_ld, 16 * k)
                                gate_up(over, 0, ex[0], k)
                                turn_h(over, k)
                                down(over, ex[0], k)
                                add_back(over, 0, k)
                    with pe.Else():
                        pe.nop()
                    for t in range(TT):
                        normalised(pe, 1, t)
                        turn_x(pe, xt_ps, t, (bank[4 + 2 * t], bank[5 + 2 * t]))

                @block.scalar
                def _(act):
                    own = Order(act, act_own)

                    def read_plain(c):
                        for t in range(TT):
                            act.wait_ge(proj, 2 * c + t + 1)
                            ps, slot = ps_proj(c, t), (2 * c + t) % 4
                            if c == 2:
                                act.copy(vbuf[:, t, 0:V_S], ps[:, 0:V_S]).then_inc(out_act, 1)
                            elif c == 6:
                                act.copy(vbuf[:, t, V_F:V_F + PIECE], ps).then_inc(out_act, 1)
                            elif c == 3:
                                act.wait_ge(turned, 2 + t + 1)
                                act.copy(hq[:, slot, 0:P], ps[:, 0:P]).then_inc(hq_act, 1)
                                act.copy(vbuf[:, t, V_S:V_S + P], ps[:, P:2 * P]).then_inc(out_act, 1)
                            else:
                                if c == 5:
                                    act.wait_ge(turned, 4 + t + 1)
                                act.copy(hq[:, slot, :], ps).then_inc(hq_act, 1)

                    def read_turned(c):
                        for t in range(TT):
                            j = 2 * TURNED.index(c) + t
                            act.wait_ge(turned, j + 1)
                            b = bank[4 + j % 2]
                            cols = slice(t * P, (t + 1) * P)
                            halves = (slice(0, HD), slice(HD, P))
                            if c == 1:
                                for src, n in ((0, T_IK), (1, T_DK)):
                                    for dst in range(2):
                                        own.mark(act.copy(qkT[halves[dst], n, cols], b[halves[src], 0:P]))
                            elif c in TILE_OF:
                                n = TILE_OF[c]
                                src = b[:, 0:2 * P].rearrange("p (a c) -> p a c", a=2)
                                own.mark(act.copy(qkT[:, n:n + 2, cols], src))
                            if c in (1, 3):
                                kv, o = (0, P) if c == 1 else (1, 0)
                                lo = 1 if t == 0 else 0
                                for g in range(GRP):
                                    own.mark(act.copy(cmpT[0:HD, kv, g, cols], b[halves[g], o:o + P]))
                                    own.mark(act.copy(cmpT[HD:P, kv, g, t * P + lo - 1:(t + 1) * P - 1], b[halves[g], o + lo:o + P]))
                            own.settle()
                            act.nop().then_inc(turned_out, 1)

                    def relu_dots(i):
                        act.wait_ge(dots, i + 1)
                        if i == 1:
                            act.wait_ge(dots_free, 2)
                        for h in range(2):
                            act.activation(rtmp[:, h, :], bank[6 + h][:, 0:3 * P], ACT.Relu).then_inc(dots_out, 1)

                    def misc():
                        own.settle()
                        act.wait_ge(out_act, 2)
                        for t in range(TT):
                            act.activation(gates[:, t, :], vbuf[:, t, M_G:M_G + 18], ACT.Exp, scale=-1.0).then_inc(gate_exp, 1)
                        act.wait_ge(fabs, 1)
                        own.link(act.activation(fz[:, 2, :], fz[:, 1, :], ACT.Exp, scale=-1.0))
                        act.activation(fz[:, 3, :], fz[:, 2, :], ACT.Ln, bias=1.0).then_inc(fln, 1)

                    def fox_rows_out():
                        act.wait_ge(cum, 1)
                        act.wait_ge(dots_free, 4)
                        for j in range(2):
                            act.activation(c_rows[:, j, :], bank[6][:, 0:T], ACT.Identity, scale=row_mix[:, 2 * j:2 * j + 1],
                                           bias=row_mix[:, 2 * j + 1:2 * j + 2]).then_inc(c_ready, 1)

                    def split_hi(n):
                        act.wait_ge(piece_ld[n % RING], piece_count(n))
                        hi_free(act, n)
                        act.copy(flat_piece(hi_of(n)), flat_piece(piece[n % RING])).then_inc(hi_ready, 1)

                    for g in range(2):
                        act.copy(x_hi[:, 4 * g:4 * g + 4, :], xT[:, 4 * g:4 * g + 4, :]).then_inc(xhi_ready, 1)
                    split_hi(2)
                    split_hi(3)
                    read_turned(0)
                    split_hi(4)
                    read_plain(2)
                    read_turned(1)
                    misc()
                    split_hi(5)
                    read_plain(3)
                    split_hi(6)
                    relu_dots(0)
                    read_plain(4)
                    relu_dots(1)
                    read_turned(3)
                    split_hi(9)
                    read_plain(5)
                    fox_rows_out()
                    read_turned(4)
                    split_hi(10)
                    read_plain(6)
                    read_turned(5)
                    split_hi(11)
                    split_hi(12)
                    act.wait_ge(gelu_u, 1)
                    act.activation(hgelu[:, 1, :], hgelu[:, 1, :], ACT.Exp, scale=1.0).then_inc(gelu_e, 1)
                    act.wait_ge(hg_ps, 1)
                    act.copy(hgT[:, :], bank[6][:, 256:256 + 2 * CROWS]).then_inc(hg_sb, 1)
                    read_turned(7)
                    act.wait_ge(kv_ps, 1)
                    act.copy(kcT[:, 0:NC], bank[6][:, 0:NC]).then_inc(kv_sb, 1)
                    act.copy(vc_sb[0:NC, :, :], bank[6][0:NC, 64:64 + P].rearrange("p (g c) -> p g c", g=GRP)).then_inc(kv_sb, 1)
                    read_turned(8)

                    def exps(u):
                        act.wait_ge(m_ready, u + 1)
                        if u >= 2:
                            act.wait_ge(pt_ps, TURN_OF_UNIT[u - 2] + 1)
                        for h in range(2):
                            for q, (a, w) in enumerate(((0, P), (P, 2 * P))):
                                c = 2 * h + q
                                own.mark(act.activation(prob[:, u % 2, h, a:a + w], bank[score_bank(u) + h][:, a:a + w], ACT.Exp,
                                                        bias=sm_neg[:, u % 2, c:c + 1], scale=SCALE, accum_out=sm_sum[:, u % 2, c:c + 1]))
                        own.settle()
                        act.nop().then_inc(e_ready, 1)

                    def heads_out(v):
                        what, u = TURNS[v]
                        kind, o, _ = UNITS[u] if what == "unit" else ("cmp", 2 + u, 0)
                        if kind in ("fox", "dsa", "cmp"):
                            act.wait_ge(pv, v + 1)
                            act.copy(xT[:, o, :], bank[6 + o % 2][:, 0:T]).then_inc(o_sb, 1)

                    act.wait_ge(sc_sub, 1)
                    act.activation(pc[:, :, :, 0:NC], pc[:, :, :, 0:NC], ACT.Exp, scale=SCALE).then_inc(sc_exp, 1)
                    exps(0)
                    read_turned(9)
                    read_turned(10)
                    for v, (what, u) in enumerate(TURNS):
                        if what == "unit" and u + 1 < NU:
                            exps(u + 1)
                        act.wait_ge(pt_ps, v + 1)
                        if v >= 2:
                            act.wait_ge(pv, v - 1)
                        if what == "unit":
                            for h in range(2):
                                own.mark(act.copy(probT[v % 2][:, h, :], bank[4 + h][:, 0:3 * P]))
                        else:
                            own.mark(act.copy(probT[v % 2][0:NC, :, :].rearrange("p h c -> p (h c)")[:, 0:2 * T], bank[4][0:NC, :]))
                        own.settle()
                        act.nop().then_inc(pt_sb, 1)
                        if v >= 1:
                            heads_out(v - 1)
                    heads_out(len(TURNS) - 1)

                    def deviation(first, t):
                        act.wait_ge(ln_var, first + t + 1)
                        act.activation(ln_s[:, t, 16:17], ln_s[:, t, 15:16], ACT.Sqrt).then_inc(ln_rs, 1)

                    def split_x(t):
                        act.copy(xs[0][:, t, :], x_sb[:, t, :]).then_inc(split_a, 1)

                    def router_out(t):
                        act.wait_ge(logits, t + 1)
                        act.activation(rt[:, 0, t, :], bank[5][:, t * NE:(t + 1) * NE], ACT.Sigmoid).then_inc(lg_exp, 1)

                    deviation(0, 0)
                    copy_xT(act, xt_ps, xt_sb, 0, 0, (bank[4], bank[5]))
                    deviation(0, 1)
                    act.wait_ge(mix, TT)
                    split_x(0)
                    router_out(0)
                    copy_xT(act, xt_ps, xt_sb, 0, 1, (bank[2], bank[3]))
                    router_out(1)
                    split_x(1)
                    for t in range(TT):
                        act.wait_ge(split_rest, t + 1)
                        act.copy(xs[1][:, t, :], rest[:, t, :]).then_inc(split_b, 1)
                    act.wait_ge(sh_ps, 1)
                    act.activation(shS[:, :, :].rearrange("p f c -> p (f c)"), bank[6], ACT.Sigmoid).then_inc(sh_exp, 1)
                    act.wait_ge(sh_ps, 2)
                    act.copy(shT[:, 0, :], bank[0][:, 0:T]).then_inc(sh_up, 1)

                    A, B, C = bank[4], bank[5], bank[6]

                    def sigmoid(sw, k):
                        act.wait_ge(sw.gu, 2 * k)
                        act.activation(sig[:, :], C[:, 0:EF], ACT.Sigmoid).then_inc(sw.ex, 1)

                    def read_gathered(sw, par, k):
                        act.wait_ge(sw.gat, k)
                        act.copy(xgT[par][:, 0:4, :], A[:, :].rearrange("p (k c) -> p k c", k=4)).then_inc(sw.xg, 1)

                    def y_high(sw, par, k):
                        act.wait_ge(sw.dn, k)
                        act.wait_ge(sw.hotT, k)
                        for c in range(2):
                            act.activation(y_hi[:, c * 512:(c + 1) * 512], (A, B)[c][:, :], ACT.Copy, scale=gslot[:, par:par + 1]).then_inc(sw.yh, 1)

                    def step(s, n, last=False, early=False):
                        sigmoid(main, n + 1)
                        if not last:
                            read_gathered(main, 1 - s, n + 2)
                        if early and n < TT:
                            act.wait_ge(sh_ps, 3 + n)
                            act.copy(shT[:, 1, n * P:(n + 1) * P], C[:, 0:P]).then_inc(sh_up, 1)
                        y_high(main, s, n + 1)

                    read_gathered(main, 0, 1)
                    for n in range(3):
                        step(n % 2, n, early=True)
                    with act.Fori(1, PAIRS // 2 - 1) as i:
                        step(1, 2 * i + 1)
                        step(0, 2 * i + 2)
                    step(1, PAIRS - 1, last=True)
                    more = act.value_load(flag[0:1, 0:1], min_val=0, max_val=1)
                    with act.If(more > 0):
                        with act.Fori(0, ROUNDS - 1) as r:
                            with act.Fori(0, PAIRS) as n:
                                k = r * PAIRS + n + 1
                                read_gathered(over, 0, k)
                                sigmoid(over, k)
                                y_high(over, 0, k)
                    with act.Else():
                        act.nop()
                    for t in range(TT):
                        deviation(TT, t)
                    for t in range(TT):
                        copy_xT(act, xt_ps, xt_sb, 4, t, (bank[4 + 2 * t], bank[5 + 2 * t]))

                @block.gpsimd
                def _(pool):
                    own = Order(pool, pool_own)
                    G = nc.gpsimd
                    G.memset(blkT[:, :, :, GRP * NC:CROWS].rearrange("p a i c -> p (a i) c"), 0.0).then_inc(pad_ready, 1)

                    def split_lo(n):
                        if n in SPLIT_OUT:
                            pool.wait_ge(piece_ld[n % RING], piece_count(n))
                            hi_free(pool, n)
                            own.link(G.tensor_copy(flat_piece(hi_of(n)), flat_piece(piece[n % RING])))
                        else:
                            pool.wait_ge(hi_ready, SPLIT.index(n) + 1)
                        G.tensor_tensor(flat_piece(piece_lo[n % RING]), flat_piece(piece[n % RING]),
                                        flat_piece(hi_of(n)).bitcast(F32), ALU.subtract).then_inc(lo_pool, 1)

                    for n in LO_POOL:
                        split_lo(n)
                    pool.wait_ge(proj, 2 * N_IN_PIECES)
                    for o in range(KD - 1):
                        pool.wait_ge(o_sb, o + 1)
                        own.link(G.tensor_copy(x_hi[:, o, :], xT[:, o, :]))
                        G.tensor_tensor(x_lo[:, o, :], xT[:, o, :], x_hi[:, o, :].bitcast(F32), ALU.subtract).then_inc(heads_split, 1)

                    def scale_half(first):
                        for t in range(TT):
                            pool.wait_ge(ln_half, first + t + 1)
                            pool.wait_ge(ln_ld, 16 * (2 if first else 1))
                            cols = slice(LN_CUT[t], D)
                            xx = x_sb[:, t, cols]
                            own.link(G.tensor_tensor(xx, xx, lnp[:, 0, cols], ALU.mult))
                            G.tensor_tensor(xx, xx, lnp[:, 1, cols], ALU.add).then_inc(ln_done_pool, 1)

                    scale_half(0)
                    for t in range(TT):
                        pool.wait_ge(split_a, t + 1)
                        G.tensor_tensor(rest[:, t, :], x_sb[:, t, :], xs[0][:, t, :], ALU.subtract).then_inc(split_rest, 1)
                    for t in range(TT):
                        pool.wait_ge(split_b, t + 1)
                        G.tensor_tensor(xs[2][:, t, :], rest[:, t, :], xs[1][:, t, :], ALU.subtract).then_inc(split_c, 1)
                    pool.wait_ge(sh_gate, 1)
                    pool.wait_ge(sh_up, 1 + TT)
                    G.tensor_tensor(shT[:, :, :], shS[:, :, :], shT[:, :, :], ALU.mult).then_inc(sh_h, 1)
                    scale_half(TT)

                @block.vector
                def _(dve):
                    own = Order(dve, dve_own)
                    V = nc.vector

                    def rotate(c):
                        for t in range(TT):
                            j = 2 * TURNED.index(c) + t
                            slot = (2 * c + t) % 4
                            dve.wait_ge(proj, 2 * c + t + 1)
                            if c >= 7:
                                prev = {7: 5, 8: 4, 9: 7, 10: 8}[c]
                                dve.wait_ge(turned, 2 * TURNED.index(prev) + t + 1)
                            ps = ps_proj(c, t)
                            ph = ps.rearrange("p (h a c) -> p h a c", h=4, a=2)
                            cs = rope_cs[:, 0, t:t + 1, :].broadcast_to([P, 4, HD])
                            tm = rope_tmp[:, :].rearrange("p (h a c) -> p h a c", h=4, a=2)
                            own.mark(V.tensor_tensor(hq[:, slot, :].rearrange("p (h c) -> p h c", h=4), ps.rearrange("p (h c) -> p h c", h=4), cs, ALU.mult))
                            for a in range(2):
                                sn = rope_cs[:, 1, t:t + 1, a * 32:(a + 1) * 32].broadcast_to([P, 4, 32])
                                own.mark(V.tensor_tensor(tm[:, :, a, :], ph[:, :, 1 - a, :], sn, ALU.mult))
                            own.settle()
                            dve.nop().then_inc(out_dve, 1)
                            own.link(V.tensor_tensor(hq[:, slot, :], hq[:, slot, :], rope_tmp[:, :], ALU.add))
                            dve.nop().then_inc(hq_dve, 1)

                    def misc():
                        dve.wait_ge(out_act, 2)
                        dve.wait_ge(small_ld, 32)
                        for t in range(TT):
                            own.mark(V.tensor_tensor(fz[:, 0, t * 4:t * 4 + 4], vbuf[:, t, M_F:M_F + 4], biases[:, 0:FOX], ALU.add))
                            own.mark(V.tensor_scalar(w_idx[:, t, :], vbuf[:, t, M_W:M_W + 4], IDX ** -0.5, HD ** -0.5, ALU.mult, ALU.mult))
                        own.settle()
                        own.link(V.tensor_scalar(fz[:, 1, :], fz[:, 0, :], -1.0, None, ALU.mult))
                        V.tensor_tensor(fz[:, 1, :], fz[:, 1, :], fz[:, 0, :], ALU.max).then_inc(fabs, 1)
                        dve.wait_ge(gate_exp, 2)
                        own.link(V.tensor_scalar(gates[:, :, :], gates[:, :, :], 1.0, None, ALU.add))
                        own.link(V.reciprocal(gates[:, :, :], gates[:, :, :]))
                        own.link(V.tensor_scalar(fz[:, 0, :], fz[:, 0, :], 0.0, None, ALU.min))
                        dve.wait_ge(fln, 1)
                        V.tensor_tensor(fz[:, 3, :], fz[:, 0, :], fz[:, 3, :], ALU.subtract).then_inc(lf_ready, 1)

                    def index_sum(i):
                        for h in range(2):
                            n = 2 * i + h
                            dve.wait_ge(dots_out, n + 1)
                            for t, (a, w) in enumerate(((0, P), (P, 2 * P))):
                                wt = w_idx[:, t, n:n + 1]
                                if n == 0:
                                    own.mark(V.tensor_scalar(score[:, a:a + w], rtmp[:, h, a:a + w], wt, None, ALU.mult))
                                else:
                                    own.mark(V.scalar_tensor_tensor(score[:, a:a + w], rtmp[:, h, a:a + w], wt, score[:, a:a + w], ALU.mult, ALU.add))
                            own.settle()
                            dve.nop().then_inc(dots_free, 1)

                    def index_top():
                        for a in (0, 2 * P):
                            own.mark(V.tensor_tensor(score[:, a:a + P], score[:, a:a + P], cmask[:, 0, :], ALU.add))
                        own.settle()
                        for a, w in ((0, P), (P, 2 * P)):
                            s = score[:, a:a + w]
                            for _ in range(TOPK // 8):
                                own.link(V.max(top8[:, :], s))
                                own.link(V.match_replace(s, top8[:, :], s, TAKEN))
                        own.link(V.tensor_scalar(score[:, :], score[:, :], -2.0e38, NEG, ALU.is_gt, ALU.mult))
                        for a in (0, 2 * P):
                            own.mark(V.tensor_tensor(score[:, a:a + P], score[:, a:a + P], cmask[:, 0, :], ALU.add))
                        own.settle()
                        V.tensor_copy(dmask[:, :], score[:, :]).then_inc(dmask_ready, 1)

                    def blocks(kv):
                        dve.wait_ge(turned_out, 4 if kv == 0 else 6)
                        dve.wait_ge(small_ld, 32)
                        pe_row = smalls[:, 2 * HD + kv * CPAIRS:2 * HD + (kv + 1) * CPAIRS]
                        for i in range(CPAIRS):
                            blk = blkT[:, kv, i, 0:GRP * NC].rearrange("p (g c) -> p g c", g=GRP)
                            src = cmpT[:, kv, :, 2 * i:2 * i + CMP_STRIDE * (NC - 1) + 1:CMP_STRIDE]
                            own.mark(V.tensor_scalar(blk, src, pe_row[:, i:i + 1], None, ALU.add))
                        own.settle()
                        dve.nop().then_inc(blk_ready, 1)

                    def split_lo(n):
                        dve.wait_ge(hi_ready, SPLIT.index(n) + 1)
                        V.tensor_tensor(flat_piece(piece_lo[n % RING]), flat_piece(piece[n % RING]),
                                        flat_piece(hi_of(n)).bitcast(F32), ALU.subtract).then_inc(lo_dve, 1)

                    for g in range(2):
                        dve.wait_ge(xhi_ready, g + 1)
                        V.tensor_tensor(x_lo[:, 4 * g:4 * g + 4, :], xT[:, 4 * g:4 * g + 4, :], x_hi[:, 4 * g:4 * g + 4, :].bitcast(F32), ALU.subtract).then_inc(xlo_ready, 1)
                    rotate(0)
                    split_lo(2)
                    split_lo(3)
                    rotate(1)
                    misc()
                    split_lo(6)
                    index_sum(0)
                    index_sum(1)
                    blocks(0)
                    blocks(1)
                    index_top()

                    def maxima(u):
                        dve.wait_ge(s_ready, u + 1)
                        m = sm_max[:, u % 2, :].rearrange("p (h q) -> p q h", h=2)
                        for h in range(2):
                            for q, (a, w) in enumerate(((0, P), (P, 2 * P))):
                                own.mark(V.tensor_reduce(m[:, q, h:h + 1], bank[score_bank(u) + h][:, a:a + w], AX, ALU.max))
                        own.settle()
                        V.tensor_scalar(sm_neg[:, u % 2, :], sm_max[:, u % 2, :], -SCALE, None, ALU.mult).then_inc(m_ready, 1)

                    gv = gates[:, :, :].rearrange("p t (b g r) -> p b r g t", b=3, g=GRP)

                    def normalise(u):
                        kind, o, i = UNITS[u]
                        dve.wait_ge(e_ready, u + 1)
                        r = sm_r[:, u % 2, :]
                        own.link(V.reciprocal(r, sm_sum[:, u % 2, :]))
                        if kind in ("slc", "win"):
                            rv = r.rearrange("p (h q) -> p h q", h=2)
                            own.link(V.tensor_tensor(rv, rv, gv[:, 1 if kind == "slc" else 2, i], ALU.mult))
                        for h in range(2):
                            for q, (a, w) in enumerate(((0, P), (P, 2 * P))):
                                pr = prob[:, u % 2, h, a:a + w]
                                own.mark(V.tensor_scalar(pr, pr, r[:, 2 * h + q:2 * h + q + 1], None, ALU.mult))
                        own.settle()
                        dve.nop().then_inc(p_ready, 1)

                    dve.wait_ge(hid, 1)
                    hx, hu, ho = (hgelu[:, j, :] for j in range(3))
                    own.link(V.tensor_copy(hx, bank[7][0:2 * CROWS, 0:P]))
                    own.link(V.tensor_tensor(hu, hx, hx, ALU.mult))
                    c1 = float(np.sqrt(2 / np.pi))
                    own.link(V.tensor_scalar(hu, hu, -2 * c1 * 0.044715, -2 * c1, ALU.mult, ALU.add))
                    own.link(V.tensor_tensor(hu, hu, hx, ALU.mult))
                    V.tensor_scalar(hu, hu, 80.0, None, ALU.min).then_inc(gelu_u, 1)
                    dve.wait_ge(gelu_e, 1)
                    own.link(V.tensor_scalar(hu, hu, 1.0, None, ALU.add))
                    own.link(V.reciprocal(hu, hu))
                    V.tensor_tensor(ho, hx, hu, ALU.mult).then_inc(gelu_ready, 1)
                    rotate(7)
                    split_lo(12)
                    rotate(8)
                    rotate(9)
                    dve.wait_ge(sc_ps, 1)
                    heads = REP * GRP
                    for t in range(TT):
                        for g in range(GRP):
                            ps = bank[6 + g][:, t * REP * 16:(t + 1) * REP * 16].rearrange("p (h c) -> p h c", h=REP)[:, :, 0:NC]
                            own.mark(V.tensor_tensor(pc[:, t, g:heads:GRP, 0:NC], ps, cvis[:, t:t + 1, 0:NC].broadcast_to([P, REP, NC]), ALU.add))
                    own.settle()
                    own.link(V.tensor_reduce(pcs[:, 0, :].rearrange("p (t h) -> p t h", t=TT), pc[:, :, :, 0:NC], AX, ALU.max))
                    for t in range(TT):
                        mx = pcs[:, 0, t * heads:(t + 1) * heads].unsqueeze(2).broadcast_to([P, heads, NC])
                        own.mark(V.tensor_tensor(pc[:, t, :, 0:NC], pc[:, t, :, 0:NC], mx, ALU.subtract))
                    own.settle()
                    dve.nop().then_inc(sc_sub, 1)
                    maxima(0)
                    rotate(10)

                    def cmp_norm():
                        dve.wait_ge(sc_exp, 1)
                        own.link(V.tensor_reduce(pcs[:, 1, :].rearrange("p (t h) -> p t h", t=TT), pc[:, :, :, 0:NC], AX, ALU.add))
                        own.link(V.reciprocal(pcs[:, 2, :], pcs[:, 1, :]))
                        for t in range(TT):
                            w = pcs[:, 2, t * heads:(t + 1) * heads]
                            wv = w.rearrange("p (r g) -> p r g", r=REP)
                            own.link(V.scalar_tensor_tensor(wv, wv, anyvis[:, t:t + 1], gv[:, 0, :, :, t], ALU.mult, ALU.mult))
                            own.mark(V.tensor_tensor(pc[:, t, :, 0:NC], pc[:, t, :, 0:NC], w.unsqueeze(2).broadcast_to([P, heads, NC]), ALU.mult))
                        own.settle()
                        dve.nop().then_inc(pc_ready, 1)

                    cmp_norm()
                    maxima(1)
                    for u in range(NU):
                        normalise(u)
                        if u + 2 < NU:
                            maxima(u + 2)
                    o = KD - 1
                    dve.wait_ge(o_sb, KD)
                    dve.wait_ge(heads_split, KD - 1)
                    own.link(V.tensor_copy(x_hi[:, o, :], xT[:, o, :]))
                    V.tensor_tensor(x_lo[:, o, :], xT[:, o, :], x_hi[:, o, :].bitcast(F32), ALU.subtract).then_inc(heads_split, 1)

                    def norm(first, ready, counts):
                        for t in range(TT):
                            if ready is not None:
                                dve.wait_ge(ready, counts[t])
                            for c in range(2):
                                xx = x_sb[:, t, c * 512:(c + 1) * 512]
                                own.link(V.scalar_tensor_tensor(xx, xx, ALPHA, bank[2 * t + c], ALU.mult, ALU.add))
                                own.mark(V.bn_stats(ln_s[:, t, c * 6:c * 6 + 6], xx))
                            own.settle()
                            own.link(V.bn_aggr(ln_s[:, t, 12:14], ln_s[:, t, 0:12]))
                            V.tensor_scalar(ln_s[:, t, 15:16], ln_s[:, t, 13:14], LN_EPS, None, ALU.add).then_inc(ln_var, 1)
                            dve.wait_ge(ln_rs, first + t + 1)
                            own.link(V.reciprocal(ln_s[:, t, 17:18], ln_s[:, t, 16:17]))
                            y0, h, r = ln_s[:, t, 17:18], ln_s[:, t, 18:19], ln_s[:, t, 19:20]
                            own.link(V.tensor_tensor(h, y0, y0, ALU.mult))
                            own.link(V.tensor_tensor(h, h, ln_s[:, t, 15:16], ALU.mult))
                            own.link(V.tensor_scalar(h, h, -0.5, 1.5, ALU.mult, ALU.add))
                            own.link(V.tensor_tensor(r, y0, h, ALU.mult))
                            cut = LN_CUT[t]
                            V.tensor_scalar(x_sb[:, t, cut:D], x_sb[:, t, cut:D], ln_s[:, t, 12:13], r, ALU.subtract, ALU.mult).then_inc(ln_half, 1)
                            if cut:
                                xx = x_sb[:, t, 0:cut]
                                dve.wait_ge(ln_ld, 16 * (2 if first else 1))
                                own.link(V.scalar_tensor_tensor(xx, xx, ln_s[:, t, 12:13], lnp[:, 0, 0:cut], ALU.subtract, ALU.mult))
                                V.scalar_tensor_tensor(xx, xx, r, lnp[:, 1, 0:cut], ALU.mult, ALU.add).then_inc(ln_done, 1)

                    norm(0, mix, (1, 2))

                    sg, sb, sl, gw, rk = (rt[:, j, :, :] for j in range(5))
                    for t in range(TT):
                        dve.wait_ge(lg_exp, t + 1)
                        own.link(V.tensor_tensor(sb[:, t, :], sg[:, t, :], biases[:, FOX:FOX + NE], ALU.add))
                        grp, tk, gm = rsm[:, 0:8], rsm[:, 8:16], rsm[:, 16:24]
                        for g in range(NGRP):
                            own.mark(V.max(gw[:, t, g * 8:(g + 1) * 8], sb[:, t, g * 8:(g + 1) * 8]))
                        own.settle()
                        best = gw[:, t, :].rearrange("p (g c) -> p g c", g=NGRP)
                        own.link(V.tensor_reduce(grp, best[:, :, 0:2], AX, ALU.add))
                        own.link(V.max(tk, grp))
                        own.link(V.tensor_scalar(gm, grp, tk[:, 3:4], None, ALU.is_gt))
                        own.link(V.tensor_scalar(rk[:, t, 0:8], grp, tk[:, 3:4], None, ALU.is_equal))
                        own.link(V.tensor_reduce(rk[:, t, 24:25], gm, AX, ALU.add))
                        own.link(V.tensor_tensor_scan(rk[:, t, 8:16], ones[:, 0:8], rk[:, t, 0:8], rk[:, t, 24:25], ALU.mult, ALU.add))
                        own.link(V.tensor_scalar(rk[:, t, 8:16], rk[:, t, 8:16], 4.0, None, ALU.is_le))
                        own.link(V.tensor_tensor(rk[:, t, 0:8], rk[:, t, 0:8], rk[:, t, 8:16], ALU.mult))
                        own.link(V.tensor_tensor(gm, gm, rk[:, t, 0:8], ALU.max))
                        own.link(V.tensor_scalar(rk[:, t, 16:24], gm, -NEG, NEG, ALU.mult, ALU.add))
                        sbg = sb[:, t, :].rearrange("p (g c) -> p g c", g=NGRP)
                        gmb = gm.unsqueeze(2).broadcast_to([P, NGRP, 8])
                        own.link(V.tensor_tensor(sbg, sbg, gmb, ALU.mult))
                        own.link(V.tensor_tensor(sbg, sbg, rk[:, t, 16:24].unsqueeze(2).broadcast_to([P, NGRP, 8]), ALU.add))
                        own.link(V.max(tk, sb[:, t, :]))
                        own.link(V.match_replace(sb[:, t, :], tk, sb[:, t, :], TAKEN))
                        own.link(V.tensor_scalar(sl[:, t, :], sb[:, t, :], -2.0e38, None, ALU.is_le))
                    own.link(V.tensor_tensor(gw, sg, sl, ALU.mult))
                    dve.nop().then_inc(sel_ready, 1)
                    own.link(V.tensor_reduce(rsm[:, 0:TT], gw, AX, ALU.add))
                    own.link(V.reciprocal(rsm[:, 2:2 + TT], rsm[:, 0:TT]))

                    def gate_parts(t):
                        own.link(V.tensor_scalar(gw[:, t, :], gw[:, t, :], rsm[:, 2 + t:3 + t], ROUTED_SCALE, ALU.mult, ALU.mult))
                        own.link(V.tensor_copy(gw2[:, t, :, 0], gw[:, t, :]))
                        own.link(V.tensor_tensor(gwr[:, :], gw[:, t, :], gw2[:, t, :, 0], ALU.subtract))
                        own.link(V.tensor_copy(gw2[:, t, :, 1], gwr[:, :]))
                        own.link(V.tensor_tensor(gw2[:, t, :, 2], gwr[:, :], gw2[:, t, :, 1], ALU.subtract))

                    dve.wait_ge(ranks, 1)
                    own.link(V.tensor_copy(rk, bank[4][:, 0:TT * NE].rearrange("p (t e) -> p t e", t=TT)))
                    own.link(V.tensor_reduce(rsm[0:1, 8:9], bank[4][0:1, 2 * NE:3 * NE], AX, ALU.max))

                    A, B, C, R = bank[4], bank[5], bank[6], bank[7]
                    R_hot = R[:, 0:P].bitcast(BF16)

                    def one_hot(sw, par, n):
                        for t in range(TT):
                            for e in range(2):
                                ins = V.tensor_scalar(hot[par][:, t, e * SLOTS:(e + 1) * SLOTS], iota1,
                                                      rk[:, t, bass.ds(n * 2 + e, 1)], sl[:, t, bass.ds(n * 2 + e, 1)], ALU.is_equal, ALU.mult)
                                own.mark(ins)
                        own.settle()
                        dve.nop().then_inc(sw.hot, 1)

                    def read_gathered(sw, par, k):
                        dve.wait_ge(sw.gat, k)
                        V.tensor_copy(xgT[par][:, 4:8, :], B[:, :].rearrange("p (k c) -> p k c", k=4)).then_inc(sw.xg, 1)

                    def read_hotT(sw, par):
                        own.mark(V.tensor_copy(hotT[par][:, :], R_hot))
                        for e in range(2):
                            rows_ = slice(e * SLOTS, (e + 1) * SLOTS)
                            own.mark(V.tensor_reduce(gslot[rows_, par:par + 1], R[rows_, P + 3 * e:P + 3 * e + 3], AX, ALU.add))
                        own.settle()
                        dve.nop().then_inc(sw.hotT, 1)

                    def silu(sw, k):
                        dve.wait_ge(sw.ex, k)
                        own.link(V.tensor_tensor(sig[:, :], sig[:, :], C[:, 0:EF], ALU.mult))
                        V.tensor_tensor(h_sb[:, :], sig[:, :], C[:, EF:2 * EF], ALU.mult).then_inc(sw.h, 1)

                    def read_hT(sw, k):
                        dve.wait_ge(sw.ht_ps, k)
                        V.tensor_copy(hT[:, :, :].rearrange("p f c -> p (f c)"), R[:, T:T + EF]).then_inc(sw.ht, 1)

                    def y_low(sw, par, k):
                        for c in range(2):
                            dve.wait_ge(sw.yh, 2 * k + (c - 1))
                            own.mark(V.scalar_tensor_tensor(y_lo[:, c * 512:(c + 1) * 512], (A, B)[c][:, :], gslot[:, par:par + 1],
                                                            y_hi[:, c * 512:(c + 1) * 512].bitcast(F32), ALU.mult, ALU.subtract))
                        own.settle()
                        dve.nop().then_inc(sw.yl, 1)

                    def step(s, n, first=False, last=False):
                        if not last:
                            one_hot(main, 1 - s, n + 1)
                        silu(main, n + 1)
                        if not last:
                            read_gathered(main, 1 - s, n + 2)
                        read_hT(main, n + 1)
                        if not last:
                            if not first:
                                dve.wait_ge(main.sc, n)
                            read_hotT(main, 1 - s)
                        y_low(main, s, n + 1)
                        own.restart()

                    own.restart()
                    one_hot(main, 0, 0)
                    dve.wait_ge(sh_exp, 1)
                    s_all = shS[:, :, :].rearrange("p f c -> p (f c)")
                    V.tensor_tensor(s_all, s_all, bank[6], ALU.mult).then_inc(sh_gate, 1)
                    for t in range(TT):
                        gate_parts(t)
                    own.link(V.tensor_scalar(flag[0:1, 0:1], rsm[0:1, 8:9], float(SLOTS) + 0.5, None, ALU.is_gt))
                    dve.nop().then_inc(routed_ready, 1)
                    read_gathered(main, 0, 1)
                    read_hotT(main, 0)
                    step(0, 0, first=True)
                    with dve.Fori(0, PAIRS // 2 - 1) as i:
                        step(1, 2 * i + 1)
                        step(0, 2 * i + 2)
                    step(1, PAIRS - 1, last=True)
                    dve.wait_ge(main.sc, PAIRS - 1)
                    own.restart()
                    more = dve.value_load(flag[0:1, 0:1], min_val=0, max_val=1)
                    with dve.If(more > 0):
                        with dve.Fori(0, ROUNDS - 1) as r:
                            dve.wait_ge(combined, TT)
                            own.link(V.tensor_scalar(rk, rk, float(SLOTS), None, ALU.subtract))
                            own.restart()
                            with dve.Fori(0, PAIRS) as n:
                                k = r * PAIRS + n + 1
                                dve.wait_ge(over.sc, k)
                                one_hot(over, 0, n)
                                read_gathered(over, 0, k)
                                read_hotT(over, 0)
                                silu(over, k)
                                read_hT(over, k)
                                y_low(over, 0, k)
                                own.restart()
                        dve.wait_ge(over.sc, (ROUNDS - 1) * PAIRS + 1)
                    with dve.Else():
                        dve.nop()
                    norm(TT, combined, (1, 2))
                    own.settle()

            engines = (nc.sync, nc.scalar, nc.vector, nc.tensor, nc.gpsimd)
            for n, s in enumerate(names):
                engines[n % len(engines)].sem_clear(s)
            nc.all_engine_barrier()

        with nc.Block() as block:
            @block.sync
            def _(sp):
                sp.dma_start(out.rearrange("b (t p) d -> p (b t) d", p=P), x_sb[:, :, :]).then_inc(stored, 16)
                sp.wait_ge(stored, 16)


def shape_constants():
    i = np.arange(P)
    tok = np.arange(T)
    half = HD // 2
    inv = np.float32(10000.0) ** (-np.arange(half, dtype=np.float32) * np.float32(2.0 / HD))
    ang = tok.astype(np.float32)[:, None] * inv.astype(np.float32)[None, :]
    cos, sin = np.cos(ang), np.sin(ang)
    rope = np.stack([np.concatenate([cos, cos], 1), np.concatenate([-sin, sin], 1)])
    rope = rope.reshape(2, TT, P, HD).transpose(2, 0, 1, 3)
    last = np.arange(NC) * CMP_STRIDE + CMP_LEN - 1
    vis = last[None, :] <= tok[:, None]
    cvis = np.zeros((T, 16), np.float32)
    cvis[:, :NC] = np.where(vis, 0.0, NEG)
    misc = np.concatenate([cvis.reshape(TT, P, 16).transpose(1, 0, 2).reshape(P, TT * 16),
                           vis.any(1).astype(np.float32).reshape(TT, P).T,
                           np.broadcast_to(np.arange(1, SLOTS + 1, dtype=np.float32), (P, SLOTS)),
                           np.tile(np.concatenate([np.array([[1 / SCALE, 0, 0, 1], [0, 1, -1 / SCALE, 0]], np.float32), np.zeros((FROWS - 2, 4), np.float32)]), (P // FROWS, 1))], 1)
    return {
        "ident": np.eye(P, dtype=np.float32),
        "cmask": np.where(i[None, :] <= i[:, None], 0.0, NEG).astype(np.float32),
        "upper": (tok[:, None] <= tok[None, :]).astype(np.float32).reshape(TT, P, T).transpose(1, 0, 2).copy(),
        "rope": np.ascontiguousarray(rope, np.float32), "misc": np.ascontiguousarray(misc, np.float32),
        "ones": np.ones((P, T), np.float32),
    }


def column_order():
    at, off = {}, 0
    for name, width in (("fox_q", 256), ("fox_k", 256), ("fox_v", 256), ("fox_f", 4), ("nsa_q", 384), ("nsa_kc", 128), ("nsa_vc", 128),
                        ("nsa_ks", 128), ("nsa_vs", 128), ("nsa_kw", 128), ("nsa_vw", 128), ("nsa_g", 18), ("dsa_q", 384),
                        ("dsa_k", 64), ("dsa_v", 64), ("idx_q", 256), ("idx_k", 64), ("idx_w", 4)):
        at[name] = np.arange(off, off + width)
        off += width

    def head(name, h):
        return at[name][h * HD:(h + 1) * HD]

    nq = [head("nsa_q", g * REP + r) for r in range(REP) for g in range(GRP)]
    return [
        at["idx_q"],
        np.concatenate([at["idx_k"], at["dsa_k"], at["nsa_kc"]]),
        np.concatenate([at["nsa_vw"], at["dsa_v"], at["fox_f"], at["nsa_g"], at["idx_w"]]),
        np.concatenate([at["nsa_vc"], at["nsa_vs"]]),
        at["fox_q"], at["fox_k"], at["fox_v"],
        np.concatenate(nq[0:4]),
        np.concatenate(nq[4:6] + [at["nsa_ks"]]),
        at["dsa_q"][0:PIECE],
        np.concatenate([at["dsa_q"][PIECE:], at["nsa_kw"]]),
    ]


def lay_out(inputs):
    g = {k: np.asarray(v) for k, v in inputs.items()}
    L = DEPTH

    def by_partition(w):
        return w.reshape(L, -1, P, w.shape[-1]).transpose(0, 2, 1, 3)

    npieces = N_IN_PIECES + 2 + N_OUT_PIECES
    pieces = np.zeros((L, npieces, P, KD, PIECE), np.float32)
    w_in = by_partition(g["w_in"])
    for c, cols in enumerate(column_order()):
        n = STREAM.index(("in", c))
        pieces[:, n, :, :, :len(cols)] = w_in[:, :, :, cols]
    for n, name in enumerate(("cmp_w1_k", "cmp_w1_v")):
        pieces[:, STREAM.index(("cmp", n))] = by_partition(g[name]).reshape(L, P, KD, PIECE)
    heads = ([0, 1, 2, 3] + [FOX + gg * REP + r for r in range(REP) for gg in range(GRP)] + [FOX + NSA + h for h in range(DSA)])
    w_out = g["w_out"].reshape(L, 16, HD, D)[:, heads].reshape(L, D, D)
    w_out = by_partition(w_out)
    for n in range(N_OUT_PIECES):
        pieces[:, STREAM.index(("out", n))] = w_out[:, :, :, n * PIECE:(n + 1) * PIECE]

    pieces[:, 0] = np.roll(pieces[:, 0], -1, 0)

    def pos(name):
        return g[name].reshape(L, CPAIRS, P).transpose(0, 2, 1)

    small = np.concatenate([g["cmp_w2_k"], g["cmp_w2_v"], pos("cmp_pos_k"), pos("cmp_pos_v")], 2)
    rows = np.concatenate([g["fox_forget_bias"], g["b_router"]], 1)
    lnw = np.stack([np.concatenate([g["ln1_g"], g["ln1_b"]], 1), np.concatenate([g["ln2_g"], g["ln2_b"]], 1)], 1)

    def expert(gate, up, down):
        n = gate.shape[0]
        o = np.empty((n, P, EW), np.float32)
        gu = o[:, :, :EGU].reshape(n, P, KD, 2, EF)
        gu[:, :, :, 0] = gate.reshape(n, KD, P, EF).transpose(0, 2, 1, 3)
        gu[:, :, :, 1] = up.reshape(n, KD, P, EF).transpose(0, 2, 1, 3)
        o[:, :, :EGU] = gu.reshape(n, P, EGU)
        o[:, :, EGU:] = down.reshape(n, EF // P, P, D).transpose(0, 2, 1, 3).reshape(n, P, -1)
        return o

    moe = expert(g["w_gate"].reshape(L * NE, D, EF), g["w_up"].reshape(L * NE, D, EF), g["w_down"].reshape(L * NE, EF, D))
    return {
        "x": g["x"], "pieces": pieces.reshape(L, npieces, P, KD * PIECE), "rows": rows, "small": small,
        "moe_w": moe.reshape(L, NE, P, EW), "ws": expert(g["ws_gate"], g["ws_up"], g["ws_down"]),
        "router": by_partition(g["w_router"]).reshape(L, P, KD * NE), "lnw": lnw,
    }


def kernel(**inputs):
    import concourse.bacc as _bacc
    from concourse.bass_utils import run_bass_kernel_spmd as _run

    nc = _bacc.Bacc("TRN2", target_bir_lowering=False, num_devices=1)
    arrays, args = {}, {}
    for name, a in {**lay_out(inputs), **{"const_" + k: v for k, v in shape_constants().items()}}.items():
        a = np.ascontiguousarray(a)
        arrays[f"in_{name}"] = a
        args[name] = nc.dram_tensor(f"in_{name}", a.shape, mybir.dt.from_np(a.dtype), kind="ExternalInput").ap()
    out = nc.dram_tensor("out_0", (1, T, D), F32, kind="ExternalOutput").ap()
    consts = {k[6:]: args.pop(k) for k in list(args) if k.startswith("const_")}
    build(nc, consts=consts, out=out, **args)
    r = _run(nc, [arrays], core_ids=[0])
    return r.results[0]["out_0"]
```
